# Optimizing a Trainium2 kernel written in Bass

```python
import math
import jax
import jax.numpy as jnp
from jax import lax
import numpy as np

D_MODEL = 1024
BATCH = 1
SEQ = 256
DEPTH = 2

HEAD_DIM = 64
ATTN_Q_HEADS = 8
ATTN_KV_HEADS = 2
ATTN_GROUP = ATTN_Q_HEADS // ATTN_KV_HEADS
WINDOW = 128
BLOCK = 128
SPAN = BLOCK + 2 * WINDOW
N_BUCKETS = 32
MAX_DISTANCE = 128
DN_HEADS = 8
DN_DK = 64
DN_DV = 64
DN_CONV = 5
DN_CHUNK = 64
POOL_WINDOWS = (2, 4, 8, 16)
N_POOL_GROUPS = 4
POOL_GROUP = 128
ATTN_W = ATTN_Q_HEADS * HEAD_DIM
KV_W = ATTN_KV_HEADS * HEAD_DIM
DN_QK_W = DN_HEADS * DN_DK
DN_V_W = DN_HEADS * DN_DV
DN_CONV_CH = 2 * DN_QK_W + DN_V_W
POOL_W = N_POOL_GROUPS * POOL_GROUP
BRANCH_W = 512
N_BRANCH = 3
SPLIT_SIZES = (ATTN_W, KV_W, KV_W, DN_QK_W, DN_QK_W, DN_V_W, DN_V_W, 4 * DN_HEADS, POOL_W, N_BRANCH * D_MODEL)
IN_COLS = sum(SPLIT_SIZES)
D_FF = 2816
N_EXPERTS = 8
TOP_K = 2
D_FF_EXPERT = 3584
N_DENSE = (DEPTH + 1) // 2
N_MOE = DEPTH // 2
DEEPNORM_ALPHA = (2.0 * DEPTH) ** 0.25
DEEPNORM_BETA = (8.0 * DEPTH) ** -0.25
LN_EPS = 1e-5
RMS_EPS = 1e-6
NEG_INF = -1e30

kernel_name = 'hybrid_gated_attn_deltanet_pool_moe_encoder'

f32 = jnp.float32

def layer_norm(x, g, b):
    xf = x.astype(f32)
    mu = jnp.mean(xf, -1, keepdims=True)
    var = jnp.mean(jnp.square(xf - mu), -1, keepdims=True)
    return ((xf - mu) * lax.rsqrt(var + LN_EPS) * g + b).astype(x.dtype)

def _band_rel():
    q_loc = np.arange(BLOCK)[:, None]
    k_loc = np.arange(SPAN)[None, :]
    return k_loc - WINDOW - q_loc

def _t5_bucket(rel):
    nb = N_BUCKETS // 2
    max_exact = nb // 2
    n = np.abs(rel)
    large = max_exact + (np.log(np.maximum(n, 1) / max_exact) / np.log(MAX_DISTANCE / max_exact)
                         * (nb - max_exact)).astype(np.int32)
    large = np.minimum(large, nb - 1)
    return (np.where(rel > 0, nb, 0) + np.where(n < max_exact, n, large)).astype(np.int32)

def windowed_gqa(q, k, v, sink, bias):
    B, S = q.shape[0], q.shape[1]
    n_blocks = S // BLOCK
    in_window = jnp.asarray(np.abs(_band_rel()) <= WINDOW)
    qg = q.reshape(B, S, ATTN_KV_HEADS, ATTN_GROUP, HEAD_DIM)
    kp = jnp.pad(k, ((0, 0), (WINDOW, WINDOW), (0, 0), (0, 0)))
    vp = jnp.pad(v, ((0, 0), (WINDOW, WINDOW), (0, 0), (0, 0)))
    bias_g = bias.reshape(ATTN_KV_HEADS, ATTN_GROUP, BLOCK, SPAN)
    sink_g = sink.astype(f32).reshape(ATTN_KV_HEADS, ATTN_GROUP, 1, 1)
    scale = HEAD_DIM ** -0.5

    def one_block(i):
        start = i * BLOCK
        qb = lax.dynamic_slice_in_dim(qg, start, BLOCK, axis=1).astype(f32)
        kb = lax.dynamic_slice_in_dim(kp, start, SPAN, axis=1).astype(f32)
        vb = lax.dynamic_slice_in_dim(vp, start, SPAN, axis=1).astype(f32)
        kpos = start - WINDOW + jnp.arange(SPAN)
        valid = in_window & ((kpos >= 0) & (kpos < S))[None, :]
        s = jnp.einsum('bqkgd,bjkd->bkgqj', qb, kb) * scale + bias_g
        s = jnp.where(valid, s, NEG_INF)
        m = jnp.maximum(jnp.max(s, -1, keepdims=True), sink_g)
        p = jnp.exp(s - m)
        denom = jnp.sum(p, -1, keepdims=True) + jnp.exp(sink_g - m)
        o = jnp.einsum('bkgqj,bjkd->bqkgd', p / denom, vb)
        return o.astype(q.dtype)

    o = lax.map(one_block, jnp.arange(n_blocks))
    return jnp.moveaxis(o, 0, 1).reshape(B, S, ATTN_W)

def short_conv(u, w):
    pad = (DN_CONV - 1) // 2
    return lax.conv_general_dilated(u, w[:, None, :].astype(u.dtype), window_strides=(1,),
                                    padding=[(pad, pad)], dimension_numbers=('NWC', 'WIO', 'NWC'),
                                    feature_group_count=u.shape[-1])

def l2norm(t):
    return t * lax.rsqrt(jnp.sum(t * t, -1, keepdims=True) + 1e-6)

def gated_delta_chunked(q, k, v, g, beta):
    R, B, S, H, dk = q.shape
    dv = v.shape[-1]
    C = DN_CHUNK
    N = S // C

    def to_chunks(t):
        t = t.reshape(t.shape[:2] + (N, C) + t.shape[3:])
        return jnp.transpose(t, (2, 0, 1, 4, 3) + tuple(range(5, t.ndim)))

    q = l2norm(q) * (dk ** -0.5)
    k = l2norm(k)
    qc, kc, vc = to_chunks(q), to_chunks(k), to_chunks(v)
    gc, bc = to_chunks(g), to_chunks(beta)
    G = jnp.cumsum(gc, axis=-1)
    lower = jnp.tril(jnp.ones((C, C), bool))
    strict = jnp.tril(jnp.ones((C, C), bool), -1)
    diff = G[..., :, None] - G[..., None, :]
    decay = jnp.where(lower, jnp.exp(jnp.where(lower, diff, 0.0)), 0.0)
    kb = kc * bc[..., None]
    A = jnp.where(strict, jnp.einsum('...id,...jd->...ij', kb, kc) * decay, 0.0)
    rhs = jnp.concatenate([vc * bc[..., None], kb * jnp.exp(G)[..., None]], axis=-1)
    sol = lax.linalg.triangular_solve(A, rhs, left_side=True, lower=True, unit_diagonal=True)
    u_c, w_c = sol[..., :dv], sol[..., dv:]
    qk = jnp.where(lower, jnp.einsum('...id,...jd->...ij', qc, kc) * decay, 0.0)
    q_dec = qc * jnp.exp(G)[..., None]
    G_last = G[..., -1:]
    k_dec = kc * jnp.exp(G_last - G)[..., None]
    chunk_decay = jnp.exp(G_last)[..., None]

    def step(state, xs):
        q_i, k_i, qk_i, u_i, w_i, cd_i = xs
        v_new = u_i - jnp.einsum('rbhcd,rbhde->rbhce', w_i, state)
        o = jnp.einsum('rbhcd,rbhde->rbhce', q_i, state) + jnp.einsum('rbhij,rbhje->rbhie', qk_i, v_new)
        state = state * cd_i + jnp.einsum('rbhcd,rbhce->rbhde', k_i, v_new)
        return state, o

    s0 = jnp.zeros((R, B, H, dk, dv), f32)
    _, o = lax.scan(step, s0, (q_dec, k_dec, qk, u_c, w_c, chunk_decay))
    return jnp.transpose(o, (1, 2, 0, 4, 3, 5)).reshape(R, B, S, H, dv)

def delta_branch(q, k, v, z, a, b, conv_w, a_log, dt_bias, norm_w):
    B, S = q.shape[0], q.shape[1]
    dtype = q.dtype
    qkv = jax.nn.silu(short_conv(jnp.concatenate([q, k, v], -1), conv_w)).astype(f32)
    qh = qkv[..., :DN_QK_W].reshape(B, S, DN_HEADS, DN_DK)
    kh = qkv[..., DN_QK_W:2 * DN_QK_W].reshape(B, S, DN_HEADS, DN_DK)
    vh = qkv[..., 2 * DN_QK_W:].reshape(B, S, DN_HEADS, DN_DV)
    g = -jnp.exp(a_log.astype(f32)) * jax.nn.softplus(a.astype(f32) + dt_bias.astype(f32))
    beta = jax.nn.sigmoid(b.astype(f32))

    def both(t):
        return jnp.stack([t, jnp.flip(t, axis=1)])

    g2 = jnp.stack([g[:, :, 0], jnp.flip(g[:, :, 1], axis=1)])
    beta2 = jnp.stack([beta[:, :, 0], jnp.flip(beta[:, :, 1], axis=1)])
    o = gated_delta_chunked(both(qh), both(kh), both(vh), g2, beta2)
    o = o[0] + jnp.flip(o[1], axis=1)
    zh = z.astype(f32).reshape(B, S, DN_HEADS, DN_DV)
    o = o * lax.rsqrt(jnp.mean(o * o, -1, keepdims=True) + RMS_EPS) * norm_w.astype(f32) * jax.nn.silu(zh)
    return o.reshape(B, S, DN_V_W).astype(dtype)

def pool_branch(u, pool_w, pool_scale):
    B, S = u.shape[0], u.shape[1]
    groups = u.reshape(B, S, N_POOL_GROUPS, POOL_GROUP).astype(f32)
    t = np.arange(S)
    outs = []
    for gi, w in enumerate(POOL_WINDOWS):
        r = w // 2
        ug = groups[:, :, gi]
        cs = jnp.cumsum(jnp.pad(ug, ((0, 0), (r + 1, r), (0, 0))), axis=1)
        win_sum = cs[:, 2 * r + 1:] - cs[:, :S]
        count = (np.minimum(t + r, S - 1) - np.maximum(t - r, 0) + 1).astype(np.float32)
        outs.append(win_sum / jnp.asarray(count)[None, :, None] - ug)
    mixed = jnp.stack(outs, axis=2)
    y = jnp.einsum('bsgc,gcd->bsgd', mixed, pool_w.astype(f32))
    return (y.reshape(B, S, POOL_W) * pool_scale.astype(f32)).astype(u.dtype)

def hybrid_mixer(x, w_in, attn_sink, bias, conv_w, a_log, dt_bias, dn_norm_w, pool_w, pool_scale, w_branch, w_out):
    B, S = x.shape[0], x.shape[1]
    proj = x @ w_in
    points = np.cumsum(SPLIT_SIZES)[:-1].tolist()
    aq, ak, av, dq, dk, dvv, dz, dab, pu, gates = jnp.split(proj, points, axis=-1)
    o_attn = windowed_gqa(aq.reshape(B, S, ATTN_Q_HEADS, HEAD_DIM),
                          ak.reshape(B, S, ATTN_KV_HEADS, HEAD_DIM),
                          av.reshape(B, S, ATTN_KV_HEADS, HEAD_DIM), attn_sink, bias)
    dab = dab.reshape(B, S, 4, DN_HEADS)
    o_delta = delta_branch(dq, dk, dvv, dz, dab[:, :, :2], dab[:, :, 2:], conv_w, a_log, dt_bias, dn_norm_w)
    o_pool = pool_branch(pu, pool_w, pool_scale)
    branches = jnp.stack([o_attn, o_delta, o_pool], axis=2)
    up = jnp.einsum('bsnc,ncd->bsnd', branches, w_branch)
    gate = jax.nn.sigmoid(gates.reshape(B, S, N_BRANCH, D_MODEL))
    merged = jnp.sum(gate * up, axis=2)
    return merged @ w_out

def swiglu(x, w_gate, w_up, w_down):
    return (jax.nn.silu(x @ w_gate) * (x @ w_up)) @ w_down

def moe_swiglu(x, router_w, wg, wu, wd):
    logits = (x @ router_w).astype(f32)
    top_logit, top_idx = lax.top_k(logits, TOP_K)
    top_p = jax.nn.softmax(top_logit, axis=-1)
    combine = jnp.sum(jax.nn.one_hot(top_idx, N_EXPERTS, dtype=f32) * top_p[..., None], axis=-2)
    out = jnp.zeros(x.shape, f32)
    for e in range(N_EXPERTS):
        out = out + combine[..., e:e + 1] * swiglu(x, wg[e], wu[e], wd[e]).astype(f32)
    return out.astype(x.dtype)

def setup_inputs(seed: int = 0) -> dict:
    key = jax.random.key(seed)
    ks = jax.random.split(key, 24)
    L = DEPTH
    D = D_MODEL

    def nrm(k, shape, scale):
        return jax.random.normal(k, shape, f32) * scale

    x = nrm(ks[0], (BATCH, SEQ, D), 1.0)
    w_in = nrm(ks[1], (L, D, IN_COLS), D ** -0.5)
    attn_sink = nrm(ks[2], (L, ATTN_Q_HEADS), 0.5)
    rel_bias = nrm(ks[3], (N_BUCKETS, ATTN_Q_HEADS), 0.5)
    conv_w = nrm(ks[4], (L, DN_CONV, DN_CONV_CH), DN_CONV ** -0.5)
    a_log = jnp.log(jax.random.uniform(ks[5], (L, 2, DN_HEADS), f32, 1.0, 16.0))
    dt = jnp.exp(jax.random.uniform(ks[6], (L, 2, DN_HEADS), f32, math.log(1e-3), math.log(1e-1)))
    dt_bias = dt + jnp.log(-jnp.expm1(-dt))
    dn_norm_w = 1.0 + nrm(ks[7], (L, DN_DV), 0.1)
    pool_w = nrm(ks[8], (L, N_POOL_GROUPS, POOL_GROUP, POOL_GROUP), POOL_GROUP ** -0.5)
    pool_scale = 1.0 + nrm(ks[9], (L, POOL_W), 0.1)
    w_branch = nrm(ks[10], (L, N_BRANCH, BRANCH_W, D), BRANCH_W ** -0.5)
    w_out = nrm(ks[11], (L, D, D), DEEPNORM_BETA * D ** -0.5)
    ln1_g = 1.0 + nrm(ks[12], (L, D), 0.1)
    ln1_b = nrm(ks[13], (L, D), 0.02)
    ln2_g = 1.0 + nrm(ks[14], (L, D), 0.1)
    ln2_b = nrm(ks[15], (L, D), 0.02)
    ffn_w1 = nrm(ks[16], (N_DENSE, D, D_FF), D ** -0.5)
    ffn_w3 = nrm(ks[17], (N_DENSE, D, D_FF), D ** -0.5)
    ffn_w2 = nrm(ks[18], (N_DENSE, D_FF, D), DEEPNORM_BETA * D_FF ** -0.5)
    router_w = nrm(ks[19], (N_MOE, D, N_EXPERTS), D ** -0.5)
    moe_wg = nrm(ks[20], (N_MOE, N_EXPERTS, D, D_FF_EXPERT), D ** -0.5)
    moe_wu = nrm(ks[21], (N_MOE, N_EXPERTS, D, D_FF_EXPERT), D ** -0.5)
    moe_wd = nrm(ks[22], (N_MOE, N_EXPERTS, D_FF_EXPERT, D), DEEPNORM_BETA * D_FF_EXPERT ** -0.5)
    return {'x': x, 'w_in': w_in, 'attn_sink': attn_sink, 'rel_bias': rel_bias, 'conv_w': conv_w,
            'a_log': a_log, 'dt_bias': dt_bias, 'dn_norm_w': dn_norm_w, 'pool_w': pool_w,
            'pool_scale': pool_scale, 'w_branch': w_branch, 'w_out': w_out, 'ln1_g': ln1_g,
            'ln1_b': ln1_b, 'ln2_g': ln2_g, 'ln2_b': ln2_b, 'ffn_w1': ffn_w1, 'ffn_w3': ffn_w3,
            'ffn_w2': ffn_w2, 'router_w': router_w, 'moe_wg': moe_wg, 'moe_wu': moe_wu, 'moe_wd': moe_wd}

def reference(x, w_in, attn_sink, rel_bias, conv_w, a_log, dt_bias, dn_norm_w, pool_w, pool_scale,
              w_branch, w_out, ln1_g, ln1_b, ln2_g, ln2_b, ffn_w1, ffn_w3, ffn_w2,
              router_w, moe_wg, moe_wu, moe_wd):
    bias = jnp.transpose(rel_bias[_t5_bucket(_band_rel())], (2, 0, 1)).astype(f32)
    h = x
    for layer in range(DEPTH):
        y = hybrid_mixer(h, w_in[layer], attn_sink[layer], bias, conv_w[layer], a_log[layer], dt_bias[layer],
                         dn_norm_w[layer], pool_w[layer], pool_scale[layer], w_branch[layer], w_out[layer])
        h = layer_norm(DEEPNORM_ALPHA * h + y, ln1_g[layer], ln1_b[layer])
        i = layer // 2
        if layer % 2 == 0:
            y = swiglu(h, ffn_w1[i], ffn_w3[i], ffn_w2[i])
        else:
            y = moe_swiglu(h, router_w[i], moe_wg[i], moe_wu[i], moe_wd[i])
        h = layer_norm(DEEPNORM_ALPHA * h + y, ln2_g[layer], ln2_b[layer])
    return h


_drawn_inputs = setup_inputs


def setup_inputs(seed=0):
    import zlib

    import numpy as np

    out = dict(_drawn_inputs(seed))
    spreads = {}
    factors = {'attn_sink': 36.261, 'rel_bias': 3.525, 'dn_norm_w': 3.003}
    for name, (base, spread) in spreads.items():
        noise = np.random.default_rng([zlib.crc32(name.encode()), seed]).standard_normal(out[name].shape)
        drawn = base * np.exp(spread * noise) if base else spread * noise
        out[name] = jnp.asarray(drawn.astype(out[name].dtype))
    for name, factor in factors.items():
        out[name] = (out[name] * factor).astype(out[name].dtype)
    return out
```

```python
import math
from contextlib import ExitStack

import numpy as np

import concourse.bass as bass
from concourse import mybir

F32 = mybir.dt.float32
F32R = mybir.dt.float32r
I32 = mybir.dt.int32
U32 = mybir.dt.uint32
ALU = mybir.AluOpType
ACT = mybir.ActivationFunctionType
AX = mybir.AxisListType

P = 128
DEPTH = 2
SEQ = 256
NT = SEQ // P
D = 1024
KT = D // P
HD = 64
QH, KVH = 8, 2
DNH = 8
CONV = 5
CHUNK = 64
BR = 512
BT = BR // P
NB = 3
N_BUCKETS = 32
MAX_DISTANCE = 128
WINDOW = 128
STRIP = 3 * P
POOL_WINDOWS = (2, 4, 8, 16)
DFF = 2816
DFFE = 3584
NE = 8
ALPHA = (2.0 * DEPTH) ** 0.25
LN_EPS = 1e-5
NEG = -1e30
LEVELS = 6

C_Q, C_K, C_DQ, C_DK, C_DV, C_Z, C_AB, C_PU, C_G = 0, 512, 768, 1280, 1792, 2304, 2816, 2848, 3360

CAP = 96
TOP_K = 2
MAXP = (SEQ * TOP_K + NE * (CAP - 1)) // CAP

SLOT = 4096
SUB = 1024
HI_BUFS = 4
MIX_SLOTS, DENSE_SLOTS, MOE_SLOTS = 4, 6, 7

SETS = [(0, 0), (1, 1), (0, 1), (1, 0)]

HEAD_AT = [2 * (w % 4) + w // 4 for w in range(DNH)]

CONST = {}


def const_table():
    j, i = np.meshgrid(np.arange(P), np.arange(P), indexing="ij")
    same = (j // CHUNK) == (i // CHUNK)
    parts = [("ident", np.eye(P)), ("cum0", same & (j <= i)), ("cum1", same & (j >= i)), ("blk", same),
             ("before", j < i), ("neg0", np.where(same & (j <= i), 0.0, NEG)),
             ("neg1", np.where(same & (j >= i), 0.0, NEG))]
    for d in range(2):
        for l in range(LEVELS):
            s = 1 << l
            pair = (j // (2 * s)) == (i // (2 * s))
            lo_j, lo_i = (j % (2 * s)) < s, (i % (2 * s)) < s
            parts.append((f"lvl{d}{l}", pair & (lo_j & ~lo_i if d == 0 else ~lo_j & lo_i)))
    parts.append(("iota", np.broadcast_to(np.arange(CAP), (P, CAP))))
    parts.append(("pass_no", np.broadcast_to(np.repeat(np.arange(MAXP), NE), (P, MAXP * NE))))
    parts.append(("scal", np.broadcast_to(np.array([1e-6, LN_EPS, math.log(HD ** -0.5), 1.0]), (P, 4))))
    at = 0
    for name, a in parts:
        CONST[name] = (at, at + a.shape[1])
        at += a.shape[1]
    return np.ascontiguousarray(np.concatenate([np.asarray(a, np.float32) for _, a in parts], axis=1))


def pool_table():
    t = np.arange(SEQ)
    out = np.zeros((SEQ, len(POOL_WINDOWS), SEQ), np.float32)
    for g, w in enumerate(POOL_WINDOWS):
        r = w // 2
        count = (np.minimum(t + r, SEQ - 1) - np.maximum(t - r, 0) + 1).astype(np.float32)
        out[:, g, :] = (np.abs(t[:, None] - t[None, :]) <= r) / count[None, :] - np.eye(SEQ)
    return np.ascontiguousarray(out.reshape(NT, P, len(POOL_WINDOWS), SEQ).transpose(1, 0, 2, 3))


def bucket_table():
    rel = np.arange(-255, 257)
    nb = N_BUCKETS // 2
    max_exact = nb // 2
    n = np.abs(rel)
    large = max_exact + (np.log(np.maximum(n, 1) / max_exact) / np.log(MAX_DISTANCE / max_exact)
                         * (nb - max_exact)).astype(np.int32)
    large = np.minimum(large, nb - 1)
    bucket = np.where(rel > 0, nb, 0) + np.where(n < max_exact, n, large)
    hot = (np.arange(N_BUCKETS)[:, None] == bucket[None, :]).astype(np.float32)
    mask = np.where(n <= WINDOW, 0.0, NEG).astype(np.float32)
    return hot, np.ascontiguousarray(np.broadcast_to(mask, (QH, 512)))


class Ring:

    def __init__(self):
        self.slot, self.full, self.before, self.last = {}, {}, {}, {}
        self.count = [0] * MOE_SLOTS

    def add(self, name, slot, loads=1):
        self.slot[name] = slot
        self.count[slot] += 16 * loads
        self.full[name] = self.count[slot]
        self.before[name] = self.last.get(slot)
        self.last[slot] = name


GATE_ORDER = (2, 0, 1)
GATES = [f"gate{n}{hf}" for n in GATE_ORDER for hf in range(2)]


def mixer_ring():
    r = Ring()
    for k, name in enumerate(["dk", "dq", "dv", "kvab", "q", "z", "pu", "pool"]):
        r.add(name, k % MIX_SLOTS, 2 if name == "kvab" else 1)
    for k, name in enumerate(GATES):
        r.add(name, k % 3)
    for name, slot in (("branch2", 0), ("branch0", 1), ("branch1", 2), ("out0", 3), ("out1", 0)):
        r.add(name, slot, 2 if name == "branch0" else 1)
    return r


def build(nc, A, out):
    es = ExitStack()
    with es:
        def sb(name, n, dt=F32, p=P):
            return es.enter_context(nc.sbuf_tensor(name, [p, n], dt))

        def sem(name):
            return es.enter_context(nc.semaphore(name))

        at = {}

        def sb_at(name, n):
            t = sb(name, n)
            at[name] = nc.sbuf_base - 4 * n
            return t

        ring_mem = sb_at("ring", MIX_SLOTS * SLOT)
        h_mem = sb("h", NT * D)
        hT_mem = sb_at("hT", KT * SEQ)
        strip_mem = sb_at("strip", QH * STRIP)
        M = sb_at("M", 24064)
        cst = sb("cst", A["consts"].shape[1])
        convw = sb("convw", 12 * CONV)
        dnrow = sb("dnrow", 32)
        normw = sb("normw", HD)
        poolsc = sb("poolsc", BT)
        sinkr = sb("sinkr", 16)
        ab_mem = sb("ab", 64)
        gsm = sb("gsm", 480)
        att_s = sb("att_s", 8 * 16)
        lnst = sb("lnst", 64)
        ids = sb("ids", 16, I32)
        idx8v = sb("idx8", 16, U32)[:, :].rearrange("p (t e) -> p t e", t=NT)
        ps = [es.enter_context(nc.psum_tensor(f"ps{i}", [P, 512], F32)) for i in range(8)]

        def C(name):
            a, b = CONST[name]
            return cst[:, a:b]

        ident = C("ident")
        scal = C("scal")
        h = h_mem[:, :].rearrange("p (t d) -> p t d", t=NT)
        hT = hT_mem[:, :].rearrange("p (k s) -> p k s", k=KT)
        strip = strip_mem[:, :].rearrange("p (h c) -> p h c", h=QH)
        ab = ab_mem[:, :].rearrange("p (t c) -> p t c", t=NT)

        def m(at, n, k=None):
            v = M[:, at:at + n]
            return v if k is None else v.rearrange("p (k n) -> p k n", k=k)

        def r_view(name, under, start, n):
            return nc.alloc_sbuf_tensor_at(name, [P, n], F32R, offset=at[under] + 4 * start)

        oAT = m(0, 1024, BT)
        oPT = m(1024, 1024, BT)
        zs = m(2048, 1024, NT)
        osum = m(3072, 1024, NT)
        qT = m(4096, 1024, BT)
        kT = m(5120, 1024, BT)
        ktok = m(6144, 1024, NT)
        vtok = m(7168, 1024, NT)
        S = m(8192, 1024).rearrange("p (d k n) -> p d k n", d=2, k=4)
        Sc = m(9216, 1024).rearrange("p (d k n) -> p d k n", d=2, k=4)
        vnew = m(10240, 1024, 2)
        mixT = m(8192, 1024, BT)
        kept = [11264 + 3072 * s for s in range(2)]
        qkd = [m(a, 1024, DNH) for a in kept]
        u_s = [m(a + 1024, 512) for a in kept]
        wT = [m(a + 1536, 512, 4) for a in kept]
        qdec = [m(a + 2048, 512, 4) for a in kept]
        kdec = [m(a + 2560, 512) for a in kept]
        W0 = 17408
        Dm = m(W0, 1024, DNH)
        AT = m(W0 + 1024, 1024, DNH)
        XT = m(W0 + 2048, 1024, DNH)
        X = m(W0 + 3072, 1024, DNH)
        AL = m(W0 + 4096, 1024, DNH)
        Rv = m(W0 + 5120, 512)
        Rw = m(W0 + 5632, 512)
        eGp = m(W0 + 6144, 512, 4)
        poolw = m(9216, 512, BT)
        convin = m(11264, 12 * 260, 12)
        Sall = m(11264, 4096).rearrange("p (m e j) -> p m e j", m=8, e=2)
        qA = m(15360, 1024, 4)
        kA = m(16384, 256)
        vA = m(16640, 256, NT)
        pu = m(16896, 1024, NT)
        vT = m(17920, 1024, BT)
        PT = m(18944, 1024, 2)
        sq = m(19968, 2048, 4)
        rs = m(22016, 2048, 4)
        oDT = m(4096, 1024, BT)
        merged = m(6144, 2048, NT)
        gates1 = m(19968, 2048)
        gtmp = m(10240, 1024, 2)
        mT = m(0, 2048, KT)
        lng = m(2048, 1024)
        lnb = m(3072, 1024)
        sg = m(4096, 512, 2)
        aT = m(4608, 1024, 4)
        hTh = r_view("hTh", "hT", 0, KT * SEQ)[:, :].rearrange("p (k s) -> p k s", k=KT)
        hTl = r_view("hTl", "M", 0, KT * SEQ)[:, :].rearrange("p (k s) -> p k s", k=KT)
        dath = r_view("dath", "M", 5632, 1024)[:, :].rearrange("p (b s) -> p b s", b=4)
        datl = r_view("datl", "M", 6656, 1024)[:, :].rearrange("p (b s) -> p b s", b=4)
        dw_hi = r_view("dw_hi", "M", 7680, HI_BUFS * SUB)
        acc = m(4096, 2048, NT)
        disp = m(6144, 192, NT)
        comb = m(6336, 192, NT)
        combT = m(6528, 256, NT)
        y = m(6784, 1024)
        sge = m(7808, 1024, 2)
        ae = m(8832, 1024, 2)
        hot1 = m(9920, 96)
        hot2 = m(10016, 96)
        hot3 = m(10700, 96)
        xgh = r_view("xgh", "M", 0, KT * CAP)[:, :].rearrange("p (k c) -> p k c", k=KT)
        xgl = r_view("xgl", "M", KT * CAP, KT * CAP)[:, :].rearrange("p (k c) -> p k c", k=KT)
        w_hi = r_view("w_hi", "hT", 0, HI_BUFS * SUB)
        lo_ring = r_view("lo_ring", "ring", 0, MIX_SLOTS * SLOT)
        lo_extra = r_view("lo_extra", "M", 11776, (MOE_SLOTS - MIX_SLOTS) * SLOT)
        ath = r_view("ath", "strip", HI_BUFS * SUB - KT * SEQ, 8 * CAP)[:, :].rearrange("p (b j c) -> p b j c", b=2, j=4)
        atl = r_view("atl", "M", 10800, 8 * CAP)[:, :].rearrange("p (b j c) -> p b j c", b=2, j=4)
        assert at["strip"] == at["hT"] + 4 * KT * SEQ
        router = m(10600, KT * NE, KT)

        def carve(mem, at=0):
            at = [at]

            def take(n, k=None):
                v = mem[:, at[0]:at[0] + n]
                at[0] += n
                return v if k is None else v.rearrange("p (k n) -> p k n", k=k)
            return take

        take = carve(gsm)
        ax, nab, lnp, gg = take(32, NT), take(32, NT), take(32, NT), take(32, NT)
        eb, beta = take(32, NT), take(32, NT)
        Gc = take(64, 4)
        dl, eG, kds, bG = take(32, 4), take(32, 4), take(32, 4), take(32, 4)
        cd = take(32).rearrange("p (i k c) -> p i k c", i=4, k=4)
        ea = take(16)
        osr = take(16)
        take = carve(att_s)
        mx, mneg, esink, psum16, rden = take(16), take(16), take(16), take(16), take(16)
        take = carve(lnst)
        bst, bag, rstd = take(24, NT), take(4, NT), take(2)
        take = carve(M, 10112)
        lg, m8, idxf, sel = take(16, NT), take(16, NT), take(4, NT), take(16, NT)
        oh = take(32).rearrange("p (k t e) -> p k t e", k=TOP_K, t=NT)
        dm12, e12, e12p = take(2), take(2), take(2)
        rw = take(4, NT)
        cnt, nch, end, sbase = take(8), take(8), take(8), take(8)
        pos, slot_e = take(16, NT), take(16, NT)
        pick = take(32).rearrange("p (k t e) -> p k t e", k=TOP_K, t=NT)
        rslot = take(4, NT)
        cmp_p = take(MAXP * NE, MAXP)
        idf = take(MAXP)

        def slot(s):
            return ring_mem[:, s * SLOT:(s + 1) * SLOT] if s < MIX_SLOTS else m(11776 + (s - MIX_SLOTS) * SLOT, SLOT)

        def w_lo(s):
            return lo_ring[:, s * SLOT:(s + 1) * SLOT] if s < MIX_SLOTS else lo_extra[:, (s - MIX_SLOTS) * SLOT:(s - MIX_SLOTS + 1) * SLOT]

        def gate_at(unit, n=1):
            v = slot(3) if unit < 8 else gates1
            return v[:, (unit % 8) * 512:(unit % 8 + n) * 512]

        ring = mixer_ring()
        dense = mixer_ring()
        used = {"dk": ("p1_mm", 4), "dq": ("p1_mm", 8), "dv": ("p1_mm", 12), "kvab": ("p1_mm", 17), "q": ("p1_mm", 21),
                "z": ("p1_mm", 23), "pu": ("p1_mm", 25), "pool": ("up_ev", 8)}
        for a, n in enumerate(GATE_ORDER):
            used[f"gate{n}0"], used[f"gate{n}1"] = ("gate_mm", 4 * a + 2), ("gate_mm", 4 * a + 4)
            used[f"branch{n}"] = ("up_mm", 4 * a + 4)
        used["out0"], used["out1"] = ("out_mm", 2), ("out_mm", 4)
        FB = [(f, min(512, DFF - f)) for f in range(0, DFF, 512)]
        NF = DFF // P
        DPARTS = [("g", 0), ("u", 0)] + [(w, f + (w != "w")) for f in range(NF - 1) for w in "guw"] + [("w", NF - 1)]
        for b in range(len(FB)):
            for j, w in enumerate("guw"):
                dense.add(f"{w}{b}", (4, 5, 1, 2, 3, 0)[(3 * b + j) % DENSE_SLOTS])
                used[f"{w}{b}"] = ("part_mm", DPARTS.index((w, (FB[b][0] + FB[b][1]) // P - 1)) + 1)
        NFB = DFFE // 512
        moe = mixer_ring()
        def dense_part(mem, w, f):
            b, j = f // 4, f % 4
            if w == "w":
                return mem(dense.slot[f"w{b}"])[:, j * SUB:j * SUB + SUB]
            n = FB[b][1]
            return mem(dense.slot[f"{w}{b}"])[:, 0:KT * n].rearrange("p (k n) -> p k n", k=KT)[:, :, j * P:j * P + P]

        def dense_hi(n, w):
            v = dw_hi[:, (n % HI_BUFS) * SUB:(n % HI_BUFS) * SUB + SUB]
            return v if w == "w" else v.rearrange("p (k n) -> p k n", k=KT)

        PASS_ORDER = ["g0", "u0"] + [f"{w}{b + (w != 'w')}" for b in range(NFB - 1) for w in "guw"] + [f"w{NFB - 1}"]
        ahead_full = [moe.count[s] + 16 for s in range(MOE_SLOTS)]
        moe.count = list(ahead_full)
        for k, name in enumerate(PASS_ORDER):
            moe.add(name, k % MOE_SLOTS)
        PARTS = SLOT // SUB
        AHEAD = HI_BUFS - 1
        SUBS = PARTS * len(PASS_ORDER)
        last_part = {name: PARTS * k + PARTS - 1 for k, name in enumerate(PASS_ORDER)}
        PASS_CHUNKS = 3 * NFB
        PASS_ROUNDS = PASS_CHUNKS // MOE_SLOTS
        assert PASS_CHUNKS % MOE_SLOTS == 0

        def beside_dense(n, product, split):
            end = n == len(DPARTS) - 1
            for f in range(NF):
                at_n = DPARTS.index(("u", f)) + HI_BUFS - 1
                if n == at_n or end and at_n > n:
                    product(f)
                if n == at_n + 1 or end and at_n + 1 > n:
                    split(f)

        def after_part(n, product, turned_a, combine, tokens):
            lead = HI_BUFS - 1
            for b in range(NFB):
                if n == last_part[f"u{b}"] + lead:
                    product(b)
                if n == (last_part[f"g{b + 1}"] if b < NFB - 1 else last_part[f"u{b}"] + 1) + lead:
                    turned_a(b)
            if n == last_part["g1"] + lead:
                combine()
            if n == last_part[f"u{NFB - 1}"] + lead:
                tokens()

        consts_in = sem("consts_in")
        x_in = sem("x_in")
        rel_in = sem("rel_in")
        rows_mm = sem("rows_mm")
        rows_ev = sem("rows_ev")
        rows_out = sem("rows_out")
        strip_in = sem("strip_in")
        next_layer = sem("next_layer")
        out_done = sem("out_done")
        params_in, poolw_in, router_in = sem("params_in"), sem("poolw_in"), sem("router_in")
        ln1_in, ln2_in = sem("ln1_in"), sem("ln2_in")
        N_PARAMS = 5

        cleared, by_name = [], {}

        def lsem(name):
            cleared.append(sem(name))
            by_name[name] = cleared[-1]
            return cleared[-1]

        full = [lsem(f"full{s}") for s in range(MOE_SLOTS)]
        tr_mm, tr_a, tr_d = lsem("tr_mm"), lsem("tr_a"), lsem("tr_d")
        p1_mm, p1_ev = lsem("p1_mm"), lsem("p1_ev")
        pads = lsem("pads")
        conv_st = lsem("conv_st")
        silu_done = lsem("silu_done")
        sq_done, ss_mm, rs_done, nrm_done = lsem("sq_done"), lsem("ss_mm"), lsem("rs_done"), lsem("nrm_done")
        dg_v, dg_a = lsem("dg_v"), lsem("dg_a")
        sc_mm, sc_ev, sm_v, sm_a, pn_done = lsem("sc_mm"), lsem("sc_ev"), lsem("sm_v"), lsem("sm_a"), lsem("pn_done")
        pt_mm, pt_ev, pv_mm, pv_ev = lsem("pt_mm"), lsem("pt_ev"), lsem("pv_mm"), lsem("pv_ev")
        pool_mm, pool_ev = lsem("pool_mm"), lsem("pool_ev")
        kv_mm, kv_ev = lsem("kv_mm"), lsem("kv_ev")
        gc_mm, gc_v, gc_a = lsem("gc_mm"), lsem("gc_v"), lsem("gc_a")
        grow_mm, beta_mm, kk_mm, qk_mm, gp_mm = (lsem(n) for n in ("grow_mm", "beta_mm", "kk_mm", "qk_mm", "gp_mm"))
        dm_done, dexp_done, kkd_done, at_done, qkd_done = (lsem(n) for n in ("dm_done", "dexp_done", "kkd_done", "at_done", "qkd_done"))
        egp_done, qdec_done, rhs_done, xt0_st = (lsem(n) for n in ("egp_done", "qdec_done", "rhs_done", "xt0_st"))
        x_mm, x_ev, al_done, y_mm, y_ev, xy_mm, xt_done = (lsem(n) for n in ("x_mm", "x_ev", "al_done", "y_mm", "y_ev", "xy_mm", "xt_done"))
        uw_mm, u_ev, w_ev = lsem("uw_mm"), lsem("u_ev"), lsem("w_ev")
        s_zero, ws_mm, vn_done, st_mm, sc_done, s_done, o_ev = (lsem(n) for n in ("s_zero", "ws_mm", "vn_done", "st_mm", "sc_done", "s_done", "o_ev"))
        zn_done, osq_done, or_v, or_a, od_done, ot_mm, ot_ev = (lsem(n) for n in ("zn_done", "osq_done", "or_v", "or_a", "od_done", "ot_mm", "ot_ev"))
        gate_raw = lsem("gate_raw")
        gate_mm, gate_ev, up_mm, up_ev, mrg = lsem("gate_mm"), lsem("gate_ev"), lsem("up_mm"), lsem("up_ev"), lsem("mrg")
        mt_mm, mt_a, mt_d, out_mm = lsem("mt_mm"), lsem("mt_a"), lsem("mt_d"), lsem("out_mm")
        res1, lnv, lna = lsem("res1"), lsem("lnv"), lsem("lna")
        ln1_done = lsem("ln1_done")
        sg_ev, af_ev = lsem("sg_ev"), lsem("af_ev")
        res2, ln2_half, layer_done, arrived = (lsem(n) for n in ("res2", "ln2_half", "layer_done", "arrived"))
        rl_mm, rl_v, rl_a, rc_mm, ids_done = (lsem(n) for n in ("rl_mm", "rl_v", "rl_a", "rc_mm", "ids_done"))
        dispv, xg_mm, xgh_ev, xgl_ev = (lsem(n) for n in ("dispv", "xg_mm", "xgh_ev", "xgl_ev"))
        part_hi, part_lo, part_mm = lsem("part_hi"), lsem("part_lo"), lsem("part_mm")
        at_mm, ath_ev, atl_ev = lsem("at_mm"), lsem("ath_ev"), lsem("atl_ev")
        dath_ev, datl_ev = lsem("dath_ev"), lsem("datl_ev")
        ct_mm, ct_ev, ya_ev, yd_ev, cb_mm, acc_add = (lsem(n) for n in ("ct_mm", "ct_ev", "ya_ev", "yd_ev", "cb_mm", "acc_add"))

        N_P1 = 25
        block = es.enter_context(nc.Block())

        @block.sync
        def _(sp):
            sp.dma_start(cst[:, :], A["consts"]).then_inc(consts_in, 16)
            sp.dma_start(h, A["x"][0].rearrange("(t p) d -> p t d", p=P)).then_inc(x_in, 16)
            with sp.Fori(0, DEPTH) as l:
                w_in = A["w_in"][bass.ds(l, 1)].rearrange("a (k p) n -> p (a k) n", p=P)
                w_br = A["w_branch"][bass.ds(l, 1)]
                w_out = A["w_out"][bass.ds(l, 1)].rearrange("a (k p) n -> p (a k) n", p=P)

                def wait_used(name):
                    which, value = used[name]
                    sp.wait_ge(by_name[which], value)

                def put(name, src, at=0):
                    s = ring.slot[name]
                    if ring.before[name] and at == 0:
                        wait_used(ring.before[name])
                    n = src.shape[1] * src.shape[2]
                    dst = slot(s)[:, at:at + n].rearrange("p (k n) -> p k n", k=src.shape[1])
                    sp.dma_start(dst, src).then_inc(full[s], 16)

                put("dk", w_in[:, :, C_DK:C_DK + 512])
                put("dq", w_in[:, :, C_DQ:C_DQ + 512])
                put("dv", w_in[:, :, C_DV:C_DV + 512])
                put("kvab", w_in[:, :, C_K:C_K + 256])
                put("kvab", w_in[:, :, C_AB:C_AB + 32], 2048)
                put("q", w_in[:, :, C_Q:C_Q + 512])
                put("z", w_in[:, :, C_Z:C_Z + 512])
                put("pu", w_in[:, :, C_PU:C_PU + 512])
                put("pool", A["pool_c"].rearrange("p t g s -> p (t g) s"))
                for n in GATE_ORDER:
                    for hf in range(2):
                        c = C_G + n * D + hf * 512
                        put(f"gate{n}{hf}", w_in[:, :, c:c + 512])
                for n in GATE_ORDER:
                    wb = w_br[:, n].rearrange("a r n -> (a r) n")
                    if n == 0:
                        s = ring.slot["branch0"]
                        wait_used(ring.before["branch0"])
                        src = wb.rearrange("(e t d) n -> e d t n", e=2, t=4)
                        dst = slot(s).rearrange("p (t n) -> p t n", t=4)
                        for e in range(2):
                            sp.dma_start(dst[HD * e:HD * e + HD], src[e]).then_inc(full[s], 16)
                    else:
                        put(f"branch{n}", wb.rearrange("(t p) n -> p t n", p=P))
                for hf in range(2):
                    put(f"out{hf}", w_out[:, :, hf * 512:hf * 512 + 512])

                def put_dense(name, src):
                    s = dense.slot[name]
                    if dense.before[name]:
                        wait_used(dense.before[name])
                    elif s == MIX_SLOTS:
                        sp.wait_ge(ot_ev, 2)
                    n = src.shape[1] * src.shape[2]
                    sp.dma_start(slot(s)[:, 0:n].rearrange("p (k n) -> p k n", k=src.shape[1]), src).then_inc(full[s], 16)

                with sp.If(l < 1):
                    g, u, w = A["ffn_w1"][0], A["ffn_w3"][0], A["ffn_w2"][0]
                    for b, (f, n) in enumerate(FB):
                        put_dense(f"g{b}", g.rearrange("(k p) n -> p k n", p=P)[:, :, f:f + n])
                        put_dense(f"u{b}", u.rearrange("(k p) n -> p k n", p=P)[:, :, f:f + n])
                        put_dense(f"w{b}", w[f:f + n].rearrange("(k p) n -> p k n", p=P))
                with sp.Else():
                    def expert(e):
                        return (A["moe_wg"][0, e].rearrange("a (k p) n -> p (a k) n", p=P),
                                A["moe_wu"][0, e].rearrange("a (k p) n -> p (a k) n", p=P),
                                A["moe_wd"][0, e].rearrange("a (f k p) n -> f p (a k) n", p=P, k=4))

                    def chunk(k, weights):
                        name = PASS_ORDER[k]
                        w, b = weights["guw".index(name[0])], int(name[1])
                        src = w[b] if name[0] == "w" else w[:, :, b * 512:b * 512 + 512]
                        s = k % MOE_SLOTS
                        sp.dma_start(slot(s).rearrange("p (k n) -> p k n", k=src.shape[1]), src).then_inc(full[s], 16)

                    first = expert(slice(0, 1))
                    sp.wait_ge(ot_ev, 2)
                    for s in (4, 5, 1, 2, 6, 3, 0):
                        if s < MIX_SLOTS:
                            wait_used(ring.last[s])
                        elif s == MOE_SLOTS - 1:
                            sp.wait_ge(up_ev, 12)
                        chunk(s, first)
                    sp.wait_ge(ids_done, 1)
                    total = sp.value_load(ids[0:1, MAXP:MAXP + 1], min_val=1, max_val=MAXP)
                    e0 = sp.value_load(ids[0:1, 0:1], min_val=0, max_val=NE - 1)
                    for s in range(MOE_SLOTS):
                        sp.wait_ge(full[s], ahead_full[s])
                    with sp.If(e0 > 0):
                        first = expert(bass.ds(e0, 1))
                        for k in range(MOE_SLOTS):
                            chunk(k, first)
                    with sp.Else():
                        for s in range(MOE_SLOTS):
                            sp.sem_inc(full[s], 16)
                    with sp.Fori(0, MAXP) as p:
                        def ready(k, turn):
                            sp.wait_ge(part_mm, p * SUBS + (turn * SUBS + SUBS + PARTS * (k + 1 - MOE_SLOTS)))

                        with sp.If(p < total):
                            e = sp.value_load(ids[0:1, bass.ds(p, 1)], min_val=0, max_val=NE - 1)
                            weights = expert(bass.ds(e, 1))
                            for k in range(MOE_SLOTS, PASS_CHUNKS):
                                ready(k, 0)
                                chunk(k, weights)
                        with sp.If(p + 1 < total):
                            e = sp.value_load(ids[0:1, bass.ds(p + 1, 1)], min_val=0, max_val=NE - 1)
                            weights = expert(bass.ds(e, 1))
                            for k in range(MOE_SLOTS):
                                ready(k, 1)
                                chunk(k, weights)
                sp.wait_ge(layer_done, 1)
                sp.wait_ge(arrived, 4)
                for s in cleared:
                    sp.sem_clear(s)
                sp.sem_inc(next_layer, 1)
            sp.dma_start(out[0].rearrange("(t p) d -> p t d", p=P), h).then_inc(out_done, 16)
            sp.wait_ge(out_done, 16)

        @block.gpsimd
        def _(pool):
            g = nc.gpsimd
            hot = M[0:N_BUCKETS, 0:512]
            pool.dma_start(hot, A["hot"]).then_inc(rel_in, 16)
            pool.dma_start(M[0:N_BUCKETS, 512:520], A["rel_bias"]).then_inc(rel_in, 16)
            pool.dma_start(M[0:QH, 1024:1536], A["band"]).then_inc(rel_in, 16)
            pool.wait_ge(rows_ev, 1)
            pool.dma_start(A["rows"], M[0:QH, 1536:2048].rearrange("h (a n) -> h a n", a=1).to_broadcast([QH, P, 512])).then_inc(rows_out, 16)
            pool.wait_ge(rows_out, 16)
            rows = A["rows"]
            shifted = bass.AP(rows.tensor, rows.offset + P - 1, [[511, P], [P * 512, QH], [1, STRIP]])
            pool.dma_start(strip, shifted).then_inc(strip_in, 16)
            with pool.Fori(0, DEPTH) as l:
                def row(name, n):
                    return A[name][bass.ds(l, 1)].to_broadcast([P, n])

                g.memset(convin[:, :, 0:2], 0.0).then_inc(pads, 1)
                g.memset(convin[:, :, 258:260], 0.0).then_inc(pads, 1)
                pool.dma_start(convw[:, :], A["conv_w"][bass.ds(l, 1)].rearrange("a p n -> p (a n)")).then_inc(params_in, 16)
                pool.dma_start(dnrow[:, :], row("dn_rows", 32)).then_inc(params_in, 16)
                pool.dma_start(normw[:, :], row("dn_norm_w", HD)).then_inc(params_in, 16)
                pool.dma_start(poolsc[:, :], A["pool_scale"][bass.ds(l, 1)].rearrange("a p n -> p (a n)")).then_inc(params_in, 16)
                pool.dma_start(sinkr[:, :], row("sinks", 16)).then_inc(params_in, 16)
                pool.dma_start(poolw, A["pool_w"][bass.ds(l, 1)].rearrange("a g c d -> c (a g) d")).then_inc(poolw_in, 16)
                for c in range(4):
                    src = (kT if c < 2 else qT)[:, 2 * (c % 2):2 * (c % 2) + 2, :].rearrange("p a b -> p (a b)")
                    pool.wait_ge(silu_done, c + 1)
                    g.tensor_tensor(sq[:, c, :], src, src, ALU.mult).then_inc(sq_done, 1)
                pool.wait_ge(params_in, l * (16 * N_PARAMS) + 16 * N_PARAMS)
                pool.wait_ge(p1_ev, 23)
                for T in range(NT):
                    v = zs[:, T, :].rearrange("p (h d) -> p h d", h=DNH)
                    g.tensor_tensor(v, v, normw[:, :].rearrange("p (a d) -> p a d", a=1).to_broadcast([P, DNH, HD]),
                                    ALU.mult).then_inc(zn_done, 1)
                pool.wait_ge(pool_mm, 2)
                g.memset(M[:, 8192:9216], 0.0).then_inc(s_zero, 1)

                def set_tiles(i):
                    d, T = SETS[i]
                    kp = i % 2

                    def head(v):
                        return v.rearrange("p (h c) -> p h c", h=DNH)

                    def scale(v):
                        return v.rearrange("p (h c) -> p h c", c=1).to_broadcast([P, DNH, HD])

                    if i == 0:
                        pool.wait_ge(kv_ev, 4)
                        pool.wait_ge(gc_a, 2)
                        pool.wait_ge(gc_v, 6)
                        pool.wait_ge(pv_ev, 2)
                    else:
                        pool.wait_ge(uw_mm, i)
                    if i >= 2:
                        pool.wait_ge(st_mm, 4)
                    g.tensor_tensor(head(Rv), head(vtok[:, T, :]), scale(beta[:, T, 8 * d:8 * d + 8]), ALU.mult).then_inc(rhs_done, 1)
                    g.tensor_tensor(head(Rw), head(ktok[:, T, :]), scale(bG[:, i, :]), ALU.mult).then_inc(rhs_done, 1)
                    g.tensor_tensor(head(kdec[kp]), head(ktok[:, T, :]), scale(kds[:, i, :]), ALU.mult).then_inc(rhs_done, 1)
                    pool.wait_ge(at_done, i + 1)
                    lv = C(f"lvl{d}0").rearrange("p (a c) -> p a c", a=1).to_broadcast([P, 8, P])
                    idb = ident.rearrange("p (a c) -> p a c", a=1).to_broadcast([P, 8, P])
                    g.tensor_tensor(AL, AT, lv, ALU.mult).then_inc(xt0_st, 1)
                    pool.wait_ge(xt0_st, 2 * i + 1)
                    g.tensor_tensor(XT, idb, AL, ALU.subtract).then_inc(xt0_st, 1)
                    pool.wait_ge(xt0_st, 2 * i + 2)
                    pool.wait_ge(egp_done, i + 1)
                    g.tensor_tensor(qdec[kp], qT[:, :, T * P:T * P + P], eGp, ALU.mult).then_inc(qdec_done, 1)
                    g.tensor_copy(cd[:, i, :, :], eGp[:, :, (CHUNK - 1 if d == 0 else 0)::CHUNK]).then_inc(qdec_done, 1)
                    for lev in range(1, LEVELS):
                        lv = C(f"lvl{d}{lev}").rearrange("p (a c) -> p a c", a=1).to_broadcast([P, 4, P])
                        for q in range(2):
                            n = (i * 5 + lev - 1) * 2 + q
                            if lev > 1:
                                pool.wait_ge(y_mm, n - 1)
                            g.tensor_tensor(AL[:, 4 * q:4 * q + 4, :], AT[:, 4 * q:4 * q + 4, :], lv, ALU.mult).then_inc(al_done, 1)

                def scan_step(n):
                    for d in range(2):
                        i = 2 * (n // 2) + d
                        c = n if d == 0 else 3 - n
                        k = 2 * n + d
                        if n == 0:
                            pool.wait_ge(s_zero, 1)
                            pool.wait_ge(qdec_done, 4)
                        elif n == 2:
                            pool.wait_ge(qdec_done, 8)
                        if n:
                            pool.wait_ge(s_done, 2 * (k - 1))
                        cc = cd[:, i, :, c % 2].rearrange("p (k o) -> p k o", o=1).to_broadcast([P, 4, P])
                        g.tensor_tensor(Sc[:, d], S[:, d], cc, ALU.mult).then_inc(sc_done, 1)

                set_tiles(0)
                set_tiles(1)
                scan_step(0)
                scan_step(1)
                set_tiles(2)
                set_tiles(3)
                scan_step(2)
                scan_step(3)
                pool.wait_ge(o_ev, 8)
                pool.wait_ge(uw_mm, 4)
                for T in range(NT):
                    g.tensor_tensor(M[:, 17408 + 512 * T:17920 + 512 * T], osum[:, T, :], osum[:, T, :], ALU.mult).then_inc(osq_done, 1)
                pool.wait_ge(ot_ev, 2)
                pool.dma_start(lng, row("ln1_g", D)).then_inc(ln1_in, 16)
                pool.dma_start(lnb, row("ln1_b", D)).then_inc(ln1_in, 16)
                for k in range(4, 12):
                    T, hf = (k % 4) % 2, (k % 4) // 2
                    mv = merged[:, T, hf * 512:hf * 512 + 512]
                    pool.wait_ge(up_ev, k + 1)
                    if k >= 8:
                        pool.wait_ge(mrg, k - 4 - 3)
                    g.tensor_tensor(mv, mv, gtmp[:, k % 2, :], ALU.add).then_inc(mrg, 1)
                pool.wait_ge(ln1_done, NT)
                pool.dma_start(lng, row("ln2_g", D)).then_inc(ln2_in, 16)
                pool.dma_start(lnb, row("ln2_b", D)).then_inc(ln2_in, 16)
                with pool.If(l < 1):
                    pool.wait_ge(layer_done, 1)
                with pool.Else():
                    pool.dma_start(router, A["router_w"][0].rearrange("(k p) e -> p k e", p=P)).then_inc(router_in, 16)
                    pool.wait_ge(layer_done, 1)
                pool.sem_inc(arrived, 1)
                pool.wait_ge(next_layer, l + 1)

        @block.tensor
        def _(pe):
            t = nc.tensor

            def mm(o, a, b, start=True, stop=True, shared=False):
                return t.matmul(o, a, b, start=start, stop=stop, skip_group_check=shared)

            pe.wait_ge(consts_in, 16)
            pe.wait_ge(rel_in, 48)
            mm(ps[0][0:QH, :], M[0:N_BUCKETS, 512:520], M[0:N_BUCKETS, 0:512]).then_inc(rows_mm, 1)
            pe.wait_ge(rows_ev, 1)
            pe.wait_ge(x_in, 16)
            with pe.Fori(0, DEPTH) as l:
                def loaded(r, name):
                    pe.wait_ge(full[r.slot[name]], r.full[name])

                def turn_h():
                    for i in range(4):
                        T, kq = i // 2, i % 2
                        for j in range(4):
                            k = 4 * kq + j
                            last = t.transpose(ps[i][:, j * P:j * P + P], h[:, T, k * P:k * P + P], ident)
                        last.then_inc(tr_mm, 1)

                turn_h()
                pe.wait_ge(tr_a, 2)
                pe.wait_ge(tr_d, 2)
                unit = [0]

                def p1(kind, name, col, ncol, width, T=None):
                    u = unit[0]
                    if u >= 4:
                        pe.wait_ge(p1_ev, u - 3)
                    loaded(ring, name)
                    w = slot(ring.slot[name])[:, col:col + KT * width].rearrange("p (k n) -> p k n", k=KT)
                    o = ps[4 + u % 4]
                    for k in range(KT):
                        if kind == "T":
                            last = mm(o[:, 0:SEQ], w[:, k, ncol:ncol + P], hT[:, k, :], k == 0, k == KT - 1)
                        else:
                            last = mm(o[:, 0:width], hT[:, k, T * P:T * P + P], w[:, k, :], k == 0, k == KT - 1)
                    last.then_inc(p1_mm, 1)
                    unit[0] += 1

                for name in ("dk", "dq", "dv"):
                    for j in range(4):
                        p1("T", name, 0, j * P, 512)
                kv = slot(ring.slot["kvab"])

                def p1_kv():
                    u = unit[0]
                    loaded(ring, "kvab")
                    w = kv[:, 0:2048].rearrange("p (k n) -> p k n", k=KT)
                    wab = kv[:, 2048:2304].rearrange("p (k n) -> p k n", k=KT)
                    pe.wait_ge(p1_ev, u - 3)
                    for k in range(KT):
                        last = mm(ps[4 + u % 4][:, 0:SEQ], w[:, k, 0:P], hT[:, k, :], k == 0, k == KT - 1)
                    last.then_inc(p1_mm, 1)
                    for what, n, off in ((w, P, P), (wab, 32, 0)):
                        for T in range(NT):
                            unit[0] += 1
                            u = unit[0]
                            pe.wait_ge(p1_ev, u - 3)
                            for k in range(KT):
                                last = mm(ps[4 + u % 4][:, 0:n], hT[:, k, T * P:T * P + P], what[:, k, off:off + n], k == 0, k == KT - 1)
                            last.then_inc(p1_mm, 1)
                    unit[0] += 1

                p1_kv()
                for j in range(4):
                    p1("T", "q", 0, j * P, 512)
                for T in range(NT):
                    p1("R", "z", 0, 0, 512, T)
                for c in range(4):
                    pe.wait_ge(sq_done, c + 1)
                    mm(ps[c][:, :], C("blk"), sq[:, c, :]).then_inc(ss_mm, 1)

                def score(n):
                    e = n % 2
                    if n < 4:
                        pe.wait_ge(rs_done, 2 * n + 1)
                    else:
                        pe.wait_ge(sc_ev, n - 3)
                    for i in (n - e, n - e + 1):
                        Q, tt, r = i // 4, i % 4, HD * e
                        last = mm(ps[n % 4][:, (i % 2) * SEQ:(i % 2) * SEQ + SEQ], qA[r:r + HD, tt, Q * P:Q * P + P], kA[r:r + HD, :])
                    last.then_inc(sc_mm, 1)

                pe.wait_ge(p1_ev, 21)
                for n in range(4):
                    score(n)
                p1("R", "pu", 0, 0, 512, 0)
                for n in range(4, 8):
                    score(n)
                p1("R", "pu", 0, 0, 512, 1)
                pe.wait_ge(p1_ev, N_P1)
                for b, src in ((0, vT), (1, kT)):
                    if b:
                        pe.wait_ge(nrm_done, 4)
                    else:
                        pe.wait_ge(silu_done, 6)
                    for T in range(NT):
                        for j in range(4):
                            last = t.transpose(ps[4 + 2 * b + T][:, j * P:j * P + P], src[:, j, T * P:T * P + P], ident)
                        last.then_inc(kv_mm, 1)
                loaded(ring, "pool")
                B = slot(ring.slot["pool"])[:, 0:2048].rearrange("p (t g s) -> p t g s", t=NT, g=BT)
                for b in range(2):
                    pe.wait_ge(kv_ev, b + 1)
                    for g2 in range(2):
                        grp = 2 * b + g2
                        for T in range(NT):
                            last = mm(ps[4 + b][:, g2 * SEQ:g2 * SEQ + SEQ], pu[:, T, grp * P:grp * P + P], B[:, T, grp, :],
                                      T == 0, T == NT - 1)
                last.then_inc(pool_mm, 1)
                pe.wait_ge(pool_ev, 2)
                pe.wait_ge(poolw_in, l * 16 + 16)
                for b in range(2):
                    pe.wait_ge(kv_ev, b + 3)
                    for g2 in range(2):
                        grp = 2 * b + g2
                        last = mm(ps[6 + b][:, g2 * SEQ:g2 * SEQ + SEQ], poolw[:, grp, :], mixT[:, grp, :])
                last.then_inc(pool_mm, 1)
                pe.wait_ge(sc_ev, 8)
                for i in range(8):
                    Q, tt = i // 4, i % 4
                    pe.wait_ge(pn_done, i + 1)
                    if i >= 2:
                        pe.wait_ge(pt_ev, i - 1)
                    for e in range(2):
                        for jt in range(NT):
                            last = t.transpose(ps[i % 2][:, (2 * e + jt) * P:(2 * e + jt + 1) * P],
                                               Sall[:, i, e, jt * P:jt * P + P], ident)
                    last.then_inc(pt_mm, 1)

                    pe.wait_ge(pt_ev, i + 1)
                    for e in range(2):
                        for jt in range(NT):
                            last = mm(ps[2 + Q][HD * e:HD * e + HD, tt * P:tt * P + P], vA[:, jt, HD * e:HD * e + HD],
                                      PT[:, i % 2, (2 * e + jt) * P:(2 * e + jt + 1) * P], jt == 0, jt == NT - 1)
                    last.then_inc(pv_mm, 1)
                pe.wait_ge(dg_v, 6)
                for i, (d, T) in enumerate(SETS):
                    gi = gg[:, T, 8 * d:8 * d + 8]
                    mm(ps[4][:, 16 * i:16 * i + 8], C(f"cum{d}"), gi)
                    last = mm(ps[4][:, 16 * i + 8:16 * i + 16], C("blk"), gi)
                last.then_inc(gc_mm, 1)
                pe.wait_ge(pv_ev, 2)
                pe.wait_ge(gc_v, 1)
                pe.wait_ge(pool_ev, 6)

                filled = [0]

                def fill(n):
                    for _ in range(n):
                        unit, k = divmod(filled[0], KT)
                        filled[0] += 1
                        name, T = GATES[unit // 2], unit % 2
                        if k == 0:
                            loaded(ring, name)
                            if unit >= 2:
                                pe.wait_ge(gate_raw, unit - 1)
                        w = slot(ring.slot[name]).rearrange("p (k n) -> p k n", k=KT)
                        last = mm(ps[6 + unit % 2][:, :], hT[:, k, T * P:T * P + P], w[:, k, :], k == 0, k == KT - 1)
                        if k == KT - 1:
                            last.then_inc(gate_mm, 1)

                def inverse_and_sides(i):
                    d, T = SETS[i]
                    kp = i % 2
                    if i:
                        pe.wait_ge(x_ev, 10 * i)
                        pe.wait_ge(y_ev, 10 * i)
                        pe.wait_ge(xt_done, 10 * i)
                        pe.wait_ge(u_ev, i)
                        pe.wait_ge(w_ev, i)
                    if i == 2:
                        pe.wait_ge(s_done, 8)
                        pe.wait_ge(o_ev, 4)
                    for w, hh in enumerate(HEAD_AT):
                        o = ps[w // 4][:, (w % 4) * P:(w % 4) * P + P]
                        last = mm(o, gg[:, T, 8 * d + hh:8 * d + hh + 1].to_broadcast([P, P]), C(f"cum{d}"))
                    last.then_inc(grow_mm, 1)
                    for w, hh in enumerate(HEAD_AT):
                        pr, r = hh // 2, HD * (hh % 2)
                        kh = kT[r:r + HD, pr, T * P:T * P + P]
                        last = mm(ps[4 + w // 4][:, (w % 4) * P:(w % 4) * P + P], kh, kh)
                    last.then_inc(kk_mm, 1)
                    for w, hh in enumerate(HEAD_AT):
                        last = mm(ps[2 + w // 4][:, (w % 4) * P:(w % 4) * P + P],
                                  beta[:, T, 8 * d + hh:8 * d + hh + 1].to_broadcast([P, P]), ident)
                    last.then_inc(beta_mm, 1)
                    if i:
                        pe.wait_ge(gate_raw, 2 * i)
                    for w, hh in enumerate(HEAD_AT):
                        pr, r = hh // 2, HD * (hh % 2)
                        last = mm(ps[6 + w // 4][:, (w % 4) * P:(w % 4) * P + P], kT[r:r + HD, pr, T * P:T * P + P],
                                  qT[r:r + HD, pr, T * P:T * P + P])
                    last.then_inc(qk_mm, 1)
                    pe.wait_ge(dm_done, i + 1)
                    for hh in range(DNH):
                        r = HD * (hh % 2)
                        last = mm(ps[0][r:r + HD, (hh // 2) * P:(hh // 2) * P + P],
                                  gg[:, T, 8 * d + hh:8 * d + hh + 1].to_broadcast([P, HD]), C(f"cum{d}"))
                    last.then_inc(gp_mm, 1)
                    pe.wait_ge(egp_done, i + 1)
                    pe.wait_ge(at_done, i + 1)
                    pe.wait_ge(xt0_st, 2 * i + 2)
                    for lev in range(1, LEVELS):
                        for q in range(2):
                            n = (i * 5 + lev - 1) * 2 + q
                            if lev > 1:
                                pe.wait_ge(xt_done, n - 1)
                            for j in range(4):
                                last = t.transpose(ps[q][:, j * P:j * P + P], XT[:, 4 * q + j, :], ident)
                            last.then_inc(x_mm, 1)
                        if lev == 1:
                            pe.wait_ge(qkd_done, i + 1)
                        fill(2 if lev in (1, LEVELS - 1) else 1)
                        for q in range(2):
                            n = (i * 5 + lev - 1) * 2 + q
                            pe.wait_ge(x_ev, n + 1)
                            pe.wait_ge(al_done, n + 1)
                            for j in range(4):
                                last = mm(ps[2 + q][:, j * P:j * P + P], AL[:, 4 * q + j, :], X[:, 4 * q + j, :])
                            last.then_inc(y_mm, 1)
                        fill(1)
                        for q in range(2):
                            n = (i * 5 + lev - 1) * 2 + q
                            pe.wait_ge(y_ev, n + 1)
                            for j in range(4):
                                last = mm(ps[4 + q][:, j * P:j * P + P], Dm[:, 4 * q + j, :], XT[:, 4 * q + j, :])
                            last.then_inc(xy_mm, 1)
                        if lev < LEVELS - 1:
                            fill(1)
                    pe.wait_ge(xt_done, 10 * (i + 1))
                    pe.wait_ge(rhs_done, 3 * (i + 1))
                    pe.wait_ge(gate_raw, 2 * i + 2)
                    for w, hh in enumerate(HEAD_AT):
                        pr, r = hh // 2, HD * (hh % 2)
                        mm(ps[6][:, HD * hh:HD * hh + HD], XT[:, w, :], Rv[:, HD * hh:HD * hh + HD])
                        last = mm(ps[7][r:r + HD, pr * P:pr * P + P], Rw[:, HD * hh:HD * hh + HD], XT[:, w, :])
                    last.then_inc(uw_mm, 1)

                def scan_step(n):
                    if n % 2 == 0:
                        pe.wait_ge(u_ev, n + 2)
                        pe.wait_ge(w_ev, n + 2)
                        pe.wait_ge(qdec_done, 2 * (n + 2))
                        pe.wait_ge(xt_done, 10 * (n + 2))
                    if n == 0:
                        pe.wait_ge(s_zero, 1)
                    for d in range(2):
                        i, c, k = 2 * (n // 2) + d, (n if d == 0 else 3 - n), 2 * n + d
                        kp, r, b = i % 2, CHUNK * (c % 2), 3 * d
                        if n:
                            pe.wait_ge(s_done, 2 * (k - 1))
                            pe.wait_ge(o_ev, k - 1)
                        for pr in range(4):
                            mm(ps[b][r:r + CHUNK, pr * P:pr * P + P], wT[kp][:, pr, r:r + CHUNK], S[:, d, pr, :])
                            last = mm(ps[b + 1][r:r + CHUNK, pr * P:pr * P + P], qdec[kp][:, pr, r:r + CHUNK], S[:, d, pr, :],
                                      pr == 0, False, True)
                        last.then_inc(ws_mm, 1)
                    if n >= 2:
                        fill(4)
                    for d in range(2):
                        i, c, k = 2 * (n // 2) + d, (n if d == 0 else 3 - n), 2 * n + d
                        kp, r, b = i % 2, CHUNK * (c % 2), 3 * d
                        pe.wait_ge(vn_done, k + 1)
                        for pr in range(4):
                            mm(ps[b + 2][:, pr * P:pr * P + P], kdec[kp][r:r + CHUNK, pr * P:pr * P + P],
                               vnew[r:r + CHUNK, n % 2, pr * P:pr * P + P])
                        for w, hh in enumerate(HEAD_AT):
                            last = mm(ps[b + 1][r:r + CHUNK, HD * hh:HD * hh + HD], qkd[kp][r:r + CHUNK, w, r:r + CHUNK],
                                      vnew[r:r + CHUNK, n % 2, HD * hh:HD * hh + HD], False, w == DNH - 1, True)
                        last.then_inc(st_mm, 1)

                inverse_and_sides(0)
                inverse_and_sides(1)
                scan_step(0)
                scan_step(1)
                inverse_and_sides(2)
                inverse_and_sides(3)
                scan_step(2)
                scan_step(3)
                fill(3 * KT)
                pe.wait_ge(od_done, 1)
                for T in range(NT):
                    for j in range(4):
                        last = t.transpose(ps[4 + T][:, j * P:j * P + P], osum[:, T, j * P:j * P + P], ident)
                    last.then_inc(ot_mm, 1)
                pe.wait_ge(ot_ev, 2)
                pe.wait_ge(s_done, 16)
                pe.wait_ge(o_ev, 8)
                pe.wait_ge(gate_raw, 12)
                for a, n in enumerate(GATE_ORDER):
                    loaded(ring, f"branch{n}")
                    w = slot(ring.slot[f"branch{n}"]).rearrange("p (k n) -> p k n", k=BT)
                    src = (oAT, oDT, oPT)[n]
                    for hf in range(2):
                        for T in range(NT):
                            j = 2 * hf + T
                            if a:
                                pe.wait_ge(up_ev, 4 * (a - 1) + j + 1)
                            for k in range(BT):
                                last = mm(ps[4 + j][:, :], src[:, k, T * P:T * P + P], w[:, k, hf * 512:hf * 512 + 512],
                                          k == 0, k == BT - 1)
                            last.then_inc(up_mm, 1)
                pe.wait_ge(mrg, 8)
                for i in range(4):
                    T, kq = i // 2, i % 2
                    for j in range(4):
                        k = 4 * kq + j
                        last = t.transpose(ps[i][:, j * P:j * P + P], merged[:, T, k * P:k * P + P], ident)
                    last.then_inc(mt_mm, 1)
                pe.wait_ge(mt_a, 2)
                pe.wait_ge(mt_d, 2)
                for hf in range(2):
                    loaded(ring, f"out{hf}")
                    w = slot(ring.slot[f"out{hf}"]).rearrange("p (k n) -> p k n", k=KT)
                    for T in range(NT):
                        for k in range(KT):
                            last = mm(ps[4 + 2 * hf + T][:, :], mT[:, k, T * P:T * P + P], w[:, k, :], k == 0, k == KT - 1)
                        last.then_inc(out_mm, 1)
                pe.wait_ge(ln1_done, NT)
                turn_h()
                pe.wait_ge(res1, 4)
                with pe.If(l < 1):
                    pe.wait_ge(tr_d, 6)

                    def up(n, w, f):
                        if w == "g" and f >= 2:
                            pe.wait_ge(af_ev, f - 1)
                        pe.wait_ge(part_lo, n + 1)
                        hi, lo = dense_hi(n, w), dense_part(w_lo, w, f)
                        o = ps[f % 2][:, 0:SEQ] if w == "g" else ps[f % 2][:, SEQ:2 * SEQ]
                        for k in range(KT):
                            mm(o, hi[:, k, :], hTh[:, k, :], k == 0, False)
                            mm(o, hi[:, k, :], hTl[:, k, :], False, False)
                            last = mm(o, lo[:, k, :], hTh[:, k, :], False, k == KT - 1)
                        last.then_inc(part_mm, 1)

                    def down(n, f):
                        pe.wait_ge(datl_ev, f + 1)
                        pe.wait_ge(part_lo, n + 1)
                        hi, lo = dense_hi(n, "w"), dense_part(w_lo, "w", f)
                        for T in range(NT):
                            ah, al = dath[:, f % 4, T * P:T * P + P], datl[:, f % 4, T * P:T * P + P]
                            for dh in range(2):
                                o, c = ps[4 + 2 * T + dh][:, :], slice(dh * 512, dh * 512 + 512)
                                mm(o, ah, hi[:, c], f == 0, False)
                                mm(o, ah, lo[:, c], False, False)
                                last = mm(o, al, hi[:, c], False, f == NF - 1)
                        last.then_inc(part_mm, 1)

                    for n, (w, f) in enumerate(DPARTS):
                        if w == "w":
                            down(n, f)
                        else:
                            up(n, w, f)
                with pe.Else():
                    pe.wait_ge(tr_a, 4)
                    pe.wait_ge(tr_d, 4)
                    pe.wait_ge(router_in, 16)
                    for T in range(NT):
                        for k in range(KT):
                            last = mm(ps[T][:, 0:NE], hT[:, k, T * P:T * P + P], router[:, k, :], k == 0, k == KT - 1)
                        last.then_inc(rl_mm, 1)
                    pe.wait_ge(rl_v, 12)
                    one = scal[:, 3:4].to_broadcast([P, P])
                    mm(ps[2][:, 0:8], C("before"), sel[:, 0, :])
                    mm(ps[2][:, 8:16], C("before"), sel[:, 1, :], True, False)
                    mm(ps[2][:, 8:16], one, sel[:, 0, :], False, True)
                    mm(ps[2][:, 16:24], one, sel[:, 0, :], True, False)
                    mm(ps[2][:, 16:24], one, sel[:, 1, :], False, True).then_inc(rc_mm, 1)
                    pe.wait_ge(ids_done, 1)
                    pe.sem_inc(part_mm, SUBS)

                    def gather():
                        for k in range(KT):
                            for T in range(NT):
                                last = mm(ps[2 + k // 4][:, (k % 4) * CAP:(k % 4) * CAP + CAP], h[:, T, k * P:k * P + P],
                                          disp[:, T, :], T == 0, T == NT - 1)
                        last.then_inc(xg_mm, 1)

                    pe.wait_ge(dispv, 12)
                    gather()
                    total = pe.value_load(ids[0:1, MAXP:MAXP + 1], min_val=1, max_val=MAXP)
                    with pe.Fori(0, MAXP) as p:
                        with pe.If(p < total):
                            def part(name, s):
                                n = last_part[name] - (PARTS - 1) + s
                                pe.wait_ge(part_lo, p * SUBS + (n + 1))
                                at_hi = (n % HI_BUFS) * SUB
                                return w_hi[:, at_hi:at_hi + SUB], w_lo(moe.slot[name])[:, s * SUB:s * SUB + SUB]

                            def up(w, b):
                                o = ps[2 * (b % 2) + (w == "u")][0:CAP, :]
                                for s in range(PARTS):
                                    hi, lo = part(f"{w}{b}", s)
                                    for j in range(SUB // 512):
                                        k = (SUB // 512) * s + j
                                        hi_j, lo_j = hi[:, j * 512:j * 512 + 512], lo[:, j * 512:j * 512 + 512]
                                        mm(o, xgh[:, k, :], hi_j, k == 0, False)
                                        mm(o, xgh[:, k, :], lo_j, False, False)
                                        last = mm(o, xgl[:, k, :], hi_j, False, k == KT - 1)
                                    last.then_inc(part_mm, 1)

                            def turn_a(b):
                                pe.wait_ge(af_ev, p * NFB + (b + 1))
                                if b == NFB - 1:
                                    pe.wait_ge(atl_ev, p * NFB + b)
                                for j in range(4):
                                    last = t.transpose(ps[6][:, j * CAP:j * CAP + CAP], ae[0:CAP, b % 2, j * P:j * P + P], ident[0:CAP, 0:CAP])
                                last.then_inc(at_mm, 1)

                            def down(b):
                                pe.wait_ge(atl_ev, p * NFB + (b + 1))
                                for s in range(PARTS):
                                    hi, lo = part(f"w{b}", s)
                                    for a, w, stop in ((ath, hi, False), (ath, lo, False), (atl, hi, True)):
                                        for dh in range(2):
                                            last = mm(ps[4 + dh][0:CAP, :], a[:, b % 2, s, :], w[:, dh * 512:dh * 512 + 512],
                                                      b == 0 and s == 0 and a is ath and w is hi,
                                                      b == NFB - 1 and s == PARTS - 1 and stop)
                                    last.then_inc(part_mm, 1)

                            pe.wait_ge(xgl_ev, p * 2 + 2)
                            up("g", 0)
                            pe.wait_ge(acc_add, p * 4 + 4)
                            for T in range(NT):
                                last = t.transpose(ps[7][0:CAP, T * P:T * P + P], comb[:, T, :], ident)
                            last.then_inc(ct_mm, 1)
                            up("u", 0)
                            for b in range(1, NFB):
                                up("g", b)
                                if b < NFB - 1:
                                    turn_a(b - 1)
                                    up("u", b)
                                    down(b - 1)
                            turn_a(NFB - 2)
                            up("u", NFB - 1)
                            pe.wait_ge(dispv, p * 12 + 24)
                            gather()
                            turn_a(NFB - 1)
                            down(NFB - 2)
                            down(NFB - 1)
                            pe.wait_ge(ct_ev, p + 1)
                            for q in range(4):
                                T, dh = q // 2, q % 2
                                if q == 0:
                                    pe.wait_ge(ya_ev, p + 1)
                                if q == 1:
                                    pe.wait_ge(yd_ev, p + 1)
                                if q >= 2:
                                    pe.wait_ge(acc_add, p * 4 + (4 + q - 1))
                                mm(ps[7 - dh][:, :], combT[0:CAP, T, :], y[0:CAP, dh * 512:dh * 512 + 512]).then_inc(cb_mm, 1)
                pe.wait_ge(layer_done, 1)
                pe.sem_inc(arrived, 1)
                pe.wait_ge(next_layer, l + 1)

        @block.scalar
        def _(act):
            def f(o, i, func=ACT.Copy, **kw):
                return nc.scalar.activation(o, i, func, **kw)

            eps6, epsln, lnq = scal[:, 0:1], scal[:, 1:2], scal[:, 2:3]
            one = scal[:, 3:4]
            act.wait_ge(consts_in, 16)
            with act.Fori(0, DEPTH) as l:
                def turned(mm_sem, a_sem, dst, base):
                    for i in (0, 2):
                        T, kq = i // 2, i % 2
                        act.wait_ge(mm_sem, 4 * base + i + 1)
                        f(dst[:, 4 * kq:4 * kq + 4, T * P:T * P + P],
                          ps[i][:, :].rearrange("p (j q) -> p j q", j=4)).then_inc(a_sem, 1)

                turned(tr_mm, tr_a, hT, 0)
                act.wait_ge(pads, 2)
                dst = [convin[:, t, 2:258] for t in range(12)] + [kA, vA[:, 0, :], vA[:, 1, :], ab[:, 0, :], ab[:, 1, :]]
                dst += [qA[:, t, :] for t in range(4)] + [zs[:, 0, :], zs[:, 1, :], pu[:, 0, :], pu[:, 1, :]]

                def evac(u):
                    act.wait_ge(p1_mm, u + 1)
                    n = dst[u].shape[1]
                    f(dst[u], ps[4 + u % 4][:, 0:n], ACT.Silu if u in (21, 22) else ACT.Copy).then_inc(p1_ev, 1)

                def silu(j):
                    v = (kT, qT, vT)[j // 2][:, 2 * (j % 2):2 * (j % 2) + 2, :]
                    act.wait_ge(conv_st, 10 * (j + 1))
                    f(v, v, ACT.Silu).then_inc(silu_done, 1)

                for u in range(23):
                    evac(u)
                    if u >= 4 and u % 2 == 0 and (u - 4) // 2 < 6:
                        silu((u - 4) // 2)
                act.wait_ge(params_in, l * (16 * N_PARAMS) + 16 * N_PARAMS)
                f(ea, dnrow[:, 16:32], ACT.Exp).then_inc(dg_a, 1)
                act.wait_ge(dg_v, 2)
                f(lnp, nab, ACT.Exp, scale=-1.0).then_inc(dg_a, 1)
                act.wait_ge(dg_a, 2)
                f(lnp, lnp, ACT.Ln, bias=one).then_inc(dg_a, 1)
                act.wait_ge(p1_ev, 17)
                f(eb, ab[:, :, 16:32], ACT.Exp, scale=-1.0).then_inc(dg_a, 1)
                for c in range(4):
                    act.wait_ge(ss_mm, c + 1)
                    f(rs[:, c, :], ps[c][:, :], ACT.Ln, bias=eps6).then_inc(rs_done, 1)
                    act.wait_ge(rs_done, 2 * c + 1)
                    if c < 2:
                        f(rs[:, c, :], rs[:, c, :], ACT.Exp, scale=-0.5).then_inc(rs_done, 1)
                    else:
                        f(rs[:, c, :], rs[:, c, :], ACT.Exp, scale=-0.5, bias=lnq).then_inc(rs_done, 1)
                evac(23)
                evac(24)
                for b in range(4):
                    act.wait_ge(kv_mm, b + 1)
                    f((vtok, ktok)[b // 2][:, b % 2, :], ps[4 + b][:, :]).then_inc(kv_ev, 1)
                act.wait_ge(pool_mm, 1)
                for b in range(2):
                    f(mixT[:, 2 * b:2 * b + 2, :], ps[4 + b][:, :].rearrange("p (g s) -> p g s", g=2)).then_inc(pool_ev, 1)
                act.wait_ge(pool_mm, 2)
                for g in range(BT):
                    f(oPT[:, g, :], ps[6 + g // 2][:, (g % 2) * SEQ:(g % 2) * SEQ + SEQ], ACT.Identity,
                      scale=poolsc[:, g:g + 1]).then_inc(pool_ev, 1)
                act.wait_ge(sm_v, 11)
                for i in range(8):
                    for e in range(2):
                        c = 2 * i + e
                        f(Sall[:, i, e, :], Sall[:, i, e, :], ACT.Exp, bias=mneg[:, c:c + 1],
                          accum_out=psum16[:, c:c + 1]).then_inc(sm_a, 1)
                f(esink, esink, ACT.Exp).then_inc(sm_a, 1)
                for i in range(8):
                    act.wait_ge(pt_mm, i + 1)
                    if i >= 2:
                        act.wait_ge(pv_mm, i - 1)
                    f(PT[:, i % 2, :], ps[i % 2][:, :]).then_inc(pt_ev, 1)
                    if i % 4 == 3:
                        Q = i // 4
                        act.wait_ge(pv_mm, i + 1)
                        f(oAT[:, :, Q * P:Q * P + P], ps[2 + Q][:, :].rearrange("p (t q) -> p t q", t=4)).then_inc(pv_ev, 1)
                act.wait_ge(gc_v, 1)
                f(eG, Gc[:, :, 0:8], ACT.Exp).then_inc(gc_a, 1)
                act.wait_ge(gc_v, 2)
                f(kds, dl, ACT.Exp).then_inc(gc_a, 1)

                def gate_out(unit):
                    act.wait_ge(gate_mm, unit + 1)
                    f(gate_at(unit), ps[6 + unit % 2][:, :]).then_inc(gate_raw, 1)

                def set_tiles(i):
                    kp = i % 2
                    act.wait_ge(dm_done, i + 1)
                    f(Dm, Dm, ACT.Exp).then_inc(dexp_done, 1)
                    act.wait_ge(gp_mm, i + 1)
                    if i:
                        act.wait_ge(qdec_done, 2 * i)
                    f(eGp, ps[0][:, :].rearrange("p (k c) -> p k c", k=4), ACT.Exp).then_inc(egp_done, 1)
                    for lev in range(1, LEVELS):
                        for q in range(2):
                            n = (i * 5 + lev - 1) * 2 + q
                            act.wait_ge(x_mm, n + 1)
                            f(X[:, 4 * q:4 * q + 4, :], ps[q][:, :].rearrange("p (j c) -> p j c", j=4)).then_inc(x_ev, 1)
                        if lev == 1:
                            act.wait_ge(qkd_done, i + 1)
                        for q in range(2):
                            n = (i * 5 + lev - 1) * 2 + q
                            act.wait_ge(y_mm, n + 1)
                            f(Dm[:, 4 * q:4 * q + 4, :], ps[2 + q][:, :].rearrange("p (j c) -> p j c", j=4)).then_inc(y_ev, 1)
                        if lev == 3:
                            gate_out(2 * i)
                    gate_out(2 * i + 1)
                    act.wait_ge(uw_mm, i + 1)
                    f(u_s[kp], ps[6][:, :]).then_inc(u_ev, 1)

                def scan_out(n):
                    for d in range(2):
                        c, k = (n if d == 0 else 3 - n), 2 * n + d
                        r = CHUNK * (c % 2)
                        act.wait_ge(st_mm, k + 1)
                        f(osum[r:r + CHUNK, c // 2, :], ps[3 * d + 1][r:r + CHUNK, :]).then_inc(o_ev, 1)

                set_tiles(0)
                set_tiles(1)
                scan_out(0)
                scan_out(1)
                set_tiles(2)
                set_tiles(3)
                act.wait_ge(uw_mm, 4)
                gate_out(8)
                act.wait_ge(or_v, 1)
                f(osr, osr, ACT.Ln, scale=1.0 / HD, bias=eps6).then_inc(or_a, 1)
                act.wait_ge(or_a, 1)
                f(osr, osr, ACT.Exp, scale=-0.5).then_inc(or_a, 1)
                for unit in (9, 10, 11):
                    gate_out(unit)
                for T in range(NT):
                    act.wait_ge(ot_mm, T + 1)
                    f(oDT[:, :, T * P:T * P + P], ps[4 + T][:, :].rearrange("p (j q) -> p j q", j=4)).then_inc(ot_ev, 1)
                for a in range(NB):
                    act.wait_ge(gate_raw, 4 * a + 4)
                    f(gate_at(4 * a, 4), gate_at(4 * a, 4), ACT.Sigmoid).then_inc(gate_ev, 1)
                turned(mt_mm, mt_a, mT, 0)

                def norm(which):
                    for T in range(NT):
                        act.wait_ge(lnv, 10 * which + 3 * T + 3)
                        f(rstd[:, T:T + 1], bag[:, T, 1:2], ACT.Ln, bias=epsln).then_inc(lna, 1)
                        act.wait_ge(lna, 4 * which + 2 * T + 1)
                        f(rstd[:, T:T + 1], rstd[:, T:T + 1], ACT.Exp, scale=-0.5).then_inc(lna, 1)

                norm(0)
                with act.If(l < 1):
                    for i in range(4):
                        act.wait_ge(tr_mm, 4 + i + 1)
                        f(hTh[:, 4 * (i % 2):4 * (i % 2) + 4, (i // 2) * P:(i // 2) * P + P],
                          ps[i][:, :].rearrange("p (j q) -> p j q", j=4)).then_inc(tr_a, 1)

                    def silu_tile(ft):
                        act.wait_ge(part_mm, DPARTS.index(("u", ft)) + 1)
                        if ft >= 2:
                            act.wait_ge(af_ev, ft - 1)
                        f(sg[:, ft % 2, :], ps[ft % 2][:, 0:SEQ], ACT.Silu).then_inc(sg_ev, 1)

                    def a_hi(ft):
                        act.wait_ge(af_ev, ft + 1)
                        if ft >= 4:
                            act.wait_ge(part_mm, DPARTS.index(("w", ft - 4)) + 1)
                        f(dath[:, ft % 4, :], aT[:, ft % 4, :]).then_inc(dath_ev, 1)

                    for n, (w, ft) in enumerate(DPARTS):
                        if n < 2 * DENSE_SLOTS or ft % 4 == 0:
                            act.wait_ge(full[dense.slot[f"{w}{ft // 4}"]], dense.full[f"{w}{ft // 4}"])
                        if n >= HI_BUFS:
                            act.wait_ge(part_mm, n + 1 - HI_BUFS)
                        f(dense_hi(n, w), dense_part(slot, w, ft)).then_inc(part_hi, 1)
                        beside_dense(n, silu_tile, a_hi)
                    norm(1)
                with act.Else():
                    turned(tr_mm, tr_a, hT, 1)
                    act.wait_ge(rl_v, 13)
                    f(e12, dm12, ACT.Exp).then_inc(rl_a, 1)
                    act.wait_ge(ids_done, 1)

                    def xg_out(count):
                        act.wait_ge(xg_mm, count)
                        for b in range(2):
                            f(xgh[:, 4 * b:4 * b + 4, :], ps[2 + b][:, 0:4 * CAP].rearrange("p (j c) -> p j c", j=4)).then_inc(xgh_ev, 1)

                    def hi(n, p, turn):
                        name, s = PASS_ORDER[n // PARTS], n % PARTS
                        if s == 0:
                            loads = turn * (16 * PASS_ROUNDS) + moe.full[name]
                            act.wait_ge(full[moe.slot[name]], loads if p is None else p * (16 * PASS_ROUNDS) + loads)
                        uses = turn * SUBS + SUBS + n + 1 - HI_BUFS
                        act.wait_ge(part_mm, uses if p is None else p * SUBS + uses)
                        at_hi = (n % HI_BUFS) * SUB
                        f(w_hi[:, at_hi:at_hi + SUB], slot(moe.slot[name])[:, s * SUB:s * SUB + SUB]).then_inc(part_hi, 1)

                    xg_out(1)
                    for n in range(AHEAD):
                        hi(n, None, 0)
                    total = act.value_load(ids[0:1, MAXP:MAXP + 1], min_val=1, max_val=MAXP)
                    with act.Fori(0, MAXP) as p:
                        with act.If(p < total):
                            def silu(b):
                                act.wait_ge(part_mm, p * SUBS + (SUBS + last_part[f"u{b}"] + 1))
                                f(sge[0:CAP, b % 2, :], ps[2 * (b % 2)][0:CAP, :], ACT.Silu).then_inc(sg_ev, 1)

                            def a_out(b):
                                act.wait_ge(at_mm, p * NFB + (b + 1))
                                f(ath[:, b % 2, :, :], ps[6][:, 0:4 * CAP].rearrange("p (j c) -> p j c", j=4)).then_inc(ath_ev, 1)

                            def comb_out():
                                act.wait_ge(ct_mm, p + 1)
                                f(combT[0:CAP, :, :], ps[7][0:CAP, 0:NT * P].rearrange("p (t c) -> p t c", t=NT)).then_inc(ct_ev, 1)

                            for n in range(AHEAD, SUBS):
                                hi(n, p, 0)
                                after_part(n, silu, a_out, comb_out, lambda: xg_out(p + 2))
                        with act.If(p + 1 < total):
                            for n in range(AHEAD):
                                hi(n, p, 1)
                        with act.If(p < total):
                            act.wait_ge(part_mm, p * SUBS + 2 * SUBS)
                            f(y[0:CAP, 0:512], ps[4][0:CAP, :]).then_inc(ya_ev, 1)
                    norm(1)
                act.wait_ge(layer_done, 1)
                act.sem_inc(arrived, 1)
                act.wait_ge(next_layer, l + 1)

        @block.vector
        def _(dve):
            v = nc.vector

            def tt(o, a, b, op):
                return v.tensor_tensor(o, a, b, op)

            def stt(o, a, s, b, op0, op1):
                return v.scalar_tensor_tensor(out=o, in0=a, scalar=s, in1=b, op0=op0, op1=op1)

            def ts(o, a, s1, s2, op0, op1=None):
                return v.tensor_scalar(o, a, s1, s2, op0, op1) if op1 is not None else v.tensor_scalar(o, a, s1, None, op0)

            def over(x, *shape):
                return x.rearrange("p (h c) -> p h c", c=1).to_broadcast([P, x.shape[1], shape[0]])

            def again(x, k):
                return x.rearrange("p (a n) -> p a n", a=1).to_broadcast([P, k, x.shape[1]])

            dve.wait_ge(rel_in, 48)
            dve.wait_ge(rows_mm, 1)
            tt(M[0:QH, 1536:2048], ps[0][0:QH, :], M[0:QH, 1024:1536], ALU.add).then_inc(rows_ev, 1)
            with dve.Fori(0, DEPTH) as l:
                def turned(mm_sem, d_sem, dst, base):
                    for i in (1, 3):
                        T, kq = i // 2, i % 2
                        dve.wait_ge(mm_sem, 4 * base + i + 1)
                        v.tensor_copy(dst[:, 4 * kq:4 * kq + 4, T * P:T * P + P],
                                      ps[i][:, :].rearrange("p (j q) -> p j q", j=4)).then_inc(d_sem, 1)

                turned(tr_mm, tr_d, hT, 0)
                dve.wait_ge(params_in, l * (16 * N_PARAMS) + 16 * N_PARAMS)
                dve.wait_ge(pads, 2)
                for j in range(6):
                    dve.wait_ge(p1_ev, 2 * j + 2)
                    for tap in range(CONV):
                        for q in range(2):
                            t = 2 * j + q
                            o = (kT, qT, vT)[t // 4][:, t % 4, :]
                            w = convw[:, CONV * t + tap:CONV * t + tap + 1]
                            src = convin[:, t, tap:tap + SEQ]
                            if tap == 0:
                                ts(o, src, w, None, ALU.mult).then_inc(conv_st, 1)
                            else:
                                dve.wait_ge(conv_st, 10 * j + 2 * tap + q - 1)
                                stt(o, src, w, o, ALU.mult, ALU.add).then_inc(conv_st, 1)
                dve.wait_ge(p1_ev, 17)
                tt(ax, ab[:, :, 0:16], again(dnrow[:, 0:16], NT), ALU.add).then_inc(dg_v, 1)
                dve.wait_ge(dg_v, 1)
                stt(nab, ax, -1.0, ax, ALU.mult, ALU.max).then_inc(dg_v, 1)
                dve.wait_ge(dg_a, 3)
                stt(lnp, ax, 0.0, lnp, ALU.max, ALU.add).then_inc(dg_v, 1)
                dve.wait_ge(dg_v, 3)
                stt(gg, lnp, -1.0, again(ea, NT), ALU.mult, ALU.mult).then_inc(dg_v, 1)
                dve.wait_ge(dg_a, 4)
                ts(eb, eb, 1.0, None, ALU.add).then_inc(dg_v, 1)
                dve.wait_ge(dg_v, 5)
                v.reciprocal(beta, eb).then_inc(dg_v, 1)
                for c in range(4):
                    x = (kT if c < 2 else qT)[:, 2 * (c % 2):2 * (c % 2) + 2, :].rearrange("p a b -> p (a b)")
                    dve.wait_ge(rs_done, 2 * c + 2)
                    tt(x, x, rs[:, c, :], ALU.mult).then_inc(nrm_done, 1)
                dve.wait_ge(strip_in, 16)
                mx3 = mx.rearrange("p (i e) -> p i e", e=2)
                for n in range(9):
                    if n < 8:
                        e, i = n % 2, n - n % 2
                        off = P * (1 - i // 4)
                        dve.wait_ge(sc_mm, n + 1)
                        stt(Sall[:, i:i + 2, e, :], ps[n % 4][:, :].rearrange("p (i j) -> p i j", i=2), HD ** -0.5,
                            strip[:, 4 * e + i % 4:4 * e + i % 4 + 2, off:off + SEQ], ALU.mult, ALU.add).then_inc(sc_ev, 1)
                    if n:
                        e, i = (n - 1) % 2, (n - 1) - (n - 1) % 2
                        dve.wait_ge(sc_ev, n)
                        v.tensor_reduce(mx3[:, i:i + 2, e], Sall[:, i:i + 2, e, :], AX.X, ALU.max).then_inc(sm_v, 1)
                dve.wait_ge(sm_v, 8)
                tt(mx, mx, sinkr[:, :], ALU.max).then_inc(sm_v, 1)
                dve.wait_ge(sm_v, 9)
                ts(mneg, mx, -1.0, None, ALU.mult).then_inc(sm_v, 1)
                tt(esink, sinkr[:, :], mx, ALU.subtract).then_inc(sm_v, 1)
                dve.wait_ge(sm_a, 17)
                tt(rden, psum16, esink, ALU.add).then_inc(sm_v, 1)
                dve.wait_ge(sm_v, 12)
                v.reciprocal(rden, rden).then_inc(sm_v, 1)
                dve.wait_ge(sm_v, 13)
                for i in range(8):
                    tt(Sall[:, i], Sall[:, i], over(rden[:, 2 * i:2 * i + 2], SEQ), ALU.mult).then_inc(pn_done, 1)
                dve.wait_ge(gc_mm, 1)
                v.tensor_copy(Gc, ps[4][:, 0:64].rearrange("p (i c) -> p i c", i=4)).then_inc(gc_v, 1)
                dve.wait_ge(gc_v, 1)
                tt(dl, Gc[:, :, 8:16], Gc[:, :, 0:8], ALU.subtract).then_inc(gc_v, 1)
                dve.wait_ge(gc_a, 1)
                for i, (d, T) in enumerate(SETS):
                    tt(bG[:, i, :], eG[:, i, :], beta[:, T, 8 * d:8 * d + 8], ALU.mult).then_inc(gc_v, 1)

                def set_tiles(i):
                    d, T = SETS[i]
                    kp = i % 2
                    if i == 0:
                        dve.wait_ge(pv_ev, 2)
                    dve.wait_ge(grow_mm, i + 1)
                    for w, hh in enumerate(HEAD_AT):
                        last = stt(Dm[:, w, :], ps[w // 4][:, (w % 4) * P:(w % 4) * P + P], Gc[:, i, hh:hh + 1],
                                   C(f"neg{d}"), ALU.subtract, ALU.add)
                    last.then_inc(dm_done, 1)

                    def quad(x, b):
                        return x[:, 4 * b:4 * b + 4, :].rearrange("p h c -> p (h c)")

                    dve.wait_ge(dexp_done, i + 1)
                    dve.wait_ge(kk_mm, i + 1)
                    for b in range(2):
                        tt(quad(AT, b), ps[4 + b][:, :], quad(Dm, b), ALU.mult).then_inc(kkd_done, 1)
                    dve.wait_ge(beta_mm, i + 1)
                    for b in range(2):
                        dve.wait_ge(kkd_done, 2 * i + b + 1)
                        last = tt(quad(AT, b), quad(AT, b), ps[2 + b][:, :], ALU.mult)
                    last.then_inc(at_done, 1)
                    dve.wait_ge(qk_mm, i + 1)
                    for b in range(2):
                        last = tt(quad(qkd[kp], b), ps[6 + b][:, :], quad(Dm, b), ALU.mult)
                    last.then_inc(qkd_done, 1)
                    for lev in range(1, LEVELS):
                        for q in range(2):
                            n = (i * 5 + lev - 1) * 2 + q
                            dve.wait_ge(xy_mm, n + 1)
                            tt(quad(XT, q), quad(XT, q), ps[4 + q][:, :], ALU.subtract).then_inc(xt_done, 1)
                    dve.wait_ge(uw_mm, i + 1)
                    v.tensor_copy(wT[kp].rearrange("p k c -> p (k c)"), ps[7][:, :]).then_inc(w_ev, 1)

                def scan_step(n):
                    for d in range(2):
                        i, c, k = 2 * (n // 2) + d, (n if d == 0 else 3 - n), 2 * n + d
                        kp, r = i % 2, CHUNK * (c % 2)
                        dve.wait_ge(ws_mm, k + 1)
                        tt(vnew[r:r + CHUNK, n % 2, :], u_s[kp][r:r + CHUNK, :], ps[3 * d][r:r + CHUNK, :],
                           ALU.subtract).then_inc(vn_done, 1)
                    for d in range(2):
                        c, k = (n if d == 0 else 3 - n), 2 * n + d
                        r = CHUNK * (c % 2)
                        dve.wait_ge(st_mm, k + 1)
                        dve.wait_ge(sc_done, k + 1)
                        for e in range(2):
                            a = HD * e
                            tt(S[a:a + HD, d, :, a:a + HD], Sc[a:a + HD, d, :, a:a + HD],
                               ps[3 * d + 2][a:a + HD, :].rearrange("p (k n) -> p k n", k=4)[:, :, a:a + HD],
                               ALU.add).then_inc(s_done, 1)
                        if n >= 2:
                            dve.wait_ge(o_ev, 4)
                            tt(osum[r:r + CHUNK, c // 2, :], osum[r:r + CHUNK, c // 2, :], ps[3 * d + 1][r:r + CHUNK, :],
                               ALU.add).then_inc(o_ev, 1)

                set_tiles(0)
                set_tiles(1)
                scan_step(0)
                scan_step(1)
                set_tiles(2)
                set_tiles(3)
                scan_step(2)
                scan_step(3)
                dve.wait_ge(osq_done, 2)
                v.tensor_reduce(osr, M[:, 17408:18432].rearrange("p (h d) -> p h d", d=HD), AX.X, ALU.add).then_inc(or_v, 1)
                dve.wait_ge(or_a, 2)
                o16 = M[:, 3072:4096].rearrange("p (h d) -> p h d", d=HD)
                tt(o16, o16, over(osr, HD), ALU.mult).then_inc(or_v, 1)
                dve.wait_ge(or_v, 2)
                dve.wait_ge(zn_done, 2)
                tt(M[:, 3072:4096], M[:, 3072:4096], M[:, 2048:3072], ALU.mult).then_inc(od_done, 1)
                for k in range(12):
                    j = k % 4
                    T, hf = j % 2, j // 2
                    dve.wait_ge(up_mm, k + 1)
                    dve.wait_ge(gate_ev, k // 4 + 1)
                    if k >= 6:
                        dve.wait_ge(mrg, k - 5)
                    o = merged[:, T, hf * 512:hf * 512 + 512] if k < 4 else gtmp[:, k % 2, :]
                    tt(o, ps[4 + j][:, :], gate_at(k), ALU.mult).then_inc(up_ev, 1)
                turned(mt_mm, mt_d, mT, 0)
                for i in range(4):
                    hf, T = i // 2, i % 2
                    hv = h[:, T, hf * 512:hf * 512 + 512]
                    dve.wait_ge(out_mm, i + 1)
                    stt(hv, hv, ALPHA, ps[4 + i][:, :], ALU.mult, ALU.add).then_inc(res1, 1)

                def norm(which, rows_in, done_half, done):
                    b0 = 10 * which
                    for T in range(NT):
                        for hf in range(2):
                            v.bn_stats(bst[:, T, 6 * hf:6 * hf + 6], h[:, T, hf * 512:hf * 512 + 512]).then_inc(lnv, 1)
                        dve.wait_ge(lnv, b0 + 3 * T + 2)
                        v.bn_aggr(bag[:, T, :], bst[:, T, :]).then_inc(lnv, 1)
                    dve.wait_ge(rows_in, l * 32 + 32)
                    for T in range(NT):
                        dve.wait_ge(lna, 4 * which + 2 * T + 2)
                        ts(h[:, T, :], h[:, T, :], bag[:, T, 0:1], rstd[:, T:T + 1], ALU.subtract, ALU.mult).then_inc(lnv, 1)
                        dve.wait_ge(lnv, b0 + 6 + 2 * T + 1)
                        tt(h[:, T, :], h[:, T, :], lng, ALU.mult).then_inc(lnv, 1)
                        dve.wait_ge(lnv, b0 + 6 + 2 * T + 2)
                        if T == 1 and which:
                            dve.wait_ge(done_half, 1)
                        tt(h[:, T, :], h[:, T, :], lnb, ALU.add).then_inc(done_half if T == 0 else done, 1)

                dve.wait_ge(res1, 4)
                norm(0, ln1_in, ln1_done, ln1_done)
                with dve.If(l < 1):
                    for i in range(4):
                        c = (slice(4 * (i % 2), 4 * (i % 2) + 4), slice((i // 2) * P, (i // 2) * P + P))
                        dve.wait_ge(tr_a, 2 + i + 1)
                        tt(hTl[:, c[0], c[1]], ps[i][:, :].rearrange("p (j q) -> p j q", j=4), hTh[:, c[0], c[1]].bitcast(F32),
                           ALU.subtract).then_inc(tr_d, 1)

                    def product(ft):
                        dve.wait_ge(sg_ev, ft + 1)
                        if ft >= 4:
                            dve.wait_ge(datl_ev, ft - 3)
                        tt(aT[:, ft % 4, :], sg[:, ft % 2, :], ps[ft % 2][:, SEQ:2 * SEQ], ALU.mult).then_inc(af_ev, 1)

                    def a_lo(ft):
                        dve.wait_ge(dath_ev, ft + 1)
                        tt(datl[:, ft % 4, :], aT[:, ft % 4, :], dath[:, ft % 4, :].bitcast(F32), ALU.subtract).then_inc(datl_ev, 1)

                    for n, (w, ft) in enumerate(DPARTS):
                        dve.wait_ge(part_hi, n + 1)
                        tt(dense_part(w_lo, w, ft), dense_part(slot, w, ft), dense_hi(n, w).bitcast(F32), ALU.subtract).then_inc(part_lo, 1)
                        beside_dense(n, product, a_lo)
                    dve.wait_ge(part_mm, len(DPARTS))
                    for i in range(4):
                        T, dh = i // 2, i % 2
                        hv = h[:, T, dh * 512:dh * 512 + 512]
                        stt(hv, hv, ALPHA, ps[4 + i][:, :], ALU.mult, ALU.add).then_inc(res2, 1)
                    dve.wait_ge(res2, 4)
                    norm(1, ln2_in, ln2_half, layer_done)
                with dve.Else():
                    turned(tr_mm, tr_d, hT, 1)
                    for T in range(NT):
                        dve.wait_ge(rl_mm, T + 1)
                        v.tensor_copy(lg[:, T, :], ps[T][:, 0:NE]).then_inc(rl_v, 1)
                    for T in range(NT):
                        dve.wait_ge(rl_v, T + 1)
                        v.max(m8[:, T, :], lg[:, T, :]).then_inc(rl_v, 1)
                    for T in range(NT):
                        dve.wait_ge(rl_v, T + 3)
                        v.max_index(idx8v[:, T, :], m8[:, T, :], lg[:, T, :]).then_inc(rl_v, 1)
                    dve.wait_ge(rl_v, 6)
                    v.tensor_copy(idxf, idx8v[:, :, 0:TOP_K]).then_inc(rl_v, 1)
                    dve.wait_ge(rl_v, 7)
                    for k in range(TOP_K):
                        for T in range(NT):
                            ts(oh[:, k, T, :], C("iota")[:, 0:NE], idxf[:, T, k:k + 1], None, ALU.is_equal).then_inc(rl_v, 1)
                    dve.wait_ge(rl_v, 11)
                    tt(sel, oh[:, 0], oh[:, 1], ALU.add).then_inc(rl_v, 1)
                    tt(dm12, m8[:, :, 1], m8[:, :, 0], ALU.subtract).then_inc(rl_v, 1)
                    dve.wait_ge(rl_a, 1)
                    ts(e12p, e12, 1.0, None, ALU.add).then_inc(rl_v, 1)
                    dve.wait_ge(rl_v, 14)
                    v.reciprocal(rw[:, :, 0], e12p).then_inc(rl_v, 1)
                    dve.wait_ge(rl_v, 15)
                    tt(rw[:, :, 1], e12, rw[:, :, 0], ALU.mult).then_inc(rl_v, 1)
                    dve.wait_ge(rc_mm, 1)
                    v.tensor_copy(cnt, ps[2][:, 16:24]).then_inc(rl_v, 1)
                    v.tensor_copy(pos, ps[2][:, 0:16].rearrange("p (t e) -> p t e", t=NT)).then_inc(rl_v, 1)
                    dve.wait_ge(rl_v, 18)
                    ts(nch, cnt, 0.0, None, ALU.is_gt).then_inc(rl_v, 1)
                    step = 19
                    for k in range(CAP, SEQ, CAP):
                        dve.wait_ge(rl_v, step)
                        stt(nch, cnt, float(k), nch, ALU.is_gt, ALU.add).then_inc(rl_v, 1)
                        step += 1
                    dve.wait_ge(rl_v, step)
                    v.tensor_tensor_scan(end, scal[:, 3:4].to_broadcast([P, NE]), nch, 0.0, ALU.mult, ALU.add).then_inc(rl_v, 1)
                    dve.wait_ge(rl_v, step + 1)
                    tt(sbase, end, nch, ALU.subtract).then_inc(rl_v, 1)
                    dve.wait_ge(rl_v, step + 2)
                    stt(slot_e, again(sbase, NT), float(CAP), pos, ALU.mult, ALU.add).then_inc(rl_v, 1)
                    dve.wait_ge(rl_v, step + 3)
                    for k in range(TOP_K):
                        tt(pick[:, k], oh[:, k], slot_e, ALU.mult).then_inc(rl_v, 1)
                    dve.wait_ge(rl_v, step + 5)
                    for k in range(TOP_K):
                        v.tensor_reduce(rslot[:, :, k], pick[:, k], AX.X, ALU.add).then_inc(rl_v, 1)
                    tt(cmp_p, C("pass_no").rearrange("p (n e) -> p n e", e=NE), again(end, MAXP), ALU.is_ge).then_inc(rl_v, 1)
                    dve.wait_ge(rl_v, step + 8)
                    v.tensor_reduce(idf, cmp_p, AX.X, ALU.add).then_inc(rl_v, 1)
                    dve.wait_ge(rl_v, step + 9)
                    ts(ids[:, 0:MAXP], idf, float(NE - 1), None, ALU.min).then_inc(rl_v, 1)
                    v.tensor_copy(ids[:, MAXP:MAXP + 1], end[:, NE - 1:NE]).then_inc(rl_v, 1)
                    ts(acc, h, ALPHA, None, ALU.mult).then_inc(rl_v, 1)
                    dve.wait_ge(rl_v, step + 12)
                    dve.sem_inc(acc_add, 4)
                    dve.sem_inc(ids_done, 1)

                    def dispatch(turn):
                        for T in range(NT):
                            b = 6 * T
                            s1, s2 = rslot[:, T, 0:1], rslot[:, T, 1:2]
                            if turn is not None or T:
                                dve.wait_ge(dispv, b if turn is None else turn * 12 + (12 + b))
                            ts(hot1, C("iota"), s1, None, ALU.is_equal).then_inc(dispv, 1)
                            ts(hot2, C("iota"), s1, rw[:, T, 0:1], ALU.is_equal, ALU.mult).then_inc(dispv, 1)
                            ts(hot3, C("iota"), s2, rw[:, T, 1:2], ALU.is_equal, ALU.mult).then_inc(dispv, 1)
                            dve.wait_ge(dispv, b + 1 if turn is None else turn * 12 + (12 + b + 1))
                            stt(disp[:, T, :], C("iota"), s2, hot1, ALU.is_equal, ALU.add).then_inc(dispv, 1)
                            dve.wait_ge(dispv, b + 4 if turn is None else turn * 12 + (12 + b + 4))
                            tt(comb[:, T, :], hot2, hot3, ALU.add).then_inc(dispv, 1)
                            ts(rslot[:, T, :], rslot[:, T, :], float(-CAP), None, ALU.add).then_inc(dispv, 1)

                    def xg_low(count, first):
                        for b in range(2):
                            dve.wait_ge(xgh_ev, count + (first + b))
                            tt(xgl[:, 4 * b:4 * b + 4, :], ps[2 + b][:, 0:4 * CAP].rearrange("p (j c) -> p j c", j=4),
                               xgh[:, 4 * b:4 * b + 4, :].bitcast(F32), ALU.subtract).then_inc(xgl_ev, 1)

                    def lo(n, p, turn):
                        name, s = PASS_ORDER[n // PARTS], n % PARTS
                        done = turn * SUBS + n + 1
                        dve.wait_ge(part_hi, done if p is None else p * SUBS + done)
                        at_hi = (n % HI_BUFS) * SUB
                        tt(w_lo(moe.slot[name])[:, s * SUB:s * SUB + SUB], slot(moe.slot[name])[:, s * SUB:s * SUB + SUB],
                           w_hi[:, at_hi:at_hi + SUB].bitcast(F32), ALU.subtract).then_inc(part_lo, 1)

                    dispatch(None)
                    xg_low(0, 1)
                    for n in range(AHEAD):
                        lo(n, None, 0)
                    total = dve.value_load(ids[0:1, MAXP:MAXP + 1], min_val=1, max_val=MAXP)
                    with dve.Fori(0, MAXP) as p:
                        with dve.If(p < total):
                            def mult(b):
                                dve.wait_ge(sg_ev, p * NFB + (b + 1))
                                tt(ae[0:CAP, b % 2, :], sge[0:CAP, b % 2, :], ps[2 * (b % 2) + 1][0:CAP, :], ALU.mult).then_inc(af_ev, 1)

                            def a_low(b):
                                dve.wait_ge(ath_ev, p * NFB + (b + 1))
                                tt(atl[:, b % 2, :, :], ps[6][:, 0:4 * CAP].rearrange("p (j c) -> p j c", j=4),
                                   ath[:, b % 2, :, :].bitcast(F32), ALU.subtract).then_inc(atl_ev, 1)

                            def next_dispatch():
                                dve.wait_ge(ct_mm, p + 1)
                                dispatch(p)

                            for n in range(AHEAD, SUBS):
                                lo(n, p, 0)
                                after_part(n, mult, a_low, next_dispatch, lambda: xg_low(p * 2, 3))
                        with dve.If(p + 1 < total):
                            for n in range(AHEAD):
                                lo(n, p, 1)
                        with dve.If(p < total):
                            dve.wait_ge(part_mm, p * SUBS + 2 * SUBS)
                            v.tensor_copy(y[0:CAP, 512:1024], ps[5][0:CAP, :]).then_inc(yd_ev, 1)
                            for q in range(4):
                                T, dh = q // 2, q % 2
                                av = acc[:, T, dh * 512:dh * 512 + 512]
                                dve.wait_ge(cb_mm, p * 4 + (q + 1))
                                if q == 0:
                                    dve.wait_ge(acc_add, p * 4 + 4)
                                tt(av, av, ps[7 - dh][:, :], ALU.add).then_inc(acc_add, 1)
                    dve.wait_ge(acc_add, total * 4 + 4)
                    v.tensor_copy(h, acc).then_inc(res2, 1)
                    dve.wait_ge(res2, 1)
                    norm(1, ln2_in, ln2_half, layer_done)
                dve.wait_ge(layer_done, 1)
                dve.sem_inc(arrived, 1)
                dve.wait_ge(next_layer, l + 1)


_INS = ["x", "w_in", "w_branch", "w_out", "pool_w", "rel_bias", "dn_norm_w", "ln1_g", "ln1_b", "ln2_g", "ln2_b",
        "ffn_w1", "ffn_w3", "ffn_w2", "router_w", "moe_wg", "moe_wu", "moe_wd"]


def kernel(**inputs):
    from concourse import bacc
    from concourse.bass_utils import run_bass_kernel_spmd

    a = {n: np.ascontiguousarray(inputs[n]) for n in _INS}
    cw = np.asarray(inputs["conv_w"]).reshape(DEPTH, CONV, 3, 4, P)
    cw = np.concatenate([cw[:, :, 1:2], cw[:, :, 0:1], cw[:, :, 2:3]], axis=2)
    w_in = a["w_in"].copy()
    w_in[:, :, C_Q:C_K] = w_in[:, :, C_Q:C_K].reshape(DEPTH, D, 2, 4, HD).transpose(0, 1, 3, 2, 4).reshape(DEPTH, D, 512)
    a["w_in"] = w_in
    a["conv_w"] = np.ascontiguousarray(cw.transpose(0, 4, 2, 3, 1).reshape(DEPTH, P, 12 * CONV))
    a["dn_rows"] = np.ascontiguousarray(np.concatenate(
        [np.asarray(inputs["dt_bias"]).reshape(DEPTH, 16), np.asarray(inputs["a_log"]).reshape(DEPTH, 16)], axis=1))
    sinks = np.asarray(inputs["attn_sink"]).reshape(DEPTH, 2, 4).transpose(0, 2, 1).reshape(DEPTH, 8)
    a["sinks"] = np.ascontiguousarray(np.concatenate([sinks, sinks], axis=1))
    a["pool_scale"] = np.ascontiguousarray(np.asarray(inputs["pool_scale"]).reshape(DEPTH, BT, P).transpose(0, 2, 1))
    a["consts"] = const_table()
    a["pool_c"] = pool_table()
    a["hot"], a["band"] = bucket_table()

    nc = bacc.Bacc("TRN2", target_bir_lowering=False, num_devices=1)
    A = {n: nc.dram_tensor(f"in_{n}", x.shape, F32, kind="ExternalInput").ap() for n, x in a.items()}
    A["rows"] = nc.dram_tensor("rows", (QH, P, 512), F32, kind="Internal").ap()
    out = nc.dram_tensor("out", (1, SEQ, D), F32, kind="ExternalOutput").ap()
    build(nc, A, out)
    r = run_bass_kernel_spmd(nc, [{f"in_{n}": x for n, x in a.items()}], core_ids=[0])
    return r.results[0]["out"]
```

```python
import math
from contextlib import ExitStack

import numpy as np

import concourse.bass as bass
from concourse import mybir

F32 = mybir.dt.float32
F32R = mybir.dt.float32r
I32 = mybir.dt.int32
U32 = mybir.dt.uint32
ALU = mybir.AluOpType
ACT = mybir.ActivationFunctionType
AX = mybir.AxisListType

P = 128
DEPTH = 2
SEQ = 256
NT = SEQ // P
D = 1024
KT = D // P
HD = 64
QH = 8
DNH = 8
CONV = 5
CHUNK = 64
BR = 512
BT = BR // P
N_BUCKETS = 32
MAX_DISTANCE = 128
WINDOW = 128
STRIP = 3 * P
POOL_WINDOWS = (2, 4, 8, 16)
DFF = 2816
DFFE = 3584
NE = 8
ALPHA = (2.0 * DEPTH) ** 0.25
LN_EPS = 1e-5
NEG = -1e30
LEVELS = 6

C_Q, C_K, C_DQ, C_DK, C_DV, C_Z, C_AB, C_PU, C_G = 0, 512, 768, 1280, 1792, 2304, 2816, 2848, 3360

CAP = 96
TOP_K = 2
MAXP = (SEQ * TOP_K + NE * (CAP - 1)) // CAP

SLOT = 4096
SUB = 1024
HI_BUFS = 4
MIX_SLOTS, DENSE_SLOTS, MOE_SLOTS = 4, 6, 7

SETS = [(0, 0), (1, 1), (0, 1), (1, 0)]

HEAD_AT = [2 * (w % 4) + w // 4 for w in range(DNH)]

CONST = {}


def const_table():
    j, i = np.meshgrid(np.arange(P), np.arange(P), indexing="ij")
    same = (j // CHUNK) == (i // CHUNK)
    parts = [("ident", np.eye(P)), ("cum0", same & (j <= i)), ("cum1", same & (j >= i)), ("blk", same),
             ("before", j < i), ("neg0", np.where(same & (j <= i), 0.0, NEG)),
             ("neg1", np.where(same & (j >= i), 0.0, NEG))]
    for d in range(2):
        for l in range(LEVELS):
            s = 1 << l
            pair = (j // (2 * s)) == (i // (2 * s))
            lo_j, lo_i = (j % (2 * s)) < s, (i % (2 * s)) < s
            parts.append((f"lvl{d}{l}", pair & (lo_j & ~lo_i if d == 0 else ~lo_j & lo_i)))
    parts.append(("iota", np.broadcast_to(np.arange(CAP), (P, CAP))))
    parts.append(("pass_no", np.broadcast_to(np.repeat(np.arange(MAXP), NE), (P, MAXP * NE))))
    parts.append(("scal", np.broadcast_to(np.array([1e-6, LN_EPS, math.log(HD ** -0.5), 1.0, -0.5]), (P, 5))))
    at = 0
    for name, a in parts:
        CONST[name] = (at, at + a.shape[1])
        at += a.shape[1]
    return np.ascontiguousarray(np.concatenate([np.asarray(a, np.float32) for _, a in parts], axis=1))


def pool_table():
    t = np.arange(SEQ)
    out = np.zeros((SEQ, len(POOL_WINDOWS), SEQ), np.float32)
    for g, w in enumerate(POOL_WINDOWS):
        r = w // 2
        count = (np.minimum(t + r, SEQ - 1) - np.maximum(t - r, 0) + 1).astype(np.float32)
        out[:, g, :] = (np.abs(t[:, None] - t[None, :]) <= r) / count[None, :] - np.eye(SEQ)
    return np.ascontiguousarray(out.reshape(NT, P, len(POOL_WINDOWS), SEQ).transpose(1, 0, 2, 3))


def bucket_table():
    rel = np.arange(-255, 257)
    nb = N_BUCKETS // 2
    max_exact = nb // 2
    n = np.abs(rel)
    large = max_exact + (np.log(np.maximum(n, 1) / max_exact) / np.log(MAX_DISTANCE / max_exact)
                         * (nb - max_exact)).astype(np.int32)
    large = np.minimum(large, nb - 1)
    bucket = np.where(rel > 0, nb, 0) + np.where(n < max_exact, n, large)
    hot = (np.arange(N_BUCKETS)[:, None] == bucket[None, :]).astype(np.float32)
    mask = np.where(n <= WINDOW, 0.0, NEG).astype(np.float32)
    return hot, np.ascontiguousarray(np.broadcast_to(mask, (QH, 512)))


class Ring:

    def __init__(self):
        self.slot, self.full, self.before, self.last = {}, {}, {}, {}
        self.count = [0] * MOE_SLOTS

    def add(self, name, slot, loads=1):
        self.slot[name] = slot
        self.count[slot] += 16 * loads
        self.full[name] = self.count[slot]
        self.before[name] = self.last.get(slot)
        self.last[slot] = name


GATE_ORDER = (2, 0, 1)
GATES = [f"gate{n}{hf}" for n in GATE_ORDER for hf in range(2)]


def mixer_ring():
    r = Ring()
    for k, name in enumerate(["dk", "dq", "dv", "kvab", "q", "z", "pu", "pool"]):
        r.add(name, k % MIX_SLOTS, 0 if k < MIX_SLOTS else 1)
    for k, name in enumerate(GATES):
        r.add(name, k % 3)
    for name, slot in (("branch2", 1), ("branch0", 2), ("branch1", 4), ("out0", 1), ("out1", 2)):
        r.add(name, slot, 2 if name == "branch0" else 1)
    return r


def build(nc, A, out):
    es = ExitStack()
    with es:
        def sb(name, n, dt=F32, p=P):
            return es.enter_context(nc.sbuf_tensor(name, [p, n], dt))

        def sem(name):
            return es.enter_context(nc.semaphore(name))

        at = {}

        def sb_at(name, n):
            t = sb(name, n)
            at[name] = nc.sbuf_base - 4 * n
            return t

        ring_mem = sb_at("ring", MIX_SLOTS * SLOT)
        h_mem = sb("h", NT * D)
        hT_mem = sb_at("hT", KT * SEQ)
        strip_mem = sb_at("strip", QH * STRIP)
        M = sb_at("M", 24064)
        cst = sb("cst", A["consts"].shape[1])
        convw = sb("convw", 12 * CONV)
        dnrow = sb("dnrow", 32)
        normw = sb("normw", HD)
        poolsc = sb("poolsc", BT)
        sinkr = sb("sinkr", 16)
        ab_mem = sb("ab", 64)
        gsm = sb("gsm", 480)
        att_s = sb("att_s", 8 * 16)
        lnst = sb("lnst", 64)
        ids = sb("ids", 16, I32)
        idx8v = sb("idx8", 16, U32)[:, :].rearrange("p (t e) -> p t e", t=NT)
        ps = [es.enter_context(nc.psum_tensor(f"ps{i}", [P, 512], F32)) for i in range(8)]

        def C(name):
            a, b = CONST[name]
            return cst[:, a:b]

        ident = C("ident")
        scal = C("scal")
        h = h_mem[:, :].rearrange("p (t d) -> p t d", t=NT)
        hT = hT_mem[:, :].rearrange("p (k s) -> p k s", k=KT)
        strip = strip_mem[:, :].rearrange("p (h c) -> p h c", h=QH)
        ab = ab_mem[:, :].rearrange("p (t c) -> p t c", t=NT)

        def m(at, n, k=None):
            v = M[:, at:at + n]
            return v if k is None else v.rearrange("p (k n) -> p k n", k=k)

        def r_view(name, under, start, n):
            return nc.alloc_sbuf_tensor_at(name, [P, n], F32R, offset=at[under] + 4 * start)

        oAT = m(0, 1024, BT)
        oPT = m(1024, 1024, BT)
        zs = m(2048, 1024, NT)
        osum = m(3072, 1024, NT)
        qT = m(4096, 1024, BT)
        kT = m(5120, 1024, BT)
        ktok = m(6144, 1024, NT)
        vtok = m(7168, 1024, NT)
        S = m(8192, 1024).rearrange("p (d k n) -> p d k n", d=2, k=4)
        Sc = m(9216, 1024).rearrange("p (d k n) -> p d k n", d=2, k=4)
        vnew = m(10240, 1024, 2)
        mixT = m(8192, 1024, BT)
        kept = [11264 + 3072 * s for s in range(2)]
        qkd = [m(a, 1024, DNH) for a in kept]
        u_s = [m(a + 1024, 512) for a in kept]
        wT = [m(a + 1536, 512, 4) for a in kept]
        qdec = [m(a + 2048, 512, 4) for a in kept]
        kdec = [m(a + 2560, 512) for a in kept]
        W0 = 17408
        Dm = m(W0, 1024, DNH)
        AT = m(W0 + 1024, 1024, DNH)
        XT = m(W0 + 2048, 1024, DNH)
        X = m(W0 + 3072, 1024, DNH)
        AL = m(W0 + 4096, 1024, DNH)
        Rv = m(W0 + 5120, 512)
        Rw = m(W0 + 5632, 512)
        eGp = m(W0 + 6144, 512, 4)
        poolw = m(9216, 512, BT)
        convin = m(11264, 12 * 260, 12)
        Sall = m(11264, 4096).rearrange("p (m e j) -> p m e j", m=8, e=2)
        qA = m(15360, 1024, 4)
        kA = m(16384, 256)
        vA = m(16640, 256, NT)
        pu = m(16896, 1024, NT)
        vT = m(17920, 1024, BT)
        PT = m(18944, 1024, 2)
        sq = m(19968, 2048, 4)
        rs = m(22016, 2048, 4)
        oDT = m(4096, 1024, BT)
        merged = m(6144, 2048, NT)
        gates1 = m(19968, 1024)
        gtmp = m(10240, 1024, 2)
        mT = m(0, 2048, KT)
        lng = m(2048, 1024)
        lnb = m(3072, 1024)
        sg = m(4096, 512, 2)
        aT = m(4608, 1024, 4)
        hTh = r_view("hTh", "hT", 0, KT * SEQ)[:, :].rearrange("p (k s) -> p k s", k=KT)
        hTl = r_view("hTl", "M", 0, KT * SEQ)[:, :].rearrange("p (k s) -> p k s", k=KT)
        dath = r_view("dath", "M", 5632, 1024)[:, :].rearrange("p (b s) -> p b s", b=4)
        datl = r_view("datl", "M", 6656, 1024)[:, :].rearrange("p (b s) -> p b s", b=4)
        dw_hi = r_view("dw_hi", "M", 7680, HI_BUFS * SUB)
        acc = m(4096, 2048, NT)
        disp = m(6144, 192, NT)
        comb = m(6336, 192, NT)
        combT = m(6528, 256, NT)
        y = m(6784, 1024)
        sge = m(7808, 1024, 2)
        ae = m(8832, 1024, 2)
        hot1 = m(9920, 96)
        hot2 = m(10016, 96)
        hot3 = m(10700, 96)
        xgh = r_view("xgh", "M", 0, KT * CAP)[:, :].rearrange("p (k c) -> p k c", k=KT)
        xgl = r_view("xgl", "M", KT * CAP, KT * CAP)[:, :].rearrange("p (k c) -> p k c", k=KT)
        w_hi = r_view("w_hi", "hT", 0, HI_BUFS * SUB)
        lo_ring = r_view("lo_ring", "ring", 0, MIX_SLOTS * SLOT)
        lo_extra = r_view("lo_extra", "M", 11776, (MOE_SLOTS - MIX_SLOTS) * SLOT)
        ath = r_view("ath", "strip", HI_BUFS * SUB - KT * SEQ, 8 * CAP)[:, :].rearrange("p (b j c) -> p b j c", b=2, j=4)
        atl = r_view("atl", "M", 10800, 8 * CAP)[:, :].rearrange("p (b j c) -> p b j c", b=2, j=4)
        assert at["strip"] == at["hT"] + 4 * KT * SEQ
        router = m(10600, KT * NE, KT)

        xTh = r_view("xTh", "M", 0, KT * SEQ)[:, :].rearrange("p (k s) -> p k s", k=KT)
        xTl = r_view("xTl", "M", 6144, KT * SEQ)[:, :].rearrange("p (k s) -> p k s", k=KT)
        p1_bufs = [r_view(f"p1_hi{i}", "M", a, SUB) for i, a in enumerate((3072, 8192, 10240, 18944))]

        def carve(mem, at=0):
            at = [at]

            def take(n, k=None):
                v = mem[:, at[0]:at[0] + n]
                at[0] += n
                return v if k is None else v.rearrange("p (k n) -> p k n", k=k)
            return take

        take = carve(gsm)
        ax, nab, lnp, gg = take(32, NT), take(32, NT), take(32, NT), take(32, NT)
        eb, beta = take(32, NT), take(32, NT)
        Gc = take(64, 4)
        dl, eG, kds, bG = take(32, 4), take(32, 4), take(32, 4), take(32, 4)
        cd = take(32).rearrange("p (i k c) -> p i k c", i=4, k=4)
        ea = take(16)
        osr = take(16)
        take = carve(att_s)
        mx, mneg, esink, psum16, rden = take(16), take(16), take(16), take(16), take(16)
        take = carve(lnst)
        bst, bag, rstd = take(24, NT), take(4, NT), take(2)
        take = carve(M, 10112)
        lg, m8, idxf, sel = take(16, NT), take(16, NT), take(4, NT), take(16, NT)
        oh = take(32).rearrange("p (k t e) -> p k t e", k=TOP_K, t=NT)
        dm12, e12, e12p = take(2), take(2), take(2)
        rw = take(4, NT)
        cnt, nch, end, sbase = take(8), take(8), take(8), take(8)
        pos, slot_e = take(16, NT), take(16, NT)
        pick = take(32).rearrange("p (k t e) -> p k t e", k=TOP_K, t=NT)
        rslot = take(4, NT)
        cmp_p = take(MAXP * NE, MAXP)
        idf = take(MAXP)

        def slot(s):
            return ring_mem[:, s * SLOT:(s + 1) * SLOT] if s < MIX_SLOTS else m(11776 + (s - MIX_SLOTS) * SLOT, SLOT)

        P1_PARTS = [(w, j) for w in ("dk", "dq", "dv") for j in range(4)] + [("kvab", 0)]
        P1_PARTS += [(w, j) for w in ("q", "z", "pu") for j in range(4)]

        def p1_part(mem, n):
            name, j = P1_PARTS[n]
            v = mem(ring.slot[name])
            if name in ("z", "pu"):
                return v[:, j * SUB:j * SUB + SUB].rearrange("p (k n) -> p k n", n=512)
            width = 256 if name == "kvab" else 512
            return v[:, 0:KT * width].rearrange("p (k n) -> p k n", k=KT)[:, :, j * P:j * P + P]

        def p1_hi(n):
            v = p1_bufs[n % HI_BUFS][:, :]
            return v.rearrange("p (k n) -> p k n", n=512 if P1_PARTS[n][0] in ("z", "pu") else P)

        P1_LOW_V = [n for n in range(20) if n % 2]
        P1_LOW_P = [n for n in range(len(P1_PARTS)) if n not in P1_LOW_V]

        def w_lo(s):
            return lo_ring[:, s * SLOT:(s + 1) * SLOT] if s < MIX_SLOTS else lo_extra[:, (s - MIX_SLOTS) * SLOT:(s - MIX_SLOTS + 1) * SLOT]

        def gate_at(unit, n=1):
            v, first = (slot(3), 0) if unit < 8 else (slot(0), 8) if unit < 10 else (gates1, 10)
            return v[:, (unit - first) * 512:(unit - first + n) * 512]

        ring = mixer_ring()
        dense = mixer_ring()
        used = {"dk": ("p1_mm", 4), "dq": ("p1_mm", 8), "dv": ("p1_mm", 12), "kvab": ("p1_mm", 17), "q": ("p1_mm", 21),
                "z": ("p1_mm", 23), "pu": ("p1_mm", 25), "pool": ("up_ev", 8)}
        for a, n in enumerate(GATE_ORDER):
            used[f"gate{n}0"], used[f"gate{n}1"] = ("gate_mm", 4 * a + 2), ("gate_mm", 4 * a + 4)
            used[f"branch{n}"] = ("up_mm", 4 * a + 4)
        used["gate01"] = ("up_ev", 12)
        used["out0"], used["out1"] = ("out_mm", 2), ("out_mm", 4)
        FB = [(f, min(512, DFF - f)) for f in range(0, DFF, 512)]
        NF = DFF // P
        DPARTS = [("g", 0), ("u", 0)] + [(w, f + (w != "w")) for f in range(NF - 1) for w in "guw"] + [("w", NF - 1)]
        for b in range(len(FB)):
            for j, w in enumerate("guw"):
                dense.add(f"{w}{b}", (5, 3, 4, 0, 1, 2)[(3 * b + j) % DENSE_SLOTS])
                used[f"{w}{b}"] = ("part_mm", DPARTS.index((w, (FB[b][0] + FB[b][1]) // P - 1)) + 1)
        NFB = DFFE // 512
        moe = mixer_ring()
        def dense_part(mem, w, f):
            b, j = f // 4, f % 4
            if w == "w":
                return mem(dense.slot[f"w{b}"])[:, j * SUB:j * SUB + SUB]
            n = FB[b][1]
            return mem(dense.slot[f"{w}{b}"])[:, 0:KT * n].rearrange("p (k n) -> p k n", k=KT)[:, :, j * P:j * P + P]

        def dense_hi(n, w):
            v = dw_hi[:, (n % HI_BUFS) * SUB:(n % HI_BUFS) * SUB + SUB]
            return v if w == "w" else v.rearrange("p (k n) -> p k n", k=KT)

        PASS_ORDER = ["g0", "u0"] + [f"{w}{b + (w != 'w')}" for b in range(NFB - 1) for w in "guw"] + [f"w{NFB - 1}"]
        ahead_full = [moe.count[s] + 16 for s in range(MOE_SLOTS)]
        moe.count = list(ahead_full)
        for k, name in enumerate(PASS_ORDER):
            moe.add(name, k % MOE_SLOTS)
        PARTS = SLOT // SUB
        AHEAD = HI_BUFS - 1
        SUBS = PARTS * len(PASS_ORDER)
        last_part = {name: PARTS * k + PARTS - 1 for k, name in enumerate(PASS_ORDER)}
        PASS_CHUNKS = 3 * NFB
        PASS_ROUNDS = PASS_CHUNKS // MOE_SLOTS
        assert PASS_CHUNKS % MOE_SLOTS == 0

        def beside_dense(n, product, split):
            end = n == len(DPARTS) - 1
            for f in range(NF):
                at_n = DPARTS.index(("u", f)) + HI_BUFS - 1
                if n == at_n or end and at_n > n:
                    product(f)
                if n == at_n + 1 or end and at_n + 1 > n:
                    split(f)

        def after_part(n, product, turned_a, combine, next_pass, tokens):
            lead = HI_BUFS - 1
            for b in range(NFB):
                if n == last_part[f"u{b}"] + lead:
                    product(b)
                if n == (last_part[f"g{b + 1}"] if b < NFB - 1 else last_part[f"u{b}"] + 1) + lead:
                    turned_a(b)
            if n == last_part["g1"] + lead:
                combine()
            if n == last_part["g4"] + lead:
                next_pass()
            if n == last_part[f"u{NFB - 1}"] + lead:
                tokens()

        consts_in = sem("consts_in")
        x_in = sem("x_in")
        rel_in = sem("rel_in")
        rows_mm = sem("rows_mm")
        rows_ev = sem("rows_ev")
        rows_out = sem("rows_out")
        strip_in = sem("strip_in")
        next_layer = sem("next_layer")
        first_in = [sem(f"first_in{s}") for s in range(MIX_SLOTS)]
        out_done = sem("out_done")
        params_in, poolw_in, router_in = sem("params_in"), sem("poolw_in"), sem("router_in")
        ln1_in, ln2_in = sem("ln1_in"), sem("ln2_in")
        N_PARAMS = 5

        cleared, by_name = [], {}

        def lsem(name):
            cleared.append(sem(name))
            by_name[name] = cleared[-1]
            return cleared[-1]

        full = [lsem(f"full{s}") for s in range(MOE_SLOTS)]
        tr_mm, tr_a, tr_d = lsem("tr_mm"), lsem("tr_a"), lsem("tr_d")
        p1_mm, p1_ev = lsem("p1_mm"), lsem("p1_ev")
        pads = lsem("pads")
        p1_high, p1_low_v, p1_low_p, p1_used = (lsem(n) for n in ("p1_high", "p1_low_v", "p1_low_p", "p1_used"))
        conv_st = lsem("conv_st")
        silu_done = lsem("silu_done")
        sq_done, ss_mm, rs_done, nrm_done = lsem("sq_done"), lsem("ss_mm"), lsem("rs_done"), lsem("nrm_done")
        dg_v, dg_a = lsem("dg_v"), lsem("dg_a")
        sc_mm, sc_ev, sm_v, sm_a, pn_done = lsem("sc_mm"), lsem("sc_ev"), lsem("sm_v"), lsem("sm_a"), lsem("pn_done")
        pt_mm, pt_ev, pv_mm, pv_ev = lsem("pt_mm"), lsem("pt_ev"), lsem("pv_mm"), lsem("pv_ev")
        pool_mm, pool_ev = lsem("pool_mm"), lsem("pool_ev")
        kv_mm, kv_ev = lsem("kv_mm"), lsem("kv_ev")
        gc_mm, gc_v, gc_a = lsem("gc_mm"), lsem("gc_v"), lsem("gc_a")
        grow_mm, beta_mm, kk_mm, qk_mm, gp_mm = (lsem(n) for n in ("grow_mm", "beta_mm", "kk_mm", "qk_mm", "gp_mm"))
        dm_done, dexp_done, kkd_done, at_done, qkd_done = (lsem(n) for n in ("dm_done", "dexp_done", "kkd_done", "at_done", "qkd_done"))
        egp_done, qdec_done, rhs_done, xt0_st = (lsem(n) for n in ("egp_done", "qdec_done", "rhs_done", "xt0_st"))
        x_mm, x_ev, al_done, y_mm, y_ev, xy_mm, xt_done = (lsem(n) for n in ("x_mm", "x_ev", "al_done", "y_mm", "y_ev", "xy_mm", "xt_done"))
        xt0_v = lsem("xt0_v")
        uw_mm, u_ev, w_ev = lsem("uw_mm"), lsem("u_ev"), lsem("w_ev")
        s_zero, ws_mm, vn_done, st_mm, sc_done, s_done, o_ev = (lsem(n) for n in ("s_zero", "ws_mm", "vn_done", "st_mm", "sc_done", "s_done", "o_ev"))
        zn_done, osq_done, or_v, or_a, od_done, ot_mm, ot_ev = (lsem(n) for n in ("zn_done", "osq_done", "or_v", "or_a", "od_done", "ot_mm", "ot_ev"))
        gate_raw = lsem("gate_raw")
        gate_mm, gate_ev, up_mm, up_ev, mrg = lsem("gate_mm"), lsem("gate_ev"), lsem("up_mm"), lsem("up_ev"), lsem("mrg")
        mt_mm, mt_a, mt_d, out_mm = lsem("mt_mm"), lsem("mt_a"), lsem("mt_d"), lsem("out_mm")
        res1, lnp_done = lsem("res1"), lsem("lnp_done")
        lnv = [lsem("lnv0"), lsem("lnv1")]
        ln1_done = lsem("ln1_done")
        sg_ev, af_ev = lsem("sg_ev"), lsem("af_ev")
        res2, ln2_half, layer_done, arrived = (lsem(n) for n in ("res2", "ln2_half", "layer_done", "arrived"))
        rl_mm, rl_v, rl_a, rc_mm, ids_done = (lsem(n) for n in ("rl_mm", "rl_v", "rl_a", "rc_mm", "ids_done"))
        dispv, xg_mm, xgh_ev, xgl_ev = (lsem(n) for n in ("dispv", "xg_mm", "xgh_ev", "xgl_ev"))
        part_hi, part_lo, part_mm = lsem("part_hi"), lsem("part_lo"), lsem("part_mm")
        at_mm, ath_ev, atl_ev = lsem("at_mm"), lsem("ath_ev"), lsem("atl_ev")
        dath_ev, datl_ev = lsem("dath_ev"), lsem("datl_ev")
        ct_mm, ct_ev, ya_ev, yd_ev, cb_mm, acc_add = (lsem(n) for n in ("ct_mm", "ct_ev", "ya_ev", "yd_ev", "cb_mm", "acc_add"))

        def end_layer(engine, l):
            engine.wait_ge(layer_done, 1)
            engine.sem_inc(arrived, 1)
            engine.wait_ge(next_layer, l + 1)

        N_P1 = 25
        block = es.enter_context(nc.Block())

        hot = M[0:N_BUCKETS, 22016:22528]
        rel = M[0:N_BUCKETS, 22528:22536]
        band = M[0:QH, 22536:23048]
        bias_rows = M[0:QH, 23048:23560]

        @block.sync
        def _(sp):
            sp.dma_start(hot, A["hot"]).then_inc(rel_in, 16)
            sp.dma_start(rel, A["rel_bias"]).then_inc(rel_in, 16)
            sp.dma_start(band, A["band"]).then_inc(rel_in, 16)
            sp.dma_start(cst[:, :], A["consts"]).then_inc(consts_in, 16)
            sp.dma_start(h, A["x"][0].rearrange("(t p) d -> p t d", p=P)).then_inc(x_in, 16)

            def first_round(layer, wait=None):
                w = A["w_in"][layer].rearrange("(k p) n -> p k n", p=P)
                for name, col, n in (("kvab", C_K, 256), ("kvab", C_AB, 32), ("dk", C_DK, 512), ("dq", C_DQ, 512), ("dv", C_DV, 512)) \
                        if wait else (("dk", C_DK, 512), ("dq", C_DQ, 512), ("dv", C_DV, 512), ("kvab", C_K, 256), ("kvab", C_AB, 32)):
                    s = ring.slot[name]
                    if wait:
                        wait(dense.last[s])
                    at = 2048 if col == C_AB else 0
                    sp.dma_start(slot(s)[:, at:at + KT * n].rearrange("p (k n) -> p k n", k=KT), w[:, :, col:col + n]).then_inc(first_in[s], 16)

            first_round(0)
            with sp.Fori(0, DEPTH) as l:
                w_in = A["w_in"][bass.ds(l, 1)].rearrange("a (k p) n -> p (a k) n", p=P)
                w_br = A["w_branch"][bass.ds(l, 1)]
                w_out = A["w_out"][bass.ds(l, 1)].rearrange("a (k p) n -> p (a k) n", p=P)

                def wait_used(name):
                    which, value = used[name]
                    sp.wait_ge(by_name[which], value)

                def put(name, src, at=0):
                    s = ring.slot[name]
                    if ring.before[name] and at == 0:
                        wait_used(ring.before[name])
                    n = src.shape[1] * src.shape[2]
                    dst = slot(s)[:, at:at + n].rearrange("p (k n) -> p k n", k=src.shape[1])
                    sp.dma_start(dst, src).then_inc(full[s], 16)

                put("q", w_in[:, :, C_Q:C_Q + 512])
                put("z", w_in[:, :, C_Z:C_Z + 512])
                put("pu", w_in[:, :, C_PU:C_PU + 512])
                put("pool", A["pool_c"].rearrange("p t g s -> p (t g) s"))
                for n in GATE_ORDER:
                    for hf in range(2):
                        c = C_G + n * D + hf * 512
                        put(f"gate{n}{hf}", w_in[:, :, c:c + 512])
                for n in GATE_ORDER:
                    if n == 1:
                        sp.wait_ge(ot_ev, 2)
                    wb = w_br[:, n].rearrange("a r n -> (a r) n")
                    if n == 0:
                        s = ring.slot["branch0"]
                        wait_used(ring.before["branch0"])
                        src = wb.rearrange("(e t d) n -> e d t n", e=2, t=4)
                        dst = slot(s).rearrange("p (t n) -> p t n", t=4)
                        for e in range(2):
                            sp.dma_start(dst[HD * e:HD * e + HD], src[e]).then_inc(full[s], 16)
                    else:
                        put(f"branch{n}", wb.rearrange("(t p) n -> p t n", p=P))
                for hf in range(2):
                    put(f"out{hf}", w_out[:, :, hf * 512:hf * 512 + 512])

                def put_dense(name, src):
                    s = dense.slot[name]
                    if dense.before[name]:
                        wait_used(dense.before[name])
                    else:
                        sp.wait_ge(ot_ev, 2)
                    n = src.shape[1] * src.shape[2]
                    sp.dma_start(slot(s)[:, 0:n].rearrange("p (k n) -> p k n", k=src.shape[1]), src).then_inc(full[s], 16)

                with sp.If(l < 1):
                    g, u, w = A["ffn_w1"][0], A["ffn_w3"][0], A["ffn_w2"][0]
                    for b, (f, n) in enumerate(FB):
                        put_dense(f"g{b}", g.rearrange("(k p) n -> p k n", p=P)[:, :, f:f + n])
                        put_dense(f"u{b}", u.rearrange("(k p) n -> p k n", p=P)[:, :, f:f + n])
                        put_dense(f"w{b}", w[f:f + n].rearrange("(k p) n -> p k n", p=P))
                    first_round(1, wait_used)
                with sp.Else():
                    def expert(e):
                        return (A["moe_wg"][0, e].rearrange("a (k p) n -> p (a k) n", p=P),
                                A["moe_wu"][0, e].rearrange("a (k p) n -> p (a k) n", p=P),
                                A["moe_wd"][0, e].rearrange("a (f k p) n -> f p (a k) n", p=P, k=4))

                    def chunk(k, weights):
                        name = PASS_ORDER[k]
                        w, b = weights["guw".index(name[0])], int(name[1])
                        src = w[b] if name[0] == "w" else w[:, :, b * 512:b * 512 + 512]
                        s = k % MOE_SLOTS
                        sp.dma_start(slot(s).rearrange("p (k n) -> p k n", k=src.shape[1]), src).then_inc(full[s], 16)

                    first = expert(slice(0, 1))
                    sp.wait_ge(ot_ev, 2)
                    for s in (5, 3, 4, 6, 0, 1, 2):
                        if s <= MIX_SLOTS:
                            wait_used(ring.last[s])
                        elif s == MOE_SLOTS - 1:
                            sp.wait_ge(up_ev, 12)
                        chunk(s, first)
                    sp.wait_ge(ids_done, 1)
                    total = sp.value_load(ids[0:1, MAXP + 1:MAXP + 2], min_val=1, max_val=MAXP)
                    e0 = sp.value_load(ids[0:1, 0:1], min_val=0, max_val=NE - 1)
                    for s in range(MOE_SLOTS):
                        sp.wait_ge(full[s], ahead_full[s])
                    with sp.If(e0 > 0):
                        first = expert(bass.ds(e0, 1))
                        for k in range(MOE_SLOTS):
                            chunk(k, first)
                    with sp.Else():
                        for s in range(MOE_SLOTS):
                            sp.sem_inc(full[s], 16)
                    with sp.Fori(0, MAXP) as p:
                        def ready(k, turn):
                            sp.wait_ge(part_mm, p * SUBS + (turn * SUBS + SUBS + PARTS * (k + 1 - MOE_SLOTS)))

                        with sp.If(p < total):
                            e = sp.value_load(ids[0:1, bass.ds(p, 1)], min_val=0, max_val=NE - 1)
                            weights = expert(bass.ds(e, 1))
                            for k in range(MOE_SLOTS, PASS_CHUNKS):
                                ready(k, 0)
                                chunk(k, weights)
                            e = sp.value_load(ids[0:1, bass.ds(p + 1, 1)], min_val=0, max_val=NE - 1)
                            ready(0, 1)
                            chunk(0, expert(bass.ds(e, 1)))
                        with sp.If(p + 1 < total):
                            e = sp.value_load(ids[0:1, bass.ds(p + 1, 1)], min_val=0, max_val=NE - 1)
                            weights = expert(bass.ds(e, 1))
                            for k in range(1, MOE_SLOTS):
                                ready(k, 1)
                                chunk(k, weights)
                sp.wait_ge(layer_done, 1)
                sp.wait_ge(arrived, 4)
                assert [s.num for s in cleared] == list(range(cleared[0].num, cleared[0].num + len(cleared)))
                sp.sem_clear(range(cleared[0].num, cleared[-1].num + 1))
                sp.sem_inc(next_layer, 1)
            sp.dma_start(out[0].rearrange("(t p) d -> p t d", p=P), h).then_inc(out_done, 16)
            sp.wait_ge(out_done, 16)

        @block.gpsimd
        def _(pool):
            g = nc.gpsimd
            pool.wait_ge(consts_in, 16)
            with pool.Fori(0, DEPTH) as l:
                def row(name, n):
                    return A[name][bass.ds(l, 1)].to_broadcast([P, n])

                g.memset(convin[:, :, 0:2], 0.0).then_inc(pads, 1)
                g.memset(convin[:, :, 258:260], 0.0).then_inc(pads, 1)
                pool.dma_start(convw[:, :], A["conv_w"][bass.ds(l, 1)].rearrange("a p n -> p (a n)")).then_inc(params_in, 16)
                pool.dma_start(dnrow[:, :], row("dn_rows", 32)).then_inc(params_in, 16)
                pool.dma_start(normw[:, :], row("dn_norm_w", HD)).then_inc(params_in, 16)
                pool.dma_start(poolsc[:, :], A["pool_scale"][bass.ds(l, 1)].rearrange("a p n -> p (a n)")).then_inc(params_in, 16)
                pool.dma_start(sinkr[:, :], row("sinks", 16)).then_inc(params_in, 16)
                pool.dma_start(poolw, A["pool_w"][bass.ds(l, 1)].rearrange("a g c d -> c (a g) d")).then_inc(poolw_in, 16)
                def low(n):
                    pool.wait_ge(p1_high, n + 1)
                    g.tensor_tensor(p1_part(w_lo, n), p1_part(slot, n), p1_hi(n).bitcast(F32), ALU.subtract).then_inc(p1_low_p, 1)

                for n in P1_LOW_P[:3]:
                    low(n)
                with pool.If(l < 1):
                    pool.wait_ge(rows_ev, 1)
                    pool.dma_start(A["rows"], bias_rows.rearrange("h (a n) -> h a n", a=1).to_broadcast([QH, P, 512])).then_inc(rows_out, 16)
                    for n in P1_LOW_P[3:6]:
                        low(n)
                    pool.wait_ge(rows_out, 16)
                    rows = A["rows"]
                    shifted = bass.AP(rows.tensor, rows.offset + P - 1, [[511, P], [P * 512, QH], [1, STRIP]])
                    pool.dma_start(strip, shifted).then_inc(strip_in, 16)
                with pool.Else():
                    for n in P1_LOW_P[3:6]:
                        low(n)
                for n in P1_LOW_P[6:9]:
                    low(n)
                for c in range(4):
                    low(P1_LOW_P[9 + c])
                    src = (kT if c < 2 else qT)[:, 2 * (c % 2):2 * (c % 2) + 2, :].rearrange("p a b -> p (a b)")
                    pool.wait_ge(silu_done, c + 1)
                    g.tensor_tensor(sq[:, c, :], src, src, ALU.mult).then_inc(sq_done, 1)
                for n in P1_LOW_P[13:]:
                    low(n)
                pool.wait_ge(params_in, l * (16 * N_PARAMS) + 16 * N_PARAMS)
                pool.wait_ge(p1_ev, 23)
                for T in range(NT):
                    v = zs[:, T, :].rearrange("p (h d) -> p h d", h=DNH)
                    g.tensor_tensor(v, v, normw[:, :].rearrange("p (a d) -> p a d", a=1).to_broadcast([P, DNH, HD]),
                                    ALU.mult).then_inc(zn_done, 1)
                pool.wait_ge(pool_mm, 2)
                g.memset(M[:, 8192:9216], 0.0).then_inc(s_zero, 1)

                def norm(which):
                    for T in range(NT):
                        pool.wait_ge(lnv[T], 6 * which + 4)
                        g.tensor_tensor(rstd[:, T:T + 1], rstd[:, T:T + 1], scal[:, 4:5], ALU.pow).then_inc(lnp_done, 1)

                def set_tiles(i):
                    d, T = SETS[i]
                    kp = i % 2

                    def head(v):
                        return v.rearrange("p (h c) -> p h c", h=DNH)

                    def scale(v):
                        return v.rearrange("p (h c) -> p h c", c=1).to_broadcast([P, DNH, HD])

                    if i == 0:
                        pool.wait_ge(kv_ev, 4)
                        pool.wait_ge(gc_a, 2)
                        pool.wait_ge(gc_v, 6)
                        pool.wait_ge(pv_ev, 2)
                    else:
                        pool.wait_ge(uw_mm, i)
                    if i >= 2:
                        pool.wait_ge(st_mm, 4)
                    g.tensor_tensor(head(Rv), head(vtok[:, T, :]), scale(beta[:, T, 8 * d:8 * d + 8]), ALU.mult).then_inc(rhs_done, 1)
                    g.tensor_tensor(head(Rw), head(ktok[:, T, :]), scale(bG[:, i, :]), ALU.mult).then_inc(rhs_done, 1)
                    g.tensor_tensor(head(kdec[kp]), head(ktok[:, T, :]), scale(kds[:, i, :]), ALU.mult).then_inc(rhs_done, 1)
                    pool.wait_ge(at_done, i + 1)
                    lv = C(f"lvl{d}0").rearrange("p (a c) -> p a c", a=1).to_broadcast([P, 4, P])
                    idb = ident.rearrange("p (a c) -> p a c", a=1).to_broadcast([P, 4, P])
                    g.tensor_tensor(AL[:, 4:8, :], AT[:, 4:8, :], lv, ALU.mult).then_inc(xt0_st, 1)
                    pool.wait_ge(xt0_st, 2 * i + 1)
                    g.tensor_tensor(XT[:, 4:8, :], idb, AL[:, 4:8, :], ALU.subtract).then_inc(xt0_st, 1)
                    pool.wait_ge(xt0_st, 2 * i + 2)
                    pool.wait_ge(xt0_v, 2 * i + 2)
                    pool.wait_ge(egp_done, i + 1)
                    g.tensor_tensor(qdec[kp], qT[:, :, T * P:T * P + P], eGp, ALU.mult).then_inc(qdec_done, 1)
                    g.tensor_copy(cd[:, i, :, :], eGp[:, :, (CHUNK - 1 if d == 0 else 0)::CHUNK]).then_inc(qdec_done, 1)
                    for lev in range(1, LEVELS):
                        lv = C(f"lvl{d}{lev}").rearrange("p (a c) -> p a c", a=1).to_broadcast([P, 4, P])
                        for q in range(2):
                            n = (i * 5 + lev - 1) * 2 + q
                            if lev > 1:
                                pool.wait_ge(y_mm, n - 1)
                            g.tensor_tensor(AL[:, 4 * q:4 * q + 4, :], AT[:, 4 * q:4 * q + 4, :], lv, ALU.mult).then_inc(al_done, 1)

                def scan_step(n):
                    for d in range(2):
                        i = 2 * (n // 2) + d
                        c = n if d == 0 else 3 - n
                        k = 2 * n + d
                        if n == 0:
                            pool.wait_ge(s_zero, 1)
                            pool.wait_ge(qdec_done, 4)
                        elif n == 2:
                            pool.wait_ge(qdec_done, 8)
                        if n:
                            pool.wait_ge(s_done, 2 * (k - 1))
                        cc = cd[:, i, :, c % 2].rearrange("p (k o) -> p k o", o=1).to_broadcast([P, 4, P])
                        g.tensor_tensor(Sc[:, d], S[:, d], cc, ALU.mult).then_inc(sc_done, 1)

                set_tiles(0)
                set_tiles(1)
                scan_step(0)
                scan_step(1)
                set_tiles(2)
                set_tiles(3)
                scan_step(2)
                scan_step(3)
                pool.wait_ge(o_ev, 8)
                pool.wait_ge(uw_mm, 4)
                for T in range(NT):
                    g.tensor_tensor(M[:, 17408 + 512 * T:17920 + 512 * T], osum[:, T, :], osum[:, T, :], ALU.mult).then_inc(osq_done, 1)
                pool.wait_ge(ot_ev, 2)
                pool.dma_start(lng, row("ln1_g", D)).then_inc(ln1_in, 16)
                pool.dma_start(lnb, row("ln1_b", D)).then_inc(ln1_in, 16)
                for k in range(4, 12):
                    T, hf = (k % 4) % 2, (k % 4) // 2
                    mv = merged[:, T, hf * 512:hf * 512 + 512]
                    pool.wait_ge(up_ev, k + 1)
                    if k >= 8:
                        pool.wait_ge(mrg, k - 4 - 3)
                    g.tensor_tensor(mv, mv, gtmp[:, k % 2, :], ALU.add).then_inc(mrg, 1)
                norm(0)
                pool.wait_ge(ln1_done, NT)
                pool.dma_start(lng, row("ln2_g", D)).then_inc(ln2_in, 16)
                pool.dma_start(lnb, row("ln2_b", D)).then_inc(ln2_in, 16)
                with pool.If(l > 0):
                    pool.dma_start(router, A["router_w"][0].rearrange("(k p) e -> p k e", p=P)).then_inc(router_in, 16)
                norm(1)
                end_layer(pool, l)

        @block.tensor
        def _(pe):
            t = nc.tensor

            def mm(o, a, b, start=True, stop=True, shared=False):
                return t.matmul(o, a, b, start=start, stop=stop, skip_group_check=shared)

            pe.wait_ge(consts_in, 16)
            pe.wait_ge(rel_in, 48)
            mm(ps[0][0:QH, :], rel, hot).then_inc(rows_mm, 1)
            pe.wait_ge(rows_ev, 1)
            pe.wait_ge(x_in, 16)
            with pe.Fori(0, DEPTH) as l:
                def loaded(r, name):
                    if name in ("dk", "dq", "dv", "kvab"):
                        n = 32 if name == "kvab" else 16
                        pe.wait_ge(first_in[r.slot[name]], l * n + n)
                        return
                    pe.wait_ge(full[r.slot[name]], r.full[name])

                def turn_h(normed=False):
                    for i in range(4):
                        T, kq = i // 2, i % 2
                        if normed and kq == 0:
                            pe.wait_ge(ln1_done, T + 1)
                        for j in range(4):
                            k = 4 * kq + j
                            last = t.transpose(ps[i][:, j * P:j * P + P], h[:, T, k * P:k * P + P], ident)
                        last.then_inc(tr_mm, 1)

                turn_h()
                pe.wait_ge(tr_d, 4)
                unit = [0]

                def p1_halves(n):
                    loaded(ring, P1_PARTS[n][0])
                    if n in P1_LOW_V:
                        pe.wait_ge(p1_low_v, P1_LOW_V.index(n) + 1)
                    else:
                        pe.wait_ge(p1_low_p, P1_LOW_P.index(n) + 1)
                    return p1_hi(n), p1_part(w_lo, n)

                def p1_tile(name, j):
                    u = unit[0]
                    if u >= 4:
                        pe.wait_ge(p1_ev, u - 3)
                    hi, lo = p1_halves(P1_PARTS.index((name, j)))
                    o = ps[4 + u % 4][:, 0:SEQ]
                    for k in range(KT):
                        mm(o, hi[:, k, :], xTh[:, k, :], k == 0, False)
                        mm(o, hi[:, k, :], xTl[:, k, :], False, False)
                        last = mm(o, lo[:, k, :], xTh[:, k, :], False, k == KT - 1)
                    last.then_inc(p1_mm, 1)
                    unit[0] += 1

                def p1_rows(name, parts):
                    u = unit[0]
                    if parts[0] == 0:
                        pe.wait_ge(p1_ev, u - 2)
                    for s in parts:
                        hi, lo = p1_halves(P1_PARTS.index((name, s)))
                        for T in range(NT):
                            o = ps[4 + (u + T) % 4][:, :]
                            for j in range(2):
                                k = 2 * s + j
                                c = slice(T * P, T * P + P)
                                mm(o, xTh[:, k, c], hi[:, j, :], k == 0, False)
                                mm(o, xTh[:, k, c], lo[:, j, :], False, False)
                                last = mm(o, xTl[:, k, c], hi[:, j, :], False, k == KT - 1)
                            if s == 3:
                                last.then_inc(p1_mm, 1)
                        if s < 3:
                            last.then_inc(p1_used, 1)
                    if parts[-1] == 3:
                        unit[0] += 2

                for name in ("dk", "dq", "dv"):
                    for j in range(4):
                        p1_tile(name, j)
                kv = slot(ring.slot["kvab"])

                def p1_kv():
                    w = kv[:, 0:2048].rearrange("p (k n) -> p k n", k=KT)
                    wab = kv[:, 2048:2304].rearrange("p (k n) -> p k n", k=KT)
                    p1_tile("kvab", 0)
                    pe.wait_ge(tr_d, 8)
                    unit[0] -= 1
                    for what, n, off in ((w, P, P), (wab, 32, 0)):
                        for T in range(NT):
                            unit[0] += 1
                            u = unit[0]
                            pe.wait_ge(p1_ev, u - 3)
                            for k in range(KT):
                                last = mm(ps[4 + u % 4][:, 0:n], hT[:, k, T * P:T * P + P], what[:, k, off:off + n], k == 0, k == KT - 1)
                            last.then_inc(p1_mm, 1)
                    unit[0] += 1

                p1_kv()
                for j in range(4):
                    p1_tile("q", j)
                p1_rows("z", range(4))
                for c in range(4):
                    pe.wait_ge(sq_done, c + 1)
                    mm(ps[c][:, :], C("blk"), sq[:, c, :]).then_inc(ss_mm, 1)

                def score(n):
                    e = n % 2
                    if n < 4:
                        pe.wait_ge(rs_done, n + 1)
                    else:
                        pe.wait_ge(sc_ev, n - 3)
                    for i in (n - e, n - e + 1):
                        Q, tt, r = i // 4, i % 4, HD * e
                        last = mm(ps[n % 4][:, (i % 2) * SEQ:(i % 2) * SEQ + SEQ], qA[r:r + HD, tt, Q * P:Q * P + P], kA[r:r + HD, :])
                    last.then_inc(sc_mm, 1)

                pe.wait_ge(p1_ev, 21)
                for n in range(4):
                    score(n)
                p1_rows("pu", range(2))
                for n in range(4, 8):
                    score(n)
                p1_rows("pu", range(2, 4))
                pe.wait_ge(p1_ev, N_P1)
                for b, src in ((0, vT), (1, kT)):
                    if b:
                        pe.wait_ge(nrm_done, 4)
                    else:
                        pe.wait_ge(silu_done, 6)
                    for T in range(NT):
                        for j in range(4):
                            last = t.transpose(ps[4 + 2 * b + T][:, j * P:j * P + P], src[:, j, T * P:T * P + P], ident)
                        last.then_inc(kv_mm, 1)
                filled = [0]

                def fill(n):
                    for _ in range(n):
                        unit, k = divmod(filled[0], KT)
                        filled[0] += 1
                        name, T = GATES[unit // 2], unit % 2
                        if k == 0:
                            loaded(ring, name)
                            if unit >= 2:
                                pe.wait_ge(gate_raw, unit - 1)
                        w = slot(ring.slot[name]).rearrange("p (k n) -> p k n", k=KT)
                        last = mm(ps[6 + unit % 2][:, :], hT[:, k, T * P:T * P + P], w[:, k, :], k == 0, k == KT - 1)
                        if k == KT - 1:
                            last.then_inc(gate_mm, 1)

                loaded(ring, "pool")
                B = slot(ring.slot["pool"])[:, 0:2048].rearrange("p (t g s) -> p t g s", t=NT, g=BT)
                for b in range(2):
                    pe.wait_ge(kv_ev, b + 1)
                    for g2 in range(2):
                        grp = 2 * b + g2
                        for T in range(NT):
                            last = mm(ps[4 + b][:, g2 * SEQ:g2 * SEQ + SEQ], pu[:, T, grp * P:grp * P + P], B[:, T, grp, :],
                                      T == 0, T == NT - 1)
                last.then_inc(pool_mm, 1)
                pe.wait_ge(pool_ev, 2)
                pe.wait_ge(poolw_in, l * 16 + 16)
                for b in range(2):
                    pe.wait_ge(kv_ev, b + 3)
                    for g2 in range(2):
                        grp = 2 * b + g2
                        last = mm(ps[6 + b][:, g2 * SEQ:g2 * SEQ + SEQ], poolw[:, grp, :], mixT[:, grp, :])
                last.then_inc(pool_mm, 1)
                pe.wait_ge(pool_ev, 6)
                fill(2 * KT)
                pe.wait_ge(sc_ev, 8)

                def turn_probs(i):
                    pe.wait_ge(pn_done, i + 1)
                    if i >= 2:
                        pe.wait_ge(pt_ev, i - 1)
                    for e in range(2):
                        for jt in range(NT):
                            last = t.transpose(ps[i % 2][:, (2 * e + jt) * P:(2 * e + jt + 1) * P],
                                               Sall[:, i, e, jt * P:jt * P + P], ident)
                    last.then_inc(pt_mm, 1)

                turn_probs(0)
                for i in range(8):
                    Q, tt = i // 4, i % 4
                    if i < 7:
                        turn_probs(i + 1)
                    pe.wait_ge(pt_ev, i + 1)
                    for e in range(2):
                        for jt in range(NT):
                            last = mm(ps[2 + Q][HD * e:HD * e + HD, tt * P:tt * P + P], vA[:, jt, HD * e:HD * e + HD],
                                      PT[:, i % 2, (2 * e + jt) * P:(2 * e + jt + 1) * P], jt == 0, jt == NT - 1)
                    last.then_inc(pv_mm, 1)
                pe.wait_ge(dg_v, 6)
                for i, (d, T) in enumerate(SETS):
                    gi = gg[:, T, 8 * d:8 * d + 8]
                    mm(ps[4][:, 16 * i:16 * i + 8], C(f"cum{d}"), gi)
                    last = mm(ps[4][:, 16 * i + 8:16 * i + 16], C("blk"), gi)
                last.then_inc(gc_mm, 1)
                pe.wait_ge(pv_ev, 2)
                pe.wait_ge(gc_v, 1)
                pe.wait_ge(pool_ev, 6)

                def inverse_and_sides(i):
                    d, T = SETS[i]
                    kp = i % 2
                    if i:
                        pe.wait_ge(x_ev, 10 * i)
                        pe.wait_ge(y_ev, 10 * i)
                        pe.wait_ge(xt_done, 10 * i)
                        pe.wait_ge(u_ev, i)
                        pe.wait_ge(w_ev, i)
                    if i == 2:
                        pe.wait_ge(s_done, 8)
                        pe.wait_ge(o_ev, 4)
                    for w, hh in enumerate(HEAD_AT):
                        o = ps[w // 4][:, (w % 4) * P:(w % 4) * P + P]
                        last = mm(o, gg[:, T, 8 * d + hh:8 * d + hh + 1].to_broadcast([P, P]), C(f"cum{d}"))
                    last.then_inc(grow_mm, 1)
                    for w, hh in enumerate(HEAD_AT):
                        pr, r = hh // 2, HD * (hh % 2)
                        kh = kT[r:r + HD, pr, T * P:T * P + P]
                        last = mm(ps[4 + w // 4][:, (w % 4) * P:(w % 4) * P + P], kh, kh)
                    last.then_inc(kk_mm, 1)
                    for w, hh in enumerate(HEAD_AT):
                        last = mm(ps[2 + w // 4][:, (w % 4) * P:(w % 4) * P + P],
                                  beta[:, T, 8 * d + hh:8 * d + hh + 1].to_broadcast([P, P]), ident)
                    last.then_inc(beta_mm, 1)
                    pe.wait_ge(gate_raw, 2 * i + 2)
                    for w, hh in enumerate(HEAD_AT):
                        pr, r = hh // 2, HD * (hh % 2)
                        last = mm(ps[6 + w // 4][:, (w % 4) * P:(w % 4) * P + P], kT[r:r + HD, pr, T * P:T * P + P],
                                  qT[r:r + HD, pr, T * P:T * P + P])
                    last.then_inc(qk_mm, 1)
                    pe.wait_ge(dm_done, i + 1)
                    for hh in range(DNH):
                        r = HD * (hh % 2)
                        last = mm(ps[0][r:r + HD, (hh // 2) * P:(hh // 2) * P + P],
                                  gg[:, T, 8 * d + hh:8 * d + hh + 1].to_broadcast([P, HD]), C(f"cum{d}"))
                    last.then_inc(gp_mm, 1)
                    pe.wait_ge(egp_done, i + 1)
                    pe.wait_ge(at_done, i + 1)
                    for lev in range(1, LEVELS):
                        for q in range(2):
                            n = (i * 5 + lev - 1) * 2 + q
                            if lev > 1:
                                pe.wait_ge(xt_done, n - 1)
                            else:
                                pe.wait_ge((xt0_v, xt0_st)[q], 2 * i + 2)
                            for j in range(4):
                                last = t.transpose(ps[q][:, j * P:j * P + P], XT[:, 4 * q + j, :], ident)
                            last.then_inc(x_mm, 1)
                        if lev == 1:
                            pe.wait_ge(qkd_done, i + 1)
                        fill(2 if lev in (1, LEVELS - 1) else 1)
                        for q in range(2):
                            n = (i * 5 + lev - 1) * 2 + q
                            pe.wait_ge(x_ev, n + 1)
                            pe.wait_ge(al_done, n + 1)
                            for j in range(4):
                                last = mm(ps[2 + q][:, j * P:j * P + P], AL[:, 4 * q + j, :], X[:, 4 * q + j, :])
                            last.then_inc(y_mm, 1)
                        fill(1)
                        for q in range(2):
                            n = (i * 5 + lev - 1) * 2 + q
                            pe.wait_ge(y_ev, n + 1)
                            for j in range(4):
                                last = mm(ps[4 + q][:, j * P:j * P + P], Dm[:, 4 * q + j, :], XT[:, 4 * q + j, :])
                            last.then_inc(xy_mm, 1)
                        if lev < LEVELS - 1:
                            fill(1)
                    pe.wait_ge(xt_done, 10 * (i + 1))
                    pe.wait_ge(rhs_done, 3 * (i + 1))
                    pe.wait_ge(gate_raw, 2 * i + 4)
                    for w, hh in enumerate(HEAD_AT):
                        pr, r = hh // 2, HD * (hh % 2)
                        mm(ps[6][:, HD * hh:HD * hh + HD], XT[:, w, :], Rv[:, HD * hh:HD * hh + HD])
                        last = mm(ps[7][r:r + HD, pr * P:pr * P + P], Rw[:, HD * hh:HD * hh + HD], XT[:, w, :])
                    last.then_inc(uw_mm, 1)

                def scan_step(n):
                    if n % 2 == 0:
                        pe.wait_ge(u_ev, n + 2)
                        pe.wait_ge(w_ev, n + 2)
                        pe.wait_ge(qdec_done, 2 * (n + 2))
                        pe.wait_ge(xt_done, 10 * (n + 2))
                    if n == 0:
                        pe.wait_ge(s_zero, 1)
                    for d in range(2):
                        i, c, k = 2 * (n // 2) + d, (n if d == 0 else 3 - n), 2 * n + d
                        kp, r, b = i % 2, CHUNK * (c % 2), 3 * d
                        if n:
                            pe.wait_ge(s_done, 2 * (k - 1))
                            pe.wait_ge(o_ev, k - 1)
                        for pr in range(4):
                            mm(ps[b][r:r + CHUNK, pr * P:pr * P + P], wT[kp][:, pr, r:r + CHUNK], S[:, d, pr, :])
                            last = mm(ps[b + 1][r:r + CHUNK, pr * P:pr * P + P], qdec[kp][:, pr, r:r + CHUNK], S[:, d, pr, :],
                                      pr == 0, False, True)
                        last.then_inc(ws_mm, 1)
                    if n >= 2:
                        fill(4)
                    for d in range(2):
                        i, c, k = 2 * (n // 2) + d, (n if d == 0 else 3 - n), 2 * n + d
                        kp, r, b = i % 2, CHUNK * (c % 2), 3 * d
                        pe.wait_ge(vn_done, k + 1)
                        for pr in range(4):
                            mm(ps[b + 2][:, pr * P:pr * P + P], kdec[kp][r:r + CHUNK, pr * P:pr * P + P],
                               vnew[r:r + CHUNK, n % 2, pr * P:pr * P + P])
                        for w, hh in enumerate(HEAD_AT):
                            last = mm(ps[b + 1][r:r + CHUNK, HD * hh:HD * hh + HD], qkd[kp][r:r + CHUNK, w, r:r + CHUNK],
                                      vnew[r:r + CHUNK, n % 2, HD * hh:HD * hh + HD], False, w == DNH - 1, True)
                        last.then_inc(st_mm, 1)

                inverse_and_sides(0)
                inverse_and_sides(1)
                scan_step(0)
                scan_step(1)
                inverse_and_sides(2)
                inverse_and_sides(3)
                scan_step(2)
                scan_step(3)
                fill(KT)
                pe.wait_ge(od_done, 1)
                for T in range(NT):
                    for j in range(4):
                        last = t.transpose(ps[4 + T][:, j * P:j * P + P], osum[:, T, j * P:j * P + P], ident)
                    last.then_inc(ot_mm, 1)
                pe.wait_ge(ot_ev, 2)
                pe.wait_ge(s_done, 16)
                pe.wait_ge(o_ev, 8)
                pe.wait_ge(gate_raw, 12)
                for a, n in enumerate(GATE_ORDER):
                    loaded(ring, f"branch{n}")
                    w = slot(ring.slot[f"branch{n}"]).rearrange("p (k n) -> p k n", k=BT)
                    src = (oAT, oDT, oPT)[n]
                    for hf in range(2):
                        for T in range(NT):
                            j = 2 * hf + T
                            if a:
                                pe.wait_ge(up_ev, 4 * (a - 1) + j + 1)
                            for k in range(BT):
                                last = mm(ps[4 + j][:, :], src[:, k, T * P:T * P + P], w[:, k, hf * 512:hf * 512 + 512],
                                          k == 0, k == BT - 1)
                            last.then_inc(up_mm, 1)
                pe.wait_ge(mrg, 8)
                for i in range(4):
                    T, kq = i // 2, i % 2
                    for j in range(4):
                        k = 4 * kq + j
                        last = t.transpose(ps[i][:, j * P:j * P + P], merged[:, T, k * P:k * P + P], ident)
                    last.then_inc(mt_mm, 1)
                pe.wait_ge(mt_a, 2)
                pe.wait_ge(mt_d, 2)
                for hf in range(2):
                    loaded(ring, f"out{hf}")
                    w = slot(ring.slot[f"out{hf}"]).rearrange("p (k n) -> p k n", k=KT)
                    for T in range(NT):
                        for k in range(KT):
                            last = mm(ps[4 + 2 * hf + T][:, :], mT[:, k, T * P:T * P + P], w[:, k, :], k == 0, k == KT - 1)
                        last.then_inc(out_mm, 1)
                turn_h(True)
                pe.wait_ge(res1, 4)
                with pe.If(l < 1):
                    pe.wait_ge(tr_d, 12)

                    def up(n, w, f):
                        if w == "g" and f >= 2:
                            pe.wait_ge(af_ev, f - 1)
                        pe.wait_ge(part_lo, n + 1)
                        hi, lo = dense_hi(n, w), dense_part(w_lo, w, f)
                        o = ps[f % 2][:, 0:SEQ] if w == "g" else ps[f % 2][:, SEQ:2 * SEQ]
                        for k in range(KT):
                            mm(o, hi[:, k, :], hTh[:, k, :], k == 0, False)
                            mm(o, hi[:, k, :], hTl[:, k, :], False, False)
                            last = mm(o, lo[:, k, :], hTh[:, k, :], False, k == KT - 1)
                        last.then_inc(part_mm, 1)

                    def down(n, f):
                        pe.wait_ge(datl_ev, f + 1)
                        pe.wait_ge(part_lo, n + 1)
                        hi, lo = dense_hi(n, "w"), dense_part(w_lo, "w", f)
                        for T in range(NT):
                            ah, al = dath[:, f % 4, T * P:T * P + P], datl[:, f % 4, T * P:T * P + P]
                            for dh in range(2):
                                o, c = ps[4 + 2 * T + dh][:, :], slice(dh * 512, dh * 512 + 512)
                                mm(o, ah, hi[:, c], f == 0, False)
                                mm(o, ah, lo[:, c], False, False)
                                last = mm(o, al, hi[:, c], False, f == NF - 1)
                        last.then_inc(part_mm, 1)

                    for n, (w, f) in enumerate(DPARTS):
                        if w == "w":
                            down(n, f)
                        else:
                            up(n, w, f)
                with pe.Else():
                    pe.wait_ge(tr_a, 6)
                    pe.wait_ge(tr_d, 10)
                    pe.wait_ge(router_in, 16)
                    for T in range(NT):
                        for k in range(KT):
                            last = mm(ps[T][:, 0:NE], hT[:, k, T * P:T * P + P], router[:, k, :], k == 0, k == KT - 1)
                        last.then_inc(rl_mm, 1)
                    pe.wait_ge(rl_v, 12)
                    one = scal[:, 3:4].to_broadcast([P, P])
                    mm(ps[2][:, 0:8], C("before"), sel[:, 0, :])
                    mm(ps[2][:, 8:16], C("before"), sel[:, 1, :], True, False)
                    mm(ps[2][:, 8:16], one, sel[:, 0, :], False, True)
                    mm(ps[2][:, 16:24], one, sel[:, 0, :], True, False)
                    mm(ps[2][:, 16:24], one, sel[:, 1, :], False, True).then_inc(rc_mm, 1)
                    pe.wait_ge(ids_done, 1)
                    pe.sem_inc(part_mm, SUBS)

                    def gather():
                        for k in range(KT):
                            for T in range(NT):
                                last = mm(ps[2 + k // 4][:, (k % 4) * CAP:(k % 4) * CAP + CAP], h[:, T, k * P:k * P + P],
                                          disp[:, T, :], T == 0, T == NT - 1)
                        last.then_inc(xg_mm, 1)

                    pe.wait_ge(dispv, 12)
                    gather()
                    total = pe.value_load(ids[0:1, MAXP + 1:MAXP + 2], min_val=1, max_val=MAXP)
                    with pe.Fori(0, MAXP) as p:
                        with pe.If(p < total):
                            def part(name, s):
                                n = last_part[name] - (PARTS - 1) + s
                                pe.wait_ge(part_lo, p * SUBS + (n + 1))
                                at_hi = (n % HI_BUFS) * SUB
                                return w_hi[:, at_hi:at_hi + SUB], w_lo(moe.slot[name])[:, s * SUB:s * SUB + SUB]

                            def up(w, b):
                                o = ps[2 * (b % 2) + (w == "u")][0:CAP, :]
                                for s in range(PARTS):
                                    hi, lo = part(f"{w}{b}", s)
                                    for j in range(SUB // 512):
                                        k = (SUB // 512) * s + j
                                        hi_j, lo_j = hi[:, j * 512:j * 512 + 512], lo[:, j * 512:j * 512 + 512]
                                        mm(o, xgh[:, k, :], hi_j, k == 0, False)
                                        mm(o, xgh[:, k, :], lo_j, False, False)
                                        last = mm(o, xgl[:, k, :], hi_j, False, k == KT - 1)
                                    last.then_inc(part_mm, 1)

                            def turn_a(b):
                                pe.wait_ge(af_ev, p * NFB + (b + 1))
                                if b == NFB - 1:
                                    pe.wait_ge(atl_ev, p * NFB + b)
                                for j in range(4):
                                    last = t.transpose(ps[6][:, j * CAP:j * CAP + CAP], ae[0:CAP, b % 2, j * P:j * P + P], ident[0:CAP, 0:CAP])
                                last.then_inc(at_mm, 1)

                            def down(b):
                                pe.wait_ge(atl_ev, p * NFB + (b + 1))
                                for s in range(PARTS):
                                    hi, lo = part(f"w{b}", s)
                                    for a, w, stop in ((ath, hi, False), (ath, lo, False), (atl, hi, True)):
                                        for dh in range(2):
                                            last = mm(ps[4 + dh][0:CAP, :], a[:, b % 2, s, :], w[:, dh * 512:dh * 512 + 512],
                                                      b == 0 and s == 0 and a is ath and w is hi,
                                                      b == NFB - 1 and s == PARTS - 1 and stop)
                                    last.then_inc(part_mm, 1)

                            pe.wait_ge(xgl_ev, p * 2 + 2)
                            up("g", 0)
                            pe.wait_ge(acc_add, p * 4 + 4)
                            for T in range(NT):
                                last = t.transpose(ps[7][0:CAP, T * P:T * P + P], comb[:, T, :], ident)
                            last.then_inc(ct_mm, 1)
                            up("u", 0)
                            for b in range(1, NFB):
                                up("g", b)
                                if b < NFB - 1:
                                    turn_a(b - 1)
                                    up("u", b)
                                    down(b - 1)
                            turn_a(NFB - 2)
                            up("u", NFB - 1)
                            pe.wait_ge(dispv, p * 12 + 24)
                            gather()
                            turn_a(NFB - 1)
                            down(NFB - 2)
                            down(NFB - 1)
                            pe.wait_ge(ct_ev, p + 1)
                            for q in range(4):
                                T, dh = q // 2, q % 2
                                if q == 0:
                                    pe.wait_ge(ya_ev, p + 1)
                                if q == 1:
                                    pe.wait_ge(yd_ev, p + 1)
                                if q >= 2:
                                    pe.wait_ge(acc_add, p * 4 + (4 + q - 1))
                                mm(ps[7 - dh][:, :], combT[0:CAP, T, :], y[0:CAP, dh * 512:dh * 512 + 512]).then_inc(cb_mm, 1)
                end_layer(pe, l)

        @block.scalar
        def _(act):
            def f(o, i, func=ACT.Copy, **kw):
                return nc.scalar.activation(o, i, func, **kw)

            eps6, lnq = scal[:, 0:1], scal[:, 2:3]
            one = scal[:, 3:4]
            act.wait_ge(consts_in, 16)
            with act.Fori(0, DEPTH) as l:
                def turned(mm_sem, a_sem, dst, base):
                    for i in (0, 2):
                        T, kq = i // 2, i % 2
                        act.wait_ge(mm_sem, 4 * base + i + 1)
                        f(dst[:, 4 * kq:4 * kq + 4, T * P:T * P + P],
                          ps[i][:, :].rearrange("p (j q) -> p j q", j=4)).then_inc(a_sem, 1)

                def turned_hi(dst, base):
                    for i in range(4):
                        act.wait_ge(tr_mm, base + i + 1)
                        f(dst[:, 4 * (i % 2):4 * (i % 2) + 4, (i // 2) * P:(i // 2) * P + P],
                          ps[i][:, :].rearrange("p (j q) -> p j q", j=4)).then_inc(tr_a, 1)

                def high(n):
                    name = P1_PARTS[n][0]
                    if name in ("q", "z", "pu"):
                        act.wait_ge(full[ring.slot[name]], ring.full[name])
                    else:
                        act.wait_ge(first_in[ring.slot[name]], l * (32 if name == "kvab" else 16) + (32 if name == "kvab" else 16))
                    last = n - HI_BUFS
                    if last >= 17 and last < 20:
                        act.wait_ge(p1_used, last - 16)
                    elif last >= 0:
                        act.wait_ge(p1_mm, 23 if last == 20 else last + 1 + (4 if last > 12 else 0))
                    f(p1_hi(n), p1_part(slot, n)).then_inc(p1_high, 1)

                for n in range(HI_BUFS):
                    high(n)
                turned_hi(xTh, 0)
                act.wait_ge(pads, 2)
                dst = [convin[:, t, 2:258] for t in range(12)] + [kA, vA[:, 0, :], vA[:, 1, :], ab[:, 0, :], ab[:, 1, :]]
                dst += [qA[:, t, :] for t in range(4)] + [zs[:, 0, :], zs[:, 1, :], pu[:, 0, :], pu[:, 1, :]]

                def evac(u):
                    act.wait_ge(p1_mm, u + 1)
                    n = dst[u].shape[1]
                    f(dst[u], ps[4 + u % 4][:, 0:n], ACT.Silu if u in (21, 22) else ACT.Copy).then_inc(p1_ev, 1)

                def silu(j):
                    v = (kT, qT, vT)[j // 2][:, 2 * (j % 2):2 * (j % 2) + 2, :]
                    act.wait_ge(conv_st, 10 * (j + 1))
                    f(v, v, ACT.Silu).then_inc(silu_done, 1)

                for u in range(23):
                    if u == 21:
                        for n in (21, 22, 23):
                            high(n)
                    evac(u)
                    if u < 13:
                        high(u + 4)
                    elif 17 <= u < 21:
                        high(u)
                    if u >= 4 and u % 2 == 0 and (u - 4) // 2 < 6:
                        silu((u - 4) // 2)
                high(24)
                act.wait_ge(params_in, l * (16 * N_PARAMS) + 16 * N_PARAMS)
                f(ea, dnrow[:, 16:32], ACT.Exp).then_inc(dg_a, 1)
                act.wait_ge(dg_v, 2)
                f(lnp, nab, ACT.Exp, scale=-1.0).then_inc(dg_a, 1)
                act.wait_ge(p1_ev, 17)
                f(eb, ab[:, :, 16:32], ACT.Exp, scale=-1.0).then_inc(dg_a, 1)
                act.wait_ge(dg_a, 2)
                f(lnp, lnp, ACT.Ln, bias=one).then_inc(dg_a, 1)
                for c in range(4):
                    act.wait_ge(ss_mm, c + 1)
                    f(rs[:, c, :], ps[c][:, :], ACT.Ln, bias=eps6).then_inc(rs_done, 1)
                for c in range(4):
                    act.wait_ge(rs_done, c + 1)
                    if c < 2:
                        f(rs[:, c, :], rs[:, c, :], ACT.Exp, scale=-0.5).then_inc(rs_done, 1)
                    else:
                        f(rs[:, c, :], rs[:, c, :], ACT.Exp, scale=-0.5, bias=lnq).then_inc(rs_done, 1)
                evac(23)
                evac(24)
                for b in range(4):
                    act.wait_ge(kv_mm, b + 1)
                    f((vtok, ktok)[b // 2][:, b % 2, :], ps[4 + b][:, :]).then_inc(kv_ev, 1)
                act.wait_ge(pool_mm, 1)
                for b in range(2):
                    f(mixT[:, 2 * b:2 * b + 2, :], ps[4 + b][:, :].rearrange("p (g s) -> p g s", g=2)).then_inc(pool_ev, 1)
                act.wait_ge(pool_mm, 2)
                for g in range(BT):
                    f(oPT[:, g, :], ps[6 + g // 2][:, (g % 2) * SEQ:(g % 2) * SEQ + SEQ], ACT.Identity,
                      scale=poolsc[:, g:g + 1]).then_inc(pool_ev, 1)
                def gate_out(unit):
                    act.wait_ge(gate_mm, unit + 1)
                    f(gate_at(unit), ps[6 + unit % 2][:, :]).then_inc(gate_raw, 1)

                act.wait_ge(sm_v, 11)
                for i in range(8):
                    for e in range(2):
                        c = 2 * i + e
                        f(Sall[:, i, e, :], Sall[:, i, e, :], ACT.Exp, bias=mneg[:, c:c + 1],
                          accum_out=psum16[:, c:c + 1]).then_inc(sm_a, 1)
                f(esink, esink, ACT.Exp).then_inc(sm_a, 1)
                gate_out(0)
                gate_out(1)
                for i in range(8):
                    act.wait_ge(pt_mm, i + 1)
                    if i >= 2:
                        act.wait_ge(pv_mm, i - 1)
                    f(PT[:, i % 2, :], ps[i % 2][:, :]).then_inc(pt_ev, 1)
                    if i % 4 == 3:
                        Q = i // 4
                        act.wait_ge(pv_mm, i + 1)
                        f(oAT[:, :, Q * P:Q * P + P], ps[2 + Q][:, :].rearrange("p (t q) -> p t q", t=4)).then_inc(pv_ev, 1)
                act.wait_ge(gc_v, 1)
                f(eG, Gc[:, :, 0:8], ACT.Exp).then_inc(gc_a, 1)
                act.wait_ge(gc_v, 2)
                f(kds, dl, ACT.Exp).then_inc(gc_a, 1)

                def set_tiles(i):
                    kp = i % 2
                    act.wait_ge(dm_done, i + 1)
                    f(Dm, Dm, ACT.Exp).then_inc(dexp_done, 1)
                    act.wait_ge(gp_mm, i + 1)
                    if i:
                        act.wait_ge(qdec_done, 2 * i)
                    f(eGp, ps[0][:, :].rearrange("p (k c) -> p k c", k=4), ACT.Exp).then_inc(egp_done, 1)
                    for lev in range(1, LEVELS):
                        for q in range(2):
                            n = (i * 5 + lev - 1) * 2 + q
                            act.wait_ge(x_mm, n + 1)
                            f(X[:, 4 * q:4 * q + 4, :], ps[q][:, :].rearrange("p (j c) -> p j c", j=4)).then_inc(x_ev, 1)
                        if lev == 1:
                            act.wait_ge(qkd_done, i + 1)
                        for q in range(2):
                            n = (i * 5 + lev - 1) * 2 + q
                            act.wait_ge(y_mm, n + 1)
                            f(Dm[:, 4 * q:4 * q + 4, :], ps[2 + q][:, :].rearrange("p (j c) -> p j c", j=4)).then_inc(y_ev, 1)
                        if lev == 3:
                            gate_out(2 * i + 2)
                    gate_out(2 * i + 3)
                    act.wait_ge(uw_mm, i + 1)
                    f(u_s[kp], ps[6][:, :]).then_inc(u_ev, 1)

                def scan_out(n):
                    for d in range(2):
                        c, k = (n if d == 0 else 3 - n), 2 * n + d
                        r = CHUNK * (c % 2)
                        act.wait_ge(st_mm, k + 1)
                        f(osum[r:r + CHUNK, c // 2, :], ps[3 * d + 1][r:r + CHUNK, :]).then_inc(o_ev, 1)

                set_tiles(0)
                set_tiles(1)
                scan_out(0)
                scan_out(1)
                set_tiles(2)
                set_tiles(3)
                act.wait_ge(uw_mm, 4)
                gate_out(10)
                act.wait_ge(or_v, 1)
                f(osr, osr, ACT.Ln, scale=1.0 / HD, bias=eps6).then_inc(or_a, 1)
                act.wait_ge(or_a, 1)
                f(osr, osr, ACT.Exp, scale=-0.5).then_inc(or_a, 1)
                gate_out(11)
                for T in range(NT):
                    act.wait_ge(ot_mm, T + 1)
                    f(oDT[:, :, T * P:T * P + P], ps[4 + T][:, :].rearrange("p (j q) -> p j q", j=4)).then_inc(ot_ev, 1)
                for first, n in ((0, 4), (4, 4), (8, 2), (10, 2)):
                    act.wait_ge(gate_raw, first + n)
                    f(gate_at(first, n), gate_at(first, n), ACT.Sigmoid).then_inc(gate_ev, 1)
                turned(mt_mm, mt_a, mT, 0)

                with act.If(l < 1):
                    turned_hi(hTh, 4)

                    def silu_tile(ft):
                        act.wait_ge(part_mm, DPARTS.index(("u", ft)) + 1)
                        if ft >= 2:
                            act.wait_ge(af_ev, ft - 1)
                        f(sg[:, ft % 2, :], ps[ft % 2][:, 0:SEQ], ACT.Silu).then_inc(sg_ev, 1)

                    def a_hi(ft):
                        act.wait_ge(af_ev, ft + 1)
                        if ft >= 4:
                            act.wait_ge(part_mm, DPARTS.index(("w", ft - 4)) + 1)
                        f(dath[:, ft % 4, :], aT[:, ft % 4, :]).then_inc(dath_ev, 1)

                    for n, (w, ft) in enumerate(DPARTS):
                        if n < 2 * DENSE_SLOTS or ft % 4 == 0:
                            act.wait_ge(full[dense.slot[f"{w}{ft // 4}"]], dense.full[f"{w}{ft // 4}"])
                        if n >= HI_BUFS:
                            act.wait_ge(part_mm, n + 1 - HI_BUFS)
                        f(dense_hi(n, w), dense_part(slot, w, ft)).then_inc(part_hi, 1)
                        beside_dense(n, silu_tile, a_hi)
                with act.Else():
                    turned(tr_mm, tr_a, hT, 1)
                    act.wait_ge(rl_v, 13)
                    f(e12, dm12, ACT.Exp).then_inc(rl_a, 1)
                    act.wait_ge(ids_done, 1)

                    def xg_out(count):
                        act.wait_ge(xg_mm, count)
                        for b in range(2):
                            f(xgh[:, 4 * b:4 * b + 4, :], ps[2 + b][:, 0:4 * CAP].rearrange("p (j c) -> p j c", j=4)).then_inc(xgh_ev, 1)

                    def hi(n, p, turn):
                        name, s = PASS_ORDER[n // PARTS], n % PARTS
                        if s == 0:
                            loads = turn * (16 * PASS_ROUNDS) + moe.full[name]
                            act.wait_ge(full[moe.slot[name]], loads if p is None else p * (16 * PASS_ROUNDS) + loads)
                        uses = turn * SUBS + SUBS + n + 1 - HI_BUFS
                        act.wait_ge(part_mm, uses if p is None else p * SUBS + uses)
                        at_hi = (n % HI_BUFS) * SUB
                        f(w_hi[:, at_hi:at_hi + SUB], slot(moe.slot[name])[:, s * SUB:s * SUB + SUB]).then_inc(part_hi, 1)

                    xg_out(1)
                    for n in range(AHEAD):
                        hi(n, None, 0)
                    total = act.value_load(ids[0:1, MAXP + 1:MAXP + 2], min_val=1, max_val=MAXP)
                    with act.Fori(0, MAXP) as p:
                        with act.If(p < total):
                            def silu(b):
                                act.wait_ge(part_mm, p * SUBS + (SUBS + last_part[f"u{b}"] + 1))
                                f(sge[0:CAP, b % 2, :], ps[2 * (b % 2)][0:CAP, :], ACT.Silu).then_inc(sg_ev, 1)

                            def a_out(b):
                                act.wait_ge(at_mm, p * NFB + (b + 1))
                                f(ath[:, b % 2, :, :], ps[6][:, 0:4 * CAP].rearrange("p (j c) -> p j c", j=4)).then_inc(ath_ev, 1)

                            def comb_out():
                                act.wait_ge(ct_mm, p + 1)
                                f(combT[0:CAP, :, :], ps[7][0:CAP, 0:NT * P].rearrange("p (t c) -> p t c", t=NT)).then_inc(ct_ev, 1)

                            for n in range(AHEAD, SUBS):
                                hi(n, p, 0)
                                after_part(n, silu, a_out, comb_out, lambda: None, lambda: xg_out(p + 2))
                            for n in range(AHEAD):
                                hi(n, p, 1)
                            act.wait_ge(part_mm, p * SUBS + 2 * SUBS)
                            f(y[0:CAP, 0:512], ps[4][0:CAP, :]).then_inc(ya_ev, 1)
                end_layer(act, l)

        @block.vector
        def _(dve):
            v = nc.vector

            def tt(o, a, b, op):
                return v.tensor_tensor(o, a, b, op)

            def stt(o, a, s, b, op0, op1):
                return v.scalar_tensor_tensor(out=o, in0=a, scalar=s, in1=b, op0=op0, op1=op1)

            def ts(o, a, s1, s2, op0, op1=None):
                return v.tensor_scalar(o, a, s1, s2, op0, op1) if op1 is not None else v.tensor_scalar(o, a, s1, None, op0)

            def over(x, *shape):
                return x.rearrange("p (h c) -> p h c", c=1).to_broadcast([P, x.shape[1], shape[0]])

            def again(x, k):
                return x.rearrange("p (a n) -> p a n", a=1).to_broadcast([P, k, x.shape[1]])

            dve.wait_ge(rel_in, 48)
            dve.wait_ge(rows_mm, 1)
            tt(bias_rows, ps[0][0:QH, :], band, ALU.add).then_inc(rows_ev, 1)
            with dve.Fori(0, DEPTH) as l:
                def turned(mm_sem, d_sem, dst, base):
                    for i in (1, 3):
                        T, kq = i // 2, i % 2
                        dve.wait_ge(mm_sem, 4 * base + i + 1)
                        v.tensor_copy(dst[:, 4 * kq:4 * kq + 4, T * P:T * P + P],
                                      ps[i][:, :].rearrange("p (j q) -> p j q", j=4)).then_inc(d_sem, 1)

                def turned_lo(dst, hi, base):
                    for i in range(4):
                        c = (slice(4 * (i % 2), 4 * (i % 2) + 4), slice((i // 2) * P, (i // 2) * P + P))
                        dve.wait_ge(tr_a, base + i + 1)
                        tt(dst[:, c[0], c[1]], ps[i][:, :].rearrange("p (j q) -> p j q", j=4), hi[:, c[0], c[1]].bitcast(F32),
                           ALU.subtract).then_inc(tr_d, 1)

                def low(n):
                    dve.wait_ge(p1_high, n + 1)
                    tt(p1_part(w_lo, n), p1_part(slot, n), p1_hi(n).bitcast(F32), ALU.subtract).then_inc(p1_low_v, 1)

                low(1)
                turned_lo(xTl, xTh, 0)
                for i in range(4):
                    v.tensor_copy(hT[:, 4 * (i % 2):4 * (i % 2) + 4, (i // 2) * P:(i // 2) * P + P],
                                  ps[i][:, :].rearrange("p (j q) -> p j q", j=4)).then_inc(tr_d, 1)
                low(3)
                dve.wait_ge(params_in, l * (16 * N_PARAMS) + 16 * N_PARAMS)
                dve.wait_ge(pads, 2)
                for j in range(6):
                    low(2 * j + 5)
                    dve.wait_ge(p1_ev, 2 * j + 2)
                    for tap in range(CONV):
                        for q in range(2):
                            t = 2 * j + q
                            o = (kT, qT, vT)[t // 4][:, t % 4, :]
                            w = convw[:, CONV * t + tap:CONV * t + tap + 1]
                            src = convin[:, t, tap:tap + SEQ]
                            if tap == 0:
                                ts(o, src, w, None, ALU.mult).then_inc(conv_st, 1)
                            else:
                                dve.wait_ge(conv_st, 10 * j + 2 * tap + q - 1)
                                stt(o, src, w, o, ALU.mult, ALU.add).then_inc(conv_st, 1)
                low(17)
                low(19)
                dve.wait_ge(p1_ev, 17)
                tt(ax, ab[:, :, 0:16], again(dnrow[:, 0:16], NT), ALU.add).then_inc(dg_v, 1)
                dve.wait_ge(dg_v, 1)
                stt(nab, ax, -1.0, ax, ALU.mult, ALU.max).then_inc(dg_v, 1)
                dve.wait_ge(dg_a, 4)
                stt(lnp, ax, 0.0, lnp, ALU.max, ALU.add).then_inc(dg_v, 1)
                dve.wait_ge(dg_v, 3)
                stt(gg, lnp, -1.0, again(ea, NT), ALU.mult, ALU.mult).then_inc(dg_v, 1)
                dve.wait_ge(dg_a, 4)
                ts(eb, eb, 1.0, None, ALU.add).then_inc(dg_v, 1)
                dve.wait_ge(dg_v, 5)
                v.reciprocal(beta, eb).then_inc(dg_v, 1)
                for c in range(4):
                    x = (kT if c < 2 else qT)[:, 2 * (c % 2):2 * (c % 2) + 2, :].rearrange("p a b -> p (a b)")
                    dve.wait_ge(rs_done, 4 + c + 1)
                    tt(x, x, rs[:, c, :], ALU.mult).then_inc(nrm_done, 1)
                dve.wait_ge(strip_in, 16)
                mx3 = mx.rearrange("p (i e) -> p i e", e=2)
                for n in range(9):
                    if n < 8:
                        e, i = n % 2, n - n % 2
                        off = P * (1 - i // 4)
                        dve.wait_ge(sc_mm, n + 1)
                        stt(Sall[:, i:i + 2, e, :], ps[n % 4][:, :].rearrange("p (i j) -> p i j", i=2), HD ** -0.5,
                            strip[:, 4 * e + i % 4:4 * e + i % 4 + 2, off:off + SEQ], ALU.mult, ALU.add).then_inc(sc_ev, 1)
                    if n:
                        e, i = (n - 1) % 2, (n - 1) - (n - 1) % 2
                        dve.wait_ge(sc_ev, n)
                        v.tensor_reduce(mx3[:, i:i + 2, e], Sall[:, i:i + 2, e, :], AX.X, ALU.max).then_inc(sm_v, 1)
                dve.wait_ge(sm_v, 8)
                tt(mx, mx, sinkr[:, :], ALU.max).then_inc(sm_v, 1)
                dve.wait_ge(sm_v, 9)
                ts(mneg, mx, -1.0, None, ALU.mult).then_inc(sm_v, 1)
                tt(esink, sinkr[:, :], mx, ALU.subtract).then_inc(sm_v, 1)
                dve.wait_ge(sm_a, 17)
                tt(rden, psum16, esink, ALU.add).then_inc(sm_v, 1)
                dve.wait_ge(sm_v, 12)
                v.reciprocal(rden, rden).then_inc(sm_v, 1)
                dve.wait_ge(sm_v, 13)
                for i in range(8):
                    tt(Sall[:, i], Sall[:, i], over(rden[:, 2 * i:2 * i + 2], SEQ), ALU.mult).then_inc(pn_done, 1)
                dve.wait_ge(gc_mm, 1)
                v.tensor_copy(Gc, ps[4][:, 0:64].rearrange("p (i c) -> p i c", i=4)).then_inc(gc_v, 1)
                dve.wait_ge(gc_v, 1)
                tt(dl, Gc[:, :, 8:16], Gc[:, :, 0:8], ALU.subtract).then_inc(gc_v, 1)
                dve.wait_ge(gc_a, 1)
                for i, (d, T) in enumerate(SETS):
                    tt(bG[:, i, :], eG[:, i, :], beta[:, T, 8 * d:8 * d + 8], ALU.mult).then_inc(gc_v, 1)

                def set_tiles(i):
                    d, T = SETS[i]
                    kp = i % 2
                    if i == 0:
                        dve.wait_ge(pv_ev, 2)
                    dve.wait_ge(grow_mm, i + 1)
                    for w, hh in enumerate(HEAD_AT):
                        last = stt(Dm[:, w, :], ps[w // 4][:, (w % 4) * P:(w % 4) * P + P], Gc[:, i, hh:hh + 1],
                                   C(f"neg{d}"), ALU.subtract, ALU.add)
                    last.then_inc(dm_done, 1)

                    def quad(x, b):
                        return x[:, 4 * b:4 * b + 4, :].rearrange("p h c -> p (h c)")

                    dve.wait_ge(dexp_done, i + 1)
                    dve.wait_ge(kk_mm, i + 1)
                    for b in range(2):
                        tt(quad(AT, b), ps[4 + b][:, :], quad(Dm, b), ALU.mult).then_inc(kkd_done, 1)
                    dve.wait_ge(beta_mm, i + 1)
                    for b in range(2):
                        dve.wait_ge(kkd_done, 2 * i + b + 1)
                        last = tt(quad(AT, b), quad(AT, b), ps[2 + b][:, :], ALU.mult)
                    last.then_inc(at_done, 1)
                    dve.wait_ge(at_done, i + 1)
                    lv = C(f"lvl{d}0").rearrange("p (a c) -> p a c", a=1).to_broadcast([P, 4, P])
                    idb = ident.rearrange("p (a c) -> p a c", a=1).to_broadcast([P, 4, P])
                    tt(AL[:, 0:4, :], AT[:, 0:4, :], lv, ALU.mult).then_inc(xt0_v, 1)
                    dve.wait_ge(xt0_v, 2 * i + 1)
                    tt(XT[:, 0:4, :], idb, AL[:, 0:4, :], ALU.subtract).then_inc(xt0_v, 1)
                    dve.wait_ge(qk_mm, i + 1)
                    for b in range(2):
                        last = tt(quad(qkd[kp], b), ps[6 + b][:, :], quad(Dm, b), ALU.mult)
                    last.then_inc(qkd_done, 1)
                    for lev in range(1, LEVELS):
                        for q in range(2):
                            n = (i * 5 + lev - 1) * 2 + q
                            dve.wait_ge(xy_mm, n + 1)
                            tt(quad(XT, q), quad(XT, q), ps[4 + q][:, :], ALU.subtract).then_inc(xt_done, 1)
                    dve.wait_ge(uw_mm, i + 1)
                    v.tensor_copy(wT[kp].rearrange("p k c -> p (k c)"), ps[7][:, :]).then_inc(w_ev, 1)

                def scan_step(n):
                    for d in range(2):
                        i, c, k = 2 * (n // 2) + d, (n if d == 0 else 3 - n), 2 * n + d
                        kp, r = i % 2, CHUNK * (c % 2)
                        dve.wait_ge(ws_mm, k + 1)
                        tt(vnew[r:r + CHUNK, n % 2, :], u_s[kp][r:r + CHUNK, :], ps[3 * d][r:r + CHUNK, :],
                           ALU.subtract).then_inc(vn_done, 1)
                    for d in range(2):
                        c, k = (n if d == 0 else 3 - n), 2 * n + d
                        r = CHUNK * (c % 2)
                        dve.wait_ge(st_mm, k + 1)
                        dve.wait_ge(sc_done, k + 1)
                        for e in range(2):
                            a = HD * e
                            tt(S[a:a + HD, d, :, a:a + HD], Sc[a:a + HD, d, :, a:a + HD],
                               ps[3 * d + 2][a:a + HD, :].rearrange("p (k n) -> p k n", k=4)[:, :, a:a + HD],
                               ALU.add).then_inc(s_done, 1)
                        if n >= 2:
                            dve.wait_ge(o_ev, 4)
                            tt(osum[r:r + CHUNK, c // 2, :], osum[r:r + CHUNK, c // 2, :], ps[3 * d + 1][r:r + CHUNK, :],
                               ALU.add).then_inc(o_ev, 1)

                set_tiles(0)
                set_tiles(1)
                scan_step(0)
                scan_step(1)
                set_tiles(2)
                set_tiles(3)
                scan_step(2)
                scan_step(3)
                dve.wait_ge(osq_done, 2)
                v.tensor_reduce(osr, M[:, 17408:18432].rearrange("p (h d) -> p h d", d=HD), AX.X, ALU.add).then_inc(or_v, 1)
                dve.wait_ge(or_a, 2)
                o16 = M[:, 3072:4096].rearrange("p (h d) -> p h d", d=HD)
                tt(o16, o16, over(osr, HD), ALU.mult).then_inc(or_v, 1)
                dve.wait_ge(or_v, 2)
                dve.wait_ge(zn_done, 2)
                tt(M[:, 3072:4096], M[:, 3072:4096], M[:, 2048:3072], ALU.mult).then_inc(od_done, 1)
                for k in range(12):
                    j = k % 4
                    T, hf = j % 2, j // 2
                    dve.wait_ge(up_mm, k + 1)
                    dve.wait_ge(gate_ev, (1, 2, 3, 4)[k // 4 + (k >= 10)])
                    if k >= 6:
                        dve.wait_ge(mrg, k - 5)
                    o = merged[:, T, hf * 512:hf * 512 + 512] if k < 4 else gtmp[:, k % 2, :]
                    tt(o, ps[4 + j][:, :], gate_at(k), ALU.mult).then_inc(up_ev, 1)
                turned(mt_mm, mt_d, mT, 0)

                def residual(T, hf, bank, done):
                    hv = h[:, T, hf * 512:hf * 512 + 512]
                    stt(hv, hv, ALPHA, ps[bank][:, :], ALU.mult, ALU.add).then_inc(done, 1)

                def stats(T, hf, x=h):
                    v.bn_stats(bst[:, T, 6 * hf:6 * hf + 6], x[:, T, hf * 512:hf * 512 + 512]).then_inc(lnv[T], 1)

                def variance(which, T):
                    dve.wait_ge(lnv[T], 6 * which + 2)
                    v.bn_aggr(bag[:, T, :], bst[:, T, :]).then_inc(lnv[T], 1)
                    dve.wait_ge(lnv[T], 6 * which + 3)
                    ts(rstd[:, T:T + 1], bag[:, T, 1:2], LN_EPS, None, ALU.add).then_inc(lnv[T], 1)

                def norm(which, T, done, x=h):
                    dve.wait_ge(lnp_done, 2 * which + T + 1)
                    ts(h[:, T, :], x[:, T, :], bag[:, T, 0:1], rstd[:, T:T + 1], ALU.subtract, ALU.mult).then_inc(lnv[T], 1)
                    dve.wait_ge((ln1_in, ln2_in)[which], l * 32 + 32)
                    dve.wait_ge(lnv[T], 6 * which + 5)
                    tt(h[:, T, :], h[:, T, :], lng, ALU.mult).then_inc(lnv[T], 1)
                    dve.wait_ge(lnv[T], 6 * which + 6)
                    if which and T:
                        dve.wait_ge(ln2_half, 1)
                    tt(h[:, T, :], h[:, T, :], lnb, ALU.add).then_inc(done, 1)

                for hf in range(2):
                    for T in range(NT):
                        dve.wait_ge(out_mm, 2 * hf + T + 1)
                        residual(T, hf, 4 + 2 * hf + T, res1)
                        dve.wait_ge(res1, 2 * hf + T + 1)
                        stats(T, hf)
                        if hf:
                            variance(0, T)
                            norm(0, T, ln1_done)
                with dve.If(l < 1):
                    turned_lo(hTl, hTh, 4)

                    def product(ft):
                        dve.wait_ge(sg_ev, ft + 1)
                        if ft >= 4:
                            dve.wait_ge(datl_ev, ft - 3)
                        tt(aT[:, ft % 4, :], sg[:, ft % 2, :], ps[ft % 2][:, SEQ:2 * SEQ], ALU.mult).then_inc(af_ev, 1)

                    def a_lo(ft):
                        dve.wait_ge(dath_ev, ft + 1)
                        tt(datl[:, ft % 4, :], aT[:, ft % 4, :], dath[:, ft % 4, :].bitcast(F32), ALU.subtract).then_inc(datl_ev, 1)

                    for n, (w, ft) in enumerate(DPARTS):
                        dve.wait_ge(part_hi, n + 1)
                        tt(dense_part(w_lo, w, ft), dense_part(slot, w, ft), dense_hi(n, w).bitcast(F32), ALU.subtract).then_inc(part_lo, 1)
                        beside_dense(n, product, a_lo)
                    dve.wait_ge(part_mm, len(DPARTS))
                    for T in range(NT):
                        for dh in range(2):
                            residual(T, dh, 4 + 2 * T + dh, res2)
                        for dh in range(2):
                            dve.wait_ge(res2, 2 * T + dh + 1)
                            stats(T, dh)
                        variance(1, T)
                    norm(1, 0, ln2_half)
                    norm(1, 1, layer_done)
                with dve.Else():
                    turned(tr_mm, tr_d, hT, 1)
                    for T in range(NT):
                        dve.wait_ge(rl_mm, T + 1)
                        v.tensor_copy(lg[:, T, :], ps[T][:, 0:NE]).then_inc(rl_v, 1)
                    for T in range(NT):
                        dve.wait_ge(rl_v, T + 1)
                        v.max(m8[:, T, :], lg[:, T, :]).then_inc(rl_v, 1)
                    for T in range(NT):
                        dve.wait_ge(rl_v, T + 3)
                        v.max_index(idx8v[:, T, :], m8[:, T, :], lg[:, T, :]).then_inc(rl_v, 1)
                    dve.wait_ge(rl_v, 6)
                    v.tensor_copy(idxf, idx8v[:, :, 0:TOP_K]).then_inc(rl_v, 1)
                    dve.wait_ge(rl_v, 7)
                    for k in range(TOP_K):
                        for T in range(NT):
                            ts(oh[:, k, T, :], C("iota")[:, 0:NE], idxf[:, T, k:k + 1], None, ALU.is_equal).then_inc(rl_v, 1)
                    dve.wait_ge(rl_v, 11)
                    tt(sel, oh[:, 0], oh[:, 1], ALU.add).then_inc(rl_v, 1)
                    tt(dm12, m8[:, :, 1], m8[:, :, 0], ALU.subtract).then_inc(rl_v, 1)
                    dve.wait_ge(rl_a, 1)
                    ts(e12p, e12, 1.0, None, ALU.add).then_inc(rl_v, 1)
                    dve.wait_ge(rl_v, 14)
                    v.reciprocal(rw[:, :, 0], e12p).then_inc(rl_v, 1)
                    dve.wait_ge(rl_v, 15)
                    tt(rw[:, :, 1], e12, rw[:, :, 0], ALU.mult).then_inc(rl_v, 1)
                    dve.wait_ge(rc_mm, 1)
                    v.tensor_copy(cnt, ps[2][:, 16:24]).then_inc(rl_v, 1)
                    v.tensor_copy(pos, ps[2][:, 0:16].rearrange("p (t e) -> p t e", t=NT)).then_inc(rl_v, 1)
                    dve.wait_ge(rl_v, 18)
                    ts(nch, cnt, 0.0, None, ALU.is_gt).then_inc(rl_v, 1)
                    step = 19
                    for k in range(CAP, SEQ, CAP):
                        dve.wait_ge(rl_v, step)
                        stt(nch, cnt, float(k), nch, ALU.is_gt, ALU.add).then_inc(rl_v, 1)
                        step += 1
                    dve.wait_ge(rl_v, step)
                    v.tensor_tensor_scan(end, scal[:, 3:4].to_broadcast([P, NE]), nch, 0.0, ALU.mult, ALU.add).then_inc(rl_v, 1)
                    dve.wait_ge(rl_v, step + 1)
                    tt(sbase, end, nch, ALU.subtract).then_inc(rl_v, 1)
                    dve.wait_ge(rl_v, step + 2)
                    stt(slot_e, again(sbase, NT), float(CAP), pos, ALU.mult, ALU.add).then_inc(rl_v, 1)
                    dve.wait_ge(rl_v, step + 3)
                    for k in range(TOP_K):
                        tt(pick[:, k], oh[:, k], slot_e, ALU.mult).then_inc(rl_v, 1)
                    dve.wait_ge(rl_v, step + 5)
                    for k in range(TOP_K):
                        v.tensor_reduce(rslot[:, :, k], pick[:, k], AX.X, ALU.add).then_inc(rl_v, 1)
                    tt(cmp_p, C("pass_no").rearrange("p (n e) -> p n e", e=NE), again(end, MAXP), ALU.is_ge).then_inc(rl_v, 1)
                    dve.wait_ge(rl_v, step + 8)
                    v.tensor_reduce(idf, cmp_p, AX.X, ALU.add).then_inc(rl_v, 1)
                    dve.wait_ge(rl_v, step + 9)
                    ts(ids[:, 0:MAXP], idf, float(NE - 1), None, ALU.min).then_inc(rl_v, 1)
                    v.tensor_copy(ids[:, MAXP + 1:MAXP + 2], end[:, NE - 1:NE]).then_inc(rl_v, 1)
                    ts(ids[:, MAXP:MAXP + 1], end[:, NE - 1:NE], float(NE - 1), None, ALU.min).then_inc(rl_v, 1)
                    ts(acc, h, ALPHA, None, ALU.mult).then_inc(rl_v, 1)
                    dve.wait_ge(rl_v, step + 13)
                    dve.sem_inc(acc_add, 4)
                    dve.sem_inc(ids_done, 1)

                    def dispatch(turn):
                        for T in range(NT):
                            b = 6 * T
                            s1, s2 = rslot[:, T, 0:1], rslot[:, T, 1:2]
                            if turn is not None or T:
                                dve.wait_ge(dispv, b if turn is None else turn * 12 + (12 + b))
                            ts(hot1, C("iota"), s1, None, ALU.is_equal).then_inc(dispv, 1)
                            ts(hot2, C("iota"), s1, rw[:, T, 0:1], ALU.is_equal, ALU.mult).then_inc(dispv, 1)
                            ts(hot3, C("iota"), s2, rw[:, T, 1:2], ALU.is_equal, ALU.mult).then_inc(dispv, 1)
                            dve.wait_ge(dispv, b + 1 if turn is None else turn * 12 + (12 + b + 1))
                            stt(disp[:, T, :], C("iota"), s2, hot1, ALU.is_equal, ALU.add).then_inc(dispv, 1)
                            dve.wait_ge(dispv, b + 4 if turn is None else turn * 12 + (12 + b + 4))
                            tt(comb[:, T, :], hot2, hot3, ALU.add).then_inc(dispv, 1)
                            ts(rslot[:, T, :], rslot[:, T, :], float(-CAP), None, ALU.add).then_inc(dispv, 1)

                    def xg_low(count, first):
                        for b in range(2):
                            dve.wait_ge(xgh_ev, count + (first + b))
                            tt(xgl[:, 4 * b:4 * b + 4, :], ps[2 + b][:, 0:4 * CAP].rearrange("p (j c) -> p j c", j=4),
                               xgh[:, 4 * b:4 * b + 4, :].bitcast(F32), ALU.subtract).then_inc(xgl_ev, 1)

                    def lo(n, p, turn):
                        name, s = PASS_ORDER[n // PARTS], n % PARTS
                        done = turn * SUBS + n + 1
                        dve.wait_ge(part_hi, done if p is None else p * SUBS + done)
                        at_hi = (n % HI_BUFS) * SUB
                        tt(w_lo(moe.slot[name])[:, s * SUB:s * SUB + SUB], slot(moe.slot[name])[:, s * SUB:s * SUB + SUB],
                           w_hi[:, at_hi:at_hi + SUB].bitcast(F32), ALU.subtract).then_inc(part_lo, 1)

                    dispatch(None)
                    xg_low(0, 1)
                    for n in range(AHEAD):
                        lo(n, None, 0)
                    total = dve.value_load(ids[0:1, MAXP + 1:MAXP + 2], min_val=1, max_val=MAXP)
                    with dve.Fori(0, MAXP) as p:
                        with dve.If(p < total):
                            def mult(b):
                                dve.wait_ge(sg_ev, p * NFB + (b + 1))
                                tt(ae[0:CAP, b % 2, :], sge[0:CAP, b % 2, :], ps[2 * (b % 2) + 1][0:CAP, :], ALU.mult).then_inc(af_ev, 1)

                            def a_low(b):
                                dve.wait_ge(ath_ev, p * NFB + (b + 1))
                                tt(atl[:, b % 2, :, :], ps[6][:, 0:4 * CAP].rearrange("p (j c) -> p j c", j=4),
                                   ath[:, b % 2, :, :].bitcast(F32), ALU.subtract).then_inc(atl_ev, 1)

                            def next_dispatch():
                                dve.wait_ge(ct_mm, p + 1)
                                dispatch(p)

                            for n in range(AHEAD, SUBS):
                                lo(n, p, 0)
                                after_part(n, mult, a_low, lambda: None, next_dispatch, lambda: xg_low(p * 2, 3))
                            for n in range(AHEAD):
                                lo(n, p, 1)
                            dve.wait_ge(part_mm, p * SUBS + 2 * SUBS)
                            v.tensor_copy(y[0:CAP, 512:1024], ps[5][0:CAP, :]).then_inc(yd_ev, 1)
                            for q in range(4):
                                T, dh = q // 2, q % 2
                                av = acc[:, T, dh * 512:dh * 512 + 512]
                                dve.wait_ge(cb_mm, p * 4 + (q + 1))
                                if q == 0:
                                    dve.wait_ge(acc_add, p * 4 + 4)
                                tt(av, av, ps[7 - dh][:, :], ALU.add).then_inc(acc_add, 1)
                    dve.wait_ge(acc_add, total * 4 + 4)
                    for T in range(NT):
                        for dh in range(2):
                            stats(T, dh, acc)
                        variance(1, T)
                    norm(1, 0, ln2_half, acc)
                    norm(1, 1, layer_done, acc)
                end_layer(dve, l)


_INS = ["x", "w_in", "w_branch", "w_out", "pool_w", "rel_bias", "dn_norm_w", "ln1_g", "ln1_b", "ln2_g", "ln2_b",
        "ffn_w1", "ffn_w3", "ffn_w2", "router_w", "moe_wg", "moe_wu", "moe_wd"]


def kernel(**inputs):
    from concourse import bacc
    from concourse.bass_utils import run_bass_kernel_spmd

    a = {n: np.ascontiguousarray(inputs[n]) for n in _INS}
    cw = np.asarray(inputs["conv_w"]).reshape(DEPTH, CONV, 3, 4, P)
    cw = np.concatenate([cw[:, :, 1:2], cw[:, :, 0:1], cw[:, :, 2:3]], axis=2)
    w_in = a["w_in"].copy()
    w_in[:, :, C_Q:C_K] = w_in[:, :, C_Q:C_K].reshape(DEPTH, D, 2, 4, HD).transpose(0, 1, 3, 2, 4).reshape(DEPTH, D, 512)
    a["w_in"] = w_in
    a["conv_w"] = np.ascontiguousarray(cw.transpose(0, 4, 2, 3, 1).reshape(DEPTH, P, 12 * CONV))
    a["dn_rows"] = np.ascontiguousarray(np.concatenate(
        [np.asarray(inputs["dt_bias"]).reshape(DEPTH, 16), np.asarray(inputs["a_log"]).reshape(DEPTH, 16)], axis=1))
    sinks = np.asarray(inputs["attn_sink"]).reshape(DEPTH, 2, 4).transpose(0, 2, 1).reshape(DEPTH, 8)
    a["sinks"] = np.ascontiguousarray(np.concatenate([sinks, sinks], axis=1))
    a["pool_scale"] = np.ascontiguousarray(np.asarray(inputs["pool_scale"]).reshape(DEPTH, BT, P).transpose(0, 2, 1))
    a["consts"] = const_table()
    a["pool_c"] = pool_table()
    a["hot"], a["band"] = bucket_table()

    nc = bacc.Bacc("TRN2", target_bir_lowering=False, num_devices=1)
    A = {n: nc.dram_tensor(f"in_{n}", x.shape, F32, kind="ExternalInput").ap() for n, x in a.items()}
    A["rows"] = nc.dram_tensor("rows", (QH, P, 512), F32, kind="Internal").ap()
    out = nc.dram_tensor("out", (1, SEQ, D), F32, kind="ExternalOutput").ap()
    build(nc, A, out)
    r = run_bass_kernel_spmd(nc, [{f"in_{n}": x for n, x in a.items()}], core_ids=[0])
    return r.results[0]["out"]
```
